# Optimizing a Trainium2 kernel written in Bass

```python
import jax, jax.numpy as jnp
from jax import lax
import numpy as np

D_MODEL = 1024
BATCH = 1
SEQ = 256
DEPTH = 2

CHUNK = 64
RMS_EPS = 1e-6
DN_HEADS = 4
DN_DK = 128
DN_DV = 128
DN_CONV = 4
DN_QKV = 2 * DN_HEADS * DN_DK + DN_HEADS * DN_DV
DN_VAL = DN_HEADS * DN_DV
RET_HEADS = 4
RET_DK = 128
RET_DV = 128
RET_QK = RET_HEADS * RET_DK
RET_VAL = RET_HEADS * RET_DV
ROPE_BASE = 10000.0
GN_EPS = 1e-5
POOL_WINDOWS = (2, 4, 8, 16)
POOL_GROUPS = 4
POOL_GROUP = 128
POOL_WIDTH = POOL_GROUPS * POOL_GROUP
N_BRANCH = 3
D_FF = -(-8 * D_MODEL // (3 * 256)) * 256
IN_SIZES = (DN_QKV, DN_VAL, DN_HEADS, DN_HEADS, RET_QK, RET_QK, RET_VAL, RET_VAL, POOL_WIDTH, N_BRANCH * D_MODEL)
D_IN = sum(IN_SIZES)


def _split_points(sizes):
    pts, acc = [], 0
    for s in sizes[:-1]:
        acc += s
        pts.append(acc)
    return pts

def rms_norm(x, w):
    xf = x.astype(jnp.float32)
    y = xf * lax.rsqrt(jnp.mean(xf * xf, axis=-1, keepdims=True) + RMS_EPS) * w.astype(jnp.float32)
    return y.astype(x.dtype)

def l2_normalize(x):
    return x * lax.rsqrt(jnp.sum(x * x, axis=-1, keepdims=True) + 1e-6)

def causal_depthwise_conv(x, w):
    k = w.shape[0]
    return lax.conv_general_dilated(
        x, w[:, None, :].astype(x.dtype), window_strides=(1,), padding=((k - 1, 0),),
        dimension_numbers=("NWC", "WIO", "NWC"), feature_group_count=x.shape[-1])

def to_chunks(x):
    b, s, h, d = x.shape
    return x.reshape(b, s // CHUNK, CHUNK, h, d).transpose(0, 3, 1, 2, 4)

def from_chunks(x):
    b, h, n, c, d = x.shape
    return x.transpose(0, 2, 3, 1, 4).reshape(b, n * c, h * d)

def gated_delta_rule(q, k, v, beta, g):
    b, s, h, dk = q.shape
    dv = v.shape[-1]
    n = s // CHUNK
    q = to_chunks(q) * (dk ** -0.5)
    k = to_chunks(k)
    v = to_chunks(v)
    beta = beta.reshape(b, n, CHUNK, h).transpose(0, 3, 1, 2)
    g = g.reshape(b, n, CHUNK, h).transpose(0, 3, 1, 2)
    G = jnp.cumsum(g, axis=-1)
    causal = jnp.tril(jnp.ones((CHUNK, CHUNK), dtype=bool))
    strict = jnp.tril(jnp.ones((CHUNK, CHUNK), dtype=bool), k=-1)
    diff = G[..., :, None] - G[..., None, :]
    decay = jnp.where(causal, jnp.exp(jnp.where(causal, diff, 0.0)), 0.0)
    k_beta = k * beta[..., None]
    m = jnp.where(strict, jnp.einsum('bhnid,bhnjd->bhnij', k_beta, k) * decay, 0.0)
    a = m + jnp.eye(CHUNK, dtype=m.dtype)
    rhs = jnp.concatenate([v * beta[..., None], k_beta * jnp.exp(G)[..., None]], axis=-1)
    sol = lax.linalg.triangular_solve(a, rhs, left_side=True, lower=True, unit_diagonal=True)
    u, w = sol[..., :dv], sol[..., dv:]
    attn = jnp.einsum('bhnid,bhnjd->bhnij', q, k) * decay
    g_last = G[..., -1]
    q_dec = q * jnp.exp(G)[..., None]
    k_tail = k * jnp.exp(g_last[..., None] - G)[..., None]
    xs = tuple(jnp.moveaxis(t, 2, 0) for t in (u, w, attn, q_dec, k_tail, jnp.exp(g_last)))

    def step(state, inp):
        u_c, w_c, a_c, qd_c, kt_c, dl_c = inp
        v_new = u_c - jnp.einsum('bhck,bhkv->bhcv', w_c, state)
        o = jnp.einsum('bhck,bhkv->bhcv', qd_c, state) + jnp.einsum('bhcj,bhjv->bhcv', a_c, v_new)
        state = state * dl_c[..., None, None] + jnp.einsum('bhck,bhcv->bhkv', kt_c, v_new)
        return state, o

    s0 = jnp.zeros((b, h, dk, dv), dtype=q.dtype)
    _, o = lax.scan(step, s0, xs)
    return from_chunks(jnp.moveaxis(o, 0, 2))

def rotary(x):
    s, d = x.shape[1], x.shape[-1]
    half = d // 2
    inv = ROPE_BASE ** (-jnp.arange(half, dtype=jnp.float32) / half)
    ang = jnp.arange(s, dtype=jnp.float32)[:, None] * inv[None, :]
    cos = jnp.cos(ang)[None, :, None, :]
    sin = jnp.sin(ang)[None, :, None, :]
    x1, x2 = x[..., :half], x[..., half:]
    return jnp.concatenate([x1 * cos - x2 * sin, x2 * cos + x1 * sin], axis=-1)

def chunkwise_retention(q, k, v, log_gamma):
    b, s, h, dk = q.shape
    dv = v.shape[-1]
    q = to_chunks(q)
    k = to_chunks(k) * (dk ** -0.5)
    v = to_chunks(v)
    idx = jnp.arange(CHUNK, dtype=jnp.float32)
    lg = log_gamma[:, None]
    dmask = jnp.exp(jnp.abs(idx[:, None] - idx[None, :])[None] * log_gamma[:, None, None])
    scores = jnp.einsum('bhnid,bhnjd->bhnij', q, k) * dmask[:, None]
    o_inner = jnp.einsum('bhnij,bhnjv->bhniv', scores, v)
    xi = jnp.exp((idx + 1.0)[None] * lg)
    zeta = jnp.exp((CHUNK - 1.0 - idx)[None] * lg)
    kv = jnp.einsum('bhnjd,bhnjv->bhndv', k * zeta[:, None, :, None], v)
    chunk_decay = jnp.exp(CHUNK * log_gamma)

    def step(r, kv_c):
        return r * chunk_decay[:, None, None] + kv_c, r

    _, r_prev = lax.scan(step, jnp.zeros((b, h, dk, dv), dtype=kv.dtype), jnp.moveaxis(kv, 2, 0))
    r_prev = jnp.moveaxis(r_prev, 0, 2)
    o_cross = jnp.einsum('bhnid,bhndv->bhniv', q * xi[:, None, :, None], r_prev)
    o = from_chunks(o_inner + o_cross)
    return o.reshape(b, s, h, dv)

def multiscale_pool(u, w_lin, scale):
    b, s, _ = u.shape
    groups = u.reshape(b, s, POOL_GROUPS, POOL_GROUP)
    cs = jnp.cumsum(groups, axis=1)
    t = jnp.arange(1, s + 1, dtype=jnp.float32)
    pooled = []
    for gi, win in enumerate(POOL_WINDOWS):
        c = cs[:, :, gi]
        prev = jnp.pad(c, ((0, 0), (win, 0), (0, 0)))[:, :s]
        cnt = jnp.minimum(t, float(win))[None, :, None]
        pooled.append((c - prev) / cnt)
    mixed = jnp.stack(pooled, axis=2) - groups
    y = jnp.einsum('bsgc,gcd->bsgd', mixed, w_lin.astype(jnp.float32)).reshape(b, s, POOL_WIDTH)
    return y * scale.astype(jnp.float32)

def hybrid_mixer(h, w_in, dn_conv, dn_A_log, dn_dt_bias, dn_out_norm, ret_out_norm,
                 pool_w, pool_scale, w_branch_dn, w_branch_ret, w_branch_pool, w_out):
    b, s, _ = h.shape
    f32 = jnp.float32
    proj = h @ w_in
    (dn_qkv, dn_z, dn_b, dn_a, ret_q, ret_k, ret_v, ret_g, pool_u, gates) = jnp.split(
        proj, _split_points(IN_SIZES), axis=-1)

    qkv = jax.nn.silu(causal_depthwise_conv(dn_qkv, dn_conv)).astype(f32)
    q, k, v = jnp.split(qkv, [DN_HEADS * DN_DK, 2 * DN_HEADS * DN_DK], axis=-1)
    q = l2_normalize(q.reshape(b, s, DN_HEADS, DN_DK))
    k = l2_normalize(k.reshape(b, s, DN_HEADS, DN_DK))
    v = v.reshape(b, s, DN_HEADS, DN_DV)
    beta = jax.nn.sigmoid(dn_b.astype(f32))
    g = -jnp.exp(dn_A_log.astype(f32)) * jax.nn.softplus(dn_a.astype(f32) + dn_dt_bias.astype(f32))
    o_dn = gated_delta_rule(q, k, v, beta, g).reshape(b, s, DN_HEADS, DN_DV)
    o_dn = o_dn * lax.rsqrt(jnp.mean(o_dn * o_dn, axis=-1, keepdims=True) + RMS_EPS) * dn_out_norm.astype(f32)
    o_dn = o_dn.reshape(b, s, DN_VAL) * jax.nn.silu(dn_z.astype(f32))

    o_pool = multiscale_pool(pool_u.astype(f32), pool_w, pool_scale)

    log_gamma = jnp.log1p(-jnp.exp2(-5.0 - jnp.arange(RET_HEADS, dtype=f32)))
    rq = rotary(ret_q.astype(f32).reshape(b, s, RET_HEADS, RET_DK))
    rk = rotary(ret_k.astype(f32).reshape(b, s, RET_HEADS, RET_DK))
    rv = ret_v.astype(f32).reshape(b, s, RET_HEADS, RET_DV)
    o_ret = chunkwise_retention(rq, rk, rv, log_gamma)
    mu = jnp.mean(o_ret, axis=-1, keepdims=True)
    var = jnp.mean(jnp.square(o_ret - mu), axis=-1, keepdims=True)
    o_ret = ((o_ret - mu) * lax.rsqrt(var + GN_EPS)).reshape(b, s, RET_VAL) * ret_out_norm.astype(f32)
    o_ret = o_ret * jax.nn.silu(ret_g.astype(f32))

    gt = jax.nn.sigmoid(gates.astype(f32)).reshape(b, s, N_BRANCH, D_MODEL)
    y = (gt[:, :, 0] * (o_dn.astype(h.dtype) @ w_branch_dn)
         + gt[:, :, 1] * (o_pool.astype(h.dtype) @ w_branch_pool)
         + gt[:, :, 2] * (o_ret.astype(h.dtype) @ w_branch_ret))
    return y.astype(h.dtype) @ w_out

def swiglu(h, w_gate, w_up, w_down):
    return (jax.nn.silu(h @ w_gate) * (h @ w_up)) @ w_down

def first_inputs(seed: int = 0) -> dict:
    key = jax.random.key(seed)
    ks = jax.random.split(key, 24)
    f32 = jnp.float32
    L = DEPTH

    def nrm(k, shape, fan_in):
        return jax.random.normal(k, shape, f32) * (fan_in ** -0.5)

    def gain(k, shape):
        return 1.0 + 0.1 * jax.random.normal(k, shape, f32)

    dt = jnp.exp(jax.random.uniform(ks[6], (L, DN_HEADS), f32, minval=float(np.log(1e-3)), maxval=float(np.log(1e-1))))
    return {
        "x": jax.random.normal(ks[0], (BATCH, SEQ, D_MODEL), f32),
        "mix_pre_norm": gain(ks[1], (L, D_MODEL)),
        "mix_post_norm": gain(ks[2], (L, D_MODEL)),
        "w_in": nrm(ks[3], (L, D_MODEL, D_IN), D_MODEL),
        "dn_conv": nrm(ks[4], (L, DN_CONV, DN_QKV), DN_CONV),
        "dn_A_log": jnp.log(jax.random.uniform(ks[5], (L, DN_HEADS), f32, minval=1.0, maxval=16.0)),
        "dn_dt_bias": dt + jnp.log(-jnp.expm1(-dt)),
        "dn_out_norm": gain(ks[7], (L, DN_DV)),
        "ret_out_norm": gain(ks[8], (L, RET_VAL)),
        "pool_w": nrm(ks[9], (L, POOL_GROUPS, POOL_GROUP, POOL_GROUP), POOL_GROUP),
        "pool_scale": gain(ks[10], (L, POOL_WIDTH)),
        "w_branch_dn": nrm(ks[11], (L, DN_VAL, D_MODEL), DN_VAL),
        "w_branch_ret": nrm(ks[12], (L, RET_VAL, D_MODEL), RET_VAL),
        "w_branch_pool": nrm(ks[13], (L, POOL_WIDTH, D_MODEL), POOL_WIDTH),
        "w_out": nrm(ks[14], (L, D_MODEL, D_MODEL), D_MODEL),
        "ffn_pre_norm": gain(ks[15], (L, D_MODEL)),
        "ffn_post_norm": gain(ks[16], (L, D_MODEL)),
        "ffn_gate": nrm(ks[17], (L, D_MODEL, D_FF), D_MODEL),
        "ffn_up": nrm(ks[18], (L, D_MODEL, D_FF), D_MODEL),
        "ffn_down": nrm(ks[19], (L, D_FF, D_MODEL), D_FF),
    }

def first_block(x, mix_pre_norm, mix_post_norm, w_in, dn_conv, dn_A_log, dn_dt_bias, dn_out_norm,
              ret_out_norm, pool_w, pool_scale, w_branch_dn, w_branch_ret, w_branch_pool, w_out,
              ffn_pre_norm, ffn_post_norm, ffn_gate, ffn_up, ffn_down):
    for l in range(DEPTH):
        h = rms_norm(x, mix_pre_norm[l])
        m = hybrid_mixer(h, w_in[l], dn_conv[l], dn_A_log[l], dn_dt_bias[l], dn_out_norm[l],
                         ret_out_norm[l], pool_w[l], pool_scale[l], w_branch_dn[l], w_branch_ret[l],
                         w_branch_pool[l], w_out[l])
        x = x + rms_norm(m, mix_post_norm[l])
        h = rms_norm(x, ffn_pre_norm[l])
        x = x + rms_norm(swiglu(h, ffn_gate[l], ffn_up[l], ffn_down[l]), ffn_post_norm[l])
    return x


HEAD_DIM = 64
ROPE_THETA = 10000.0
NORM_EPS = 1e-6
BLOCK = 128

A_HEADS = 6
IDX_HEADS = 8
IDX_DIM = 64
TOPK_MAX = 256

B_GROUPS = ((128, 1), (512, 4), (2048, 16))
B_HEADS_PER_GROUP = 4
B_HEADS = B_HEADS_PER_GROUP * len(B_GROUPS)

C_HEADS = 8
C_KV_HEADS = 2
C_WINDOW = 128

N_BRANCHES = 3
D_FF_2 = 4 * D_MODEL

IN_WIDTHS = (A_HEADS * HEAD_DIM, HEAD_DIM, HEAD_DIM,
             IDX_HEADS * IDX_DIM, IDX_DIM, IDX_HEADS,
             B_HEADS * HEAD_DIM, B_HEADS * HEAD_DIM, B_HEADS * HEAD_DIM,
             C_HEADS * HEAD_DIM, C_KV_HEADS * HEAD_DIM, C_KV_HEADS * HEAD_DIM,
             N_BRANCHES * D_MODEL)
IN_WIDTH = sum(IN_WIDTHS)


def rmsnorm(x, g):
    xf = x.astype(jnp.float32)
    y = xf * lax.rsqrt(jnp.mean(xf * xf, axis=-1, keepdims=True) + NORM_EPS)
    return (y * g.astype(jnp.float32)).astype(x.dtype)

def rope(x, pos):
    half = x.shape[-1] // 2
    inv = ROPE_THETA ** (-jnp.arange(half, dtype=jnp.float32) / half)
    ang = pos.astype(jnp.float32)[..., None] * inv
    cos = jnp.cos(ang)[:, :, None, :].astype(x.dtype)
    sin = jnp.sin(ang)[:, :, None, :].astype(x.dtype)
    x1, x2 = x[..., :half], x[..., half:]
    return jnp.concatenate([x1 * cos - x2 * sin, x2 * cos + x1 * sin], axis=-1)

def split_columns(z):
    parts, off = [], 0
    for w in IN_WIDTHS:
        parts.append(z[..., off:off + w])
        off += w
    return parts

def over_query_blocks(fn, seq_len):
    starts = jnp.arange(seq_len // BLOCK, dtype=jnp.int32) * BLOCK
    out = lax.map(fn, starts)
    out = jnp.moveaxis(out, 0, 1)
    return out.reshape(out.shape[0], seq_len, *out.shape[3:])

def dsa_attention(q, k, v, iq, ik, iw):
    L = q.shape[1]
    topk = min(TOPK_MAX, L // 4)
    scale = HEAD_DIM ** -0.5
    idx_scale = IDX_DIM ** -0.5
    s_all = jnp.arange(L)

    def block(t0):
        t = t0 + jnp.arange(BLOCK)
        qb = lax.dynamic_slice_in_dim(q, t0, BLOCK, 1)
        iqb = lax.dynamic_slice_in_dim(iq, t0, BLOCK, 1)
        iwb = lax.dynamic_slice_in_dim(iw, t0, BLOCK, 1).astype(jnp.float32)
        rel = jax.nn.relu(jnp.einsum('bqhd,bsd->bqhs', iqb, ik).astype(jnp.float32) * idx_scale)
        score = jnp.einsum('bqh,bqhs->bqs', iwb, rel)
        causal = s_all[None, :] <= t[:, None]
        score = jnp.where(causal[None], score, -jnp.inf)
        _, idx = lax.top_k(score, topk)
        ks = jax.vmap(lambda kk, ii: kk[ii])(k, idx)
        vs = jax.vmap(lambda vv, ii: vv[ii])(v, idx)
        valid = idx <= t[None, :, None]
        logits = jnp.einsum('bqhd,bqkd->bqhk', qb, ks).astype(jnp.float32) * scale
        logits = jnp.where(valid[:, :, None, :], logits, -jnp.inf)
        p = jax.nn.softmax(logits, axis=-1)
        return jnp.einsum('bqhk,bqkd->bqhd', p.astype(vs.dtype), vs)

    return over_query_blocks(block, L)

def dilated_attention(q, k, v):
    L = q.shape[1]
    scale = HEAD_DIM ** -0.5
    hg = B_HEADS_PER_GROUP
    qs = [q[:, :, g * hg:(g + 1) * hg] for g in range(len(B_GROUPS))]
    kss = [k[:, :, g * hg:(g + 1) * hg] for g in range(len(B_GROUPS))]
    vss = [v[:, :, g * hg:(g + 1) * hg] for g in range(len(B_GROUPS))]

    def block(t0):
        t = t0 + jnp.arange(BLOCK)
        outs, lses = [], []
        for g, (window, dil) in enumerate(B_GROUPS):
            qb = lax.dynamic_slice_in_dim(qs[g], t0, BLOCK, 1)
            pos = t[:, None] - dil * jnp.arange(window // dil + 1)[None, :]
            valid = pos >= 0
            pos_c = jnp.maximum(pos, 0)
            kg = kss[g][:, pos_c]
            vg = vss[g][:, pos_c]
            logits = jnp.einsum('bqhd,bqkhd->bqhk', qb, kg).astype(jnp.float32) * scale
            logits = jnp.where(valid[None, :, None, :], logits, -jnp.inf)
            m = jnp.max(logits, axis=-1, keepdims=True)
            e = jnp.exp(logits - m)
            den = jnp.sum(e, axis=-1)
            o = jnp.einsum('bqhk,bqkhd->bqhd', (e / den[..., None]).astype(vg.dtype), vg)
            outs.append(o)
            lses.append(m[..., 0] + jnp.log(den))
        alpha = jax.nn.softmax(jnp.stack(lses, 0), axis=0)
        return jnp.einsum('gbqh,gbqhd->bqhd', alpha.astype(outs[0].dtype), jnp.stack(outs, 0))

    return over_query_blocks(block, L)

def sink_window_attention(q, k, v, sinks):
    Bsz, L = q.shape[0], q.shape[1]
    grp = C_HEADS // C_KV_HEADS
    scale = HEAD_DIM ** -0.5
    pad = ((0, 0), (BLOCK, 0), (0, 0), (0, 0))
    kp = jnp.pad(k, pad)
    vp = jnp.pad(v, pad)
    qg = q.reshape(Bsz, L, C_KV_HEADS, grp, HEAD_DIM)
    sink = sinks.astype(jnp.float32).reshape(C_KV_HEADS, grp)[:, :, None, None]

    def block(t0):
        t = t0 + jnp.arange(BLOCK)
        s = t0 - BLOCK + jnp.arange(2 * BLOCK)
        qb = lax.dynamic_slice_in_dim(qg, t0, BLOCK, 1)
        kb = lax.dynamic_slice_in_dim(kp, t0, 2 * BLOCK, 1)
        vb = lax.dynamic_slice_in_dim(vp, t0, 2 * BLOCK, 1)
        mask = (s[None, :] <= t[:, None]) & (s[None, :] > t[:, None] - C_WINDOW) & (s[None, :] >= 0)
        logits = jnp.einsum('bqkgd,bskd->bkgqs', qb, kb).astype(jnp.float32) * scale
        logits = jnp.where(mask, logits, -jnp.inf)
        m = jnp.maximum(jnp.max(logits, axis=-1, keepdims=True), sink)
        e = jnp.exp(logits - m)
        den = jnp.sum(e, axis=-1, keepdims=True) + jnp.exp(sink - m)
        p = (e / den).astype(vb.dtype)
        o = jnp.einsum('bkgqs,bskd->bqkgd', p, vb)
        return o.reshape(Bsz, BLOCK, C_HEADS, HEAD_DIM)

    return over_query_blocks(block, L)

def hybrid_mixer_2(u, pos, w_in, idx_k_norm, sinks, w_a, w_b, w_c, w_o):
    Bsz, L, _ = u.shape
    (aq, ak, av, iq, ik, iw, bq, bk, bv, cq, ck, cv, gates) = split_columns(u @ w_in)
    qa = rope(aq.reshape(Bsz, L, A_HEADS, HEAD_DIM), pos)
    ka = rope(ak[:, :, None, :], pos)[:, :, 0]
    iqr = rope(iq.reshape(Bsz, L, IDX_HEADS, IDX_DIM), pos)
    ikr = rope(rmsnorm(ik, idx_k_norm)[:, :, None, :], pos)[:, :, 0]
    o_a = dsa_attention(qa, ka, av, iqr, ikr, iw * IDX_HEADS ** -0.5)
    o_b = dilated_attention(rope(bq.reshape(Bsz, L, B_HEADS, HEAD_DIM), pos),
                            rope(bk.reshape(Bsz, L, B_HEADS, HEAD_DIM), pos),
                            bv.reshape(Bsz, L, B_HEADS, HEAD_DIM))
    o_c = sink_window_attention(rope(cq.reshape(Bsz, L, C_HEADS, HEAD_DIM), pos),
                                rope(ck.reshape(Bsz, L, C_KV_HEADS, HEAD_DIM), pos),
                                cv.reshape(Bsz, L, C_KV_HEADS, HEAD_DIM), sinks)
    g = jax.nn.sigmoid(gates.reshape(Bsz, L, N_BRANCHES, D_MODEL))
    merged = (g[:, :, 0] * (o_a.reshape(Bsz, L, -1) @ w_a)
              + g[:, :, 1] * (o_b.reshape(Bsz, L, -1) @ w_b)
              + g[:, :, 2] * (o_c.reshape(Bsz, L, -1) @ w_c))
    return merged @ w_o

def second_inputs(seed: int = 0) -> dict:
    key = jax.random.key(seed)
    ks = jax.random.split(key, 15)

    def normal(k, shape, scale):
        return jax.random.normal(k, shape, jnp.float32) * scale

    def gain(k, shape):
        return 1.0 + 0.05 * jax.random.normal(k, shape, jnp.float32)

    x = normal(ks[0], (BATCH, SEQ, D_MODEL), 1.0)
    positions = jnp.tile(jnp.arange(SEQ, dtype=jnp.int32)[None, :], (BATCH, 1))
    return {
        "x": x,
        "positions": positions,
        "attn_norm": gain(ks[1], (DEPTH, D_MODEL)),
        "w_in": normal(ks[2], (DEPTH, D_MODEL, IN_WIDTH), D_MODEL ** -0.5),
        "idx_k_norm": gain(ks[3], (DEPTH, IDX_DIM)),
        "sinks": normal(ks[4], (DEPTH, C_HEADS), 0.5),
        "w_a": normal(ks[5], (DEPTH, A_HEADS * HEAD_DIM, D_MODEL), (A_HEADS * HEAD_DIM) ** -0.5),
        "w_b": normal(ks[6], (DEPTH, B_HEADS_PER_GROUP * HEAD_DIM, D_MODEL), (B_HEADS_PER_GROUP * HEAD_DIM) ** -0.5),
        "w_c": normal(ks[7], (DEPTH, C_HEADS * HEAD_DIM, D_MODEL), (C_HEADS * HEAD_DIM) ** -0.5),
        "w_o": normal(ks[8], (DEPTH, D_MODEL, D_MODEL), D_MODEL ** -0.5),
        "mlp_norm": gain(ks[9], (DEPTH, D_MODEL)),
        "w_up": normal(ks[10], (DEPTH, D_MODEL, D_FF_2), D_MODEL ** -0.5),
        "w_down": normal(ks[11], (DEPTH, D_FF_2, D_MODEL), D_FF_2 ** -0.5),
        "final_norm": gain(ks[12], (D_MODEL,)),
    }

def second_block(x, positions, attn_norm, w_in, idx_k_norm, sinks, w_a, w_b, w_c, w_o,
              mlp_norm, w_up, w_down, final_norm):
    h = x
    for l in range(DEPTH):
        u = rmsnorm(h, attn_norm[l])
        h = h + hybrid_mixer_2(u, positions, w_in[l], idx_k_norm[l], sinks[l],
                             w_a[l], w_b[l], w_c[l], w_o[l])
        u = rmsnorm(h, mlp_norm[l])
        h = h + jnp.square(jax.nn.relu(u @ w_up[l])) @ w_down[l]
    return rmsnorm(h, final_norm)


def setup_inputs(seed=0):
    out = dict(first_inputs(seed))
    for name, value in second_inputs(seed + 1).items():
        if name != "x":
            out[name + "_2"] = value
    return out


def reference(
    x, mix_pre_norm, mix_post_norm, w_in, dn_conv, dn_A_log, dn_dt_bias, dn_out_norm,
    ret_out_norm, pool_w, pool_scale, w_branch_dn, w_branch_ret, w_branch_pool, w_out,
    ffn_pre_norm, ffn_post_norm, ffn_gate, ffn_up, ffn_down, positions_2, attn_norm_2, w_in_2,
    idx_k_norm_2, sinks_2, w_a_2, w_b_2, w_c_2, w_o_2, mlp_norm_2, w_up_2, w_down_2,
    final_norm_2,
):
    x = first_block(
        x, mix_pre_norm, mix_post_norm, w_in, dn_conv, dn_A_log, dn_dt_bias, dn_out_norm,
        ret_out_norm, pool_w, pool_scale, w_branch_dn, w_branch_ret, w_branch_pool, w_out,
        ffn_pre_norm, ffn_post_norm, ffn_gate, ffn_up, ffn_down,
    )
    return second_block(
        x, positions_2, attn_norm_2, w_in_2, idx_k_norm_2, sinks_2, w_a_2, w_b_2, w_c_2, w_o_2,
        mlp_norm_2, w_up_2, w_down_2, final_norm_2,
    )


_drawn_inputs = setup_inputs


def setup_inputs(seed=0):
    import zlib

    import numpy as np

    out = dict(_drawn_inputs(seed))
    spreads = {}
    factors = {'attn_norm_2': 3.274, 'idx_k_norm_2': 5.746, 'sinks_2': 8.0}
    for name, (base, spread) in spreads.items():
        noise = np.random.default_rng([zlib.crc32(name.encode()), seed]).standard_normal(out[name].shape)
        drawn = base * np.exp(spread * noise) if base else spread * noise
        out[name] = __import__('jax').numpy.asarray(drawn.astype(out[name].dtype))
    for name, factor in factors.items():
        out[name] = (out[name] * factor).astype(out[name].dtype)
    return out
```

```python
from contextlib import ExitStack

import numpy as np
import concourse.bass as bass
from concourse import mybir

F32 = mybir.dt.float32
F32R = mybir.dt.float32r
I32 = mybir.dt.int32
OP = mybir.AluOpType
AF = mybir.ActivationFunctionType
AX = mybir.AxisListType.X

P = 128
T = 256
D = 1024
DEPTH = 2
FF1 = 2816
FF2 = 4096
NEG = -1.0e30
TAKEN = -3.0e38
RAW = 4
RING = 3
NCHUNK = 572
EXPLN = "natural_log_exp_and_others"

CONST1 = {}
CONST2 = {}


def _columns(table, widths):
    at = 0
    for name, w in widths:
        table[name] = (at, w)
        at += w
    return at


N_CONST1 = _columns(CONST1, [
    ("ones", 128), ("eye", 128), ("eps6", 1), ("eps5", 1), ("one", 1), ("pad", 1),
    ("upper", 128), ("chunk", 128), ("lev", 6 * 128), ("levT", 6 * 128), ("rot", 128),
    ("cos", 256), ("sin", 256), ("rmask", 4 * 128), ("xi", 4 * 256), ("zeta", 4), ("cnt", 4 * 256)])
N_CONST2 = _columns(CONST2, [
    ("ones", 128), ("eye", 128), ("eps6", 1), ("eps5", 1), ("one", 1), ("pad", 1),
    ("half", 128), ("rot2", 128), ("inv", 1), ("mB0", 3 * 128), ("mB1", 3 * 256),
    ("mA0", 128), ("mA1", 256), ("mC0", 128), ("mC1", 256)])
N_CONST = max(N_CONST1, N_CONST2)

PAR1 = {}
PAR2 = {}
N_PAR1 = _columns(PAR1, [("mixpre", 8), ("mixpost", 8), ("ffnpre", 8), ("ffnpost", 8), ("conv", 48),
                         ("dnout", 1), ("retout", 4), ("pscale", 4), ("alog", 8), ("dtb", 8)])
N_PAR2 = _columns(PAR2, [("attn", 8), ("mlp", 8), ("final", 8), ("idxk", 1), ("sinks", 8)])
N_PAR = max(N_PAR1, N_PAR2)
N_SMALL = 64 + 512


class Engine:

    def __init__(self, sem):
        self.sem, self.queue, self.count, self.seen = sem, [], 0, {}

    def wait(self, *tokens):
        for sem, value in tokens:
            if self.seen.get(id(sem), 0) < value:
                self.seen[id(sem)] = value
                self.queue.append(lambda e, s=sem, v=value: e.wait_ge(s, v))

    def do(self, fn, *after):
        self.wait(*after)
        self.count += 1
        self.queue.append(lambda e, s=self.sem: fn(e).then_inc(s, 1))
        return (self.sem, self.count)

    def quiet(self, fn, *after):
        self.wait(*after)
        self.queue.append(fn)

    def done(self):
        return (self.sem, self.count)

    def play(self, e):
        for fn in self.queue:
            fn(e)


class Vec(Engine):
    def tt(self, out, a, b, op, *after):
        return self.do(lambda e: e.tensor_tensor(out, a, b, op), *after)

    def ts(self, out, a, s1, s2, op0, op1, *after):
        if op1 is None:
            return self.do(lambda e: e.tensor_scalar(out, a, s1, None, op0), *after)
        return self.do(lambda e: e.tensor_scalar(out, a, s1, s2, op0, op1), *after)

    def stt(self, out, a, s, b, op0, op1, *after):
        return self.do(lambda e: e.scalar_tensor_tensor(out=out, in0=a, scalar=s, in1=b, op0=op0, op1=op1), *after)

    def copy(self, out, a, *after):
        return self.do(lambda e: e.tensor_copy(out, a), *after)

    def red(self, out, a, op, *after):
        return self.do(lambda e: e.tensor_reduce(out, a, AX, op), *after)

    def recip(self, out, a, *after):
        return self.do(lambda e: e.reciprocal(out, a), *after)


class Act(Engine):
    table = None

    def act(self, out, a, fn, *after, scale=1.0, bias=None, accum=None):
        if fn in (AF.Exp, AF.Ln):
            want = EXPLN
        elif fn in (AF.Silu, AF.Sigmoid, AF.Sin):
            want = str(fn)
        else:
            want = None
        if want and want != self.table:
            self.table = want
            if want == EXPLN:
                self.queue.append(lambda e: e.preload_act_table_set(EXPLN))
        kw = {"scale": scale}
        if bias is not None:
            kw["bias"] = bias
        if accum is not None:
            kw["accum_out"] = accum
        return self.do(lambda e: e.activation(out, a, fn, **kw), *after)

    def copy(self, out, a, *after):
        return self.do(lambda e: e.copy(out, a), *after)


class Bank:

    def __init__(self, t):
        self.t, self.free = t, ()


def wide(ap, axis, n):
    shape = list(ap.shape)
    shape.insert(axis, n)
    return ap.unsqueeze(axis).broadcast_to(shape)


def program(nc, ins, out):
    ctx = ExitStack()
    with ctx:
        sem = lambda name: ctx.enter_context(nc.semaphore(name))
        S, A, V, G, E = Engine(sem("sp")), Act(sem("act")), Vec(sem("dve")), Vec(sem("pool")), Engine(sem("pe"))
        s_raw = [sem(f"raw{i}") for i in range(RAW)]
        s_load = sem("load")
        s_out = sem("out")
        loads = [0]

        at = [16640]

        def sb(name, shape, dt=F32, offset=None):
            n = 4
            for x in shape[1:]:
                n *= x
            if offset is None:
                offset = at[0]
                at[0] += (n + 31) // 32 * 32
            return nc.alloc_sbuf_tensor_at(name, shape, dt, offset=offset)

        xT = sb("xT", [P, 8, T])
        hh = sb("hh", [P, 8, T], F32R)
        hl = sb("hl", [P, 8, T], F32R)
        raw = sb("raw", [P, RAW, 1024])
        whi = sb("whi", [P, RING, 1024], F32R)
        wlo = sb("wlo", [P, RING, 1024], F32R)
        cst = sb("cst", [P, N_CONST])
        par = sb("par", [P, N_PAR])
        small = sb("small", [P, N_SMALL])
        region = at[0]
        nslots = (nc.sbuf_usable_end - region) // 4096
        assert nslots >= 30, nslots

        area = nc.alloc_sbuf_tensor_at("area", [P, 30 * 1024], F32, offset=region)

        def slot(name, i, n=1, dt=F32, shape=None):
            if dt == F32R:
                return sb(name, shape, dt, offset=region + 4096 * i)
            v = area[:, 1024 * i:1024 * (i + n)]
            return v.bitcast(dt) if dt != F32 else v

        banks = [Bank(ctx.enter_context(nc.psum_tensor(f"bank{i}", [P, 512], F32))) for i in range(8)]

        def C(name, table=None):
            o, w = (table or consts[0])[name]
            return cst[:, o:o + w]

        def Q(name, table=None):
            o, w = (table or pars[0])[name]
            return par[:, o:o + w]

        consts, pars = [CONST1], [PAR1]

        def load(dst, src, *after):
            S.wait(*after)
            S.queue.append(lambda e: e.dma_start(dst, src).then_inc(s_load, 16))
            loads[0] += 16
            return (s_load, loads[0])

        order = []
        hi_done, lo_done, used = {}, {}, {}
        staged = [0]
        fetched = [0]

        def fetch():
            i = fetched[0]
            if i >= NCHUNK:
                return
            fetched[0] += 1
            if i >= RAW:
                S.wait(hi_done[i - RAW], lo_done[i - RAW])
            r = i % RAW
            S.queue.append(lambda e: e.dma_start(raw[:, r, :], ins["weights"][i]).then_inc(s_raw[r], 16))

        def stage():
            i = staged[0]
            if i >= NCHUNK:
                return
            staged[0] += 1
            r, h = i % RAW, i % RING
            landed = (s_raw[r], 16 * (i // RAW + 1))
            free = [used[i - RING]] if i >= RING else []
            hi_done[i] = A.copy(whi[:, h, :], raw[:, r, :], landed, *free)
            lo_done[i] = V.tt(wlo[:, h, :], raw[:, r, :], whi[:, h, :].bitcast(F32), OP.subtract, hi_done[i], landed, *free)
            fetch()

        def chunk(what):
            i = len(order)
            order.append(what)
            while staged[0] < min(i + RING, NCHUNK):
                stage()
            E.wait(hi_done[i], lo_done[i])
            return i, whi[:, i % RING, :], wlo[:, i % RING, :]

        def mm(ps, l, r, first, last, *after, skip=False, done=False):
            fn = lambda e: e.matmul(ps, l, r, start=first, stop=last, skip_group_check=skip)
            return E.do(fn, *after) if done else E.quiet(fn, *after)

        def mm3(ps, w, x, first, last, wstat=True, skip=False, done=False):
            (wh, wl), (xh, xl) = w, x
            tok = None
            for n, (a, b) in enumerate(((wh, xh), (wh, xl), (wl, xh))):
                if not wstat:
                    a, b = b, a
                tok = mm(ps, a, b, first and n == 0, last and n == 2, skip=skip, done=done and n == 2)
            return tok

        ring = [0, [4, 5, 6, 7]]

        def next_bank():
            b = banks[ring[1][ring[0] % len(ring[1])]]
            ring[0] += 1
            return b

        def project(what, ntile, xs, nk, xtok, evac):
            E.wait(*xtok)
            total, at_ = nk * ntile, 0
            cur = None
            for m0 in range(0, ntile, 2):
                b = next_bank()
                E.wait(*b.free)
                n = min(2, ntile - m0)
                for m in range(m0, m0 + n):
                    for k in range(nk):
                        if at_ % 8 == 0:
                            cur = chunk((*what, at_ // 8))
                        i, wh, wl = cur
                        c = at_ % 8 * 128
                        at_ += 1
                        tok = mm3(b.t[:, (m - m0) * T:(m - m0 + 1) * T], (wh[:, c:c + 128], wl[:, c:c + 128]),
                                  (xs[0][:, k, :], xs[1][:, k, :]), k == 0, k == nk - 1,
                                  done=(at_ % 8 == 0 or k == nk - 1))
                        if at_ % 8 == 0:
                            used[i] = tok
                evac(m0, n, b, tok)
                yield

        def by_token(what, xtok, evac):
            E.wait(*xtok)
            bb = [next_bank(), next_bank()]
            for b in bb:
                E.wait(*b.free)
            for c in range(4):
                i, wh, wl = chunk((*what, c))
                for j in range(2):
                    k = 2 * c + j
                    w = (wh[:, 512 * j:512 * j + 512], wl[:, 512 * j:512 * j + 512])
                    for s in range(2):
                        x = (hh[:, k, 128 * s:128 * s + 128], hl[:, k, 128 * s:128 * s + 128])
                        tok = mm3(bb[s].t[:, :], w, x, k == 0, k == 7, wstat=False, done=(j == 1 and s == 1))
                used[i] = tok
            for s in range(2):
                evac(s, bb[s], tok)
            yield

        def down(what, nk, ah, al, ready, evac):
            bb = banks[0:4]
            for b in bb:
                E.wait(*b.free)
            for k in range(nk):
                E.wait(*ready[k])
                i, wh, wl = chunk((*what, k))
                for m in range(8):
                    tok = mm3(bb[m // 2].t[:, (m % 2) * T:(m % 2 + 1) * T], (wh[:, 128 * m:128 * m + 128], wl[:, 128 * m:128 * m + 128]),
                              (ah[:, k, :], al[:, k, :]), k == 0 and m % 2 == 0, k == nk - 1, skip=True, done=m == 7)
                used[i] = tok
            for j, b in enumerate(bb):
                evac(2 * j, 2, b, tok)

        def run(gen, fill=None, ratio=1):
            for _ in gen:
                for _ in range(ratio):
                    if fill is not None:
                        next(fill, None)

        def chain(*gens):
            for g in gens:
                yield from g

        def rstd_of(bank, n, scale, eps, out_ap, *after):
            a = A.act(out_ap, bank.t[:, 0:n], AF.Ln, *after, scale=scale, bias=eps)
            r = A.act(out_ap, out_ap, AF.Exp, a, scale=-0.5)
            bank.free = (a,)
            return r

        def norm_stats(src, ready, sq, rstd, scale=1.0 / D):
            s = A.act(sq[:, :], src.rearrange("p k t -> p (k t)") if len(src.shape) == 3 else src, AF.Square, *ready)
            b = next_bank()
            E.wait(s, *b.free)
            for k in range(8):
                t = mm(b.t[:, 0:T], C("ones"), sq[:, k * T:(k + 1) * T], k == 0, k == 7, done=k == 7)
            return rstd_of(b, T, scale, C("eps6"), rstd, t)

        def split_norm(gain, sq, rstd, ready, hfree):
            r = norm_stats(xT[:, :, :], ready, sq, rstd, 1.0 / D)
            for k in range(8):
                t = V.stt(sq[:, k * T:(k + 1) * T], xT[:, k, :], gain[:, k:k + 1], rstd, OP.mult, OP.mult, r)
            return split(hh[:, :, :].rearrange("p k t -> p (k t)"), hl[:, :, :].rearrange("p k t -> p (k t)"), sq[:, :], (t, *hfree))

        def split(h, l, src, ready):
            a = A.copy(h, src, *ready)
            b = V.tt(l, src, h.bitcast(F32), OP.subtract, a)
            return (a, b)

        def post_norm(m, gain, sq, rstd, ready):
            r = norm_stats(m[:, :], ready, sq, rstd)
            for k in range(8):
                t = V.stt(sq[:, k * T:(k + 1) * T], m[:, k * T:(k + 1) * T], gain[:, k:k + 1], rstd, OP.mult, OP.mult, r)
            return V.tt(xT[:, :, :].rearrange("p k t -> p (k t)"), xT[:, :, :].rearrange("p k t -> p (k t)"), sq[:, :], OP.add, t)

        def everything():
            return tuple(x.done() for x in (A, V, G, E))

        U = slot("U", 0, 3)
        KT, KB, VB = slot("KT", 0), slot("KB", 1), slot("VB", 2)
        Aq, Ak, Av = slot("Aq", 3), slot("Ak", 4), slot("Av", 5)
        QKV = slot("QKV", 3, 3)
        QK = slot("QK", 3, 2)
        SQ = slot("SQ", 6, 2)
        T0, EG, DT, M, MT, AT = (slot(n, 6 + i) for i, n in enumerate(("T0", "EG", "DT", "M", "MT", "AT")))
        X, Y, LT = slot("X", 12), slot("Y", 13), slot("LT", 14)
        SV = slot("SV", 15)
        SM = slot("SM", 16)
        Z = slot("Z", 17)
        RQ, RK, RV, RG, PU = (slot(n, 18 + i) for i, n in enumerate(("RQ", "RK", "RV", "RG", "PU")))
        RQK = slot("RQK", 18, 2)
        GT = slot("GT", 23, 2)
        YY = slot("YY", 25, 2)
        OD = slot("OD", 27)
        BH, BL = slot("BH", 28, dt=F32R, shape=[P, 4, T]), slot("BL", 29, dt=F32R, shape=[P, 4, T])
        R0, R1 = slot("R0", 0, 2), slot("R1", 2, 2)
        KZ, ST, RR, OR, SR, O2 = slot("KZ", 4), slot("ST", 5), slot("RR", 6, 2), slot("OR", 8), slot("SR", 9), slot("O2", 10)
        PA, PB, PC = slot("PA", 11), slot("PB", 12), slot("PC", 13)
        FH, FL = slot("FH", 0, dt=F32R, shape=[P, 32, T]), slot("FL", 8, dt=F32R, shape=[P, 32, T])
        FT = slot("FT", 16, 2)
        NSQ, NM = slot("NSQ", 18, 2), slot("NM", 20, 2)
        NR = slot("NR", 22)
        MO = slot("MO", 0, 2)
        MSQ = slot("MSQ", 2, 2)
        MR = slot("MR", 4)

        def v3(t, n=T):
            return t[:, :].rearrange("p (m t) -> p m t", t=n)

        def copy_to(dst, toks):
            def evac(m0, n, b, tok):
                t = A.copy(dst[:, m0 * T:(m0 + n) * T], b.t[:, 0:n * T], tok)
                b.free = (t,)
                toks.append(t)
            return evac

        def branch(what, src, ready, nk, gate, gready, first, ydone, bfree):
            n = nk * T
            s = split(BH[:, 0:nk, :].rearrange("p k t -> p (k t)"), BL[:, 0:nk, :].rearrange("p k t -> p (k t)"), src, (*ready, *bfree))
            g = A.act(gate[:, :], gate[:, :], AF.Sigmoid, *gready)

            def evac(m0, n, b, tok):
                c = slice(m0 * T, (m0 + n) * T)
                if first:
                    t = V.tt(YY[:, c], b.t[:, 0:n * T], gate[:, c], OP.mult, tok, g)
                    b.free = (t,)
                else:
                    u = V.tt(gate[:, c], b.t[:, 0:n * T], gate[:, c], OP.mult, tok, g)
                    b.free = (u,)
                    t = V.tt(YY[:, c], YY[:, c], gate[:, c], OP.add, u)
                ydone.append(t)
            return project(what, 8, (BH, BL), nk, s, evac)

        def delta_rule(qkv, z, abtok, out):
            B0, B1, B2, B3 = banks[0:4]
            bk = lambda b: b.t[:, :]
            s = A.act(SQ[:, :], QK[:, :], AF.Square, *qkv)
            for j in range(4):
                E.wait(s, *banks[j].free)
                t = mm(bk(banks[j]), C("ones"), SQ[:, 512 * j:512 * j + 512], True, True, done=True)
                r = A.act(SQ[:, 512 * j:512 * j + 512], bk(banks[j]), AF.Ln, t, bias=C("eps6"))
                banks[j].free = (r,)
            r = A.act(SQ[:, :], SQ[:, :], AF.Exp, r, scale=-0.5)
            n1 = V.stt(Aq[:, :], Aq[:, :], 128.0 ** -0.5, SQ[:, 0:1024], OP.mult, OP.mult, r)
            n2 = V.tt(Ak[:, :], Ak[:, :], SQ[:, 1024:2048], OP.mult, r)
            yield
            a_, be, g_, G_, eg, kx = (SM[:, 16 * i:16 * i + 8] for i in range(6))
            u1, u2 = SM[:, 128:136], SM[:, 144:152]
            AB = SM[:, 192:208].rearrange("p (s c) -> p c s", s=2)
            hs = lambda ap: ap.rearrange("p (h s) -> p h s", s=2)
            e1 = A.act(hs(be), AB[:, 0:4, :], AF.Exp, *abtok, scale=-1.0)
            w = V.ts(be, be, 1.0, None, OP.add, None, e1)
            bdone = V.recip(be, be, w)
            w = V.tt(hs(a_), AB[:, 4:8, :], hs(Q("dtb")), OP.add, *abtok)
            w1 = V.ts(u1, a_, -1.0, None, OP.mult, None, w)
            w1 = V.tt(u1, u1, a_, OP.max, w1)
            e1 = A.act(u1, u1, AF.Exp, w1, scale=-1.0)
            e1 = A.act(u1, u1, AF.Ln, e1, bias=C("one"))
            w = V.stt(a_, a_, 0.0, u1, OP.max, OP.add, e1)
            e2 = A.act(u2, Q("alog"), AF.Exp, abtok[0])
            gd = V.stt(g_, a_, -1.0, u2, OP.mult, OP.mult, w, e2)
            rg = V.tt(v3(T0, 128), wide(C("upper"), 1, 8), wide(g_, 2, 128), OP.mult, gd, s, r, n1, n2)
            E.wait(rg)
            for j in range(2):
                E.wait(*banks[j].free)
                t = mm(bk(banks[j]), C("ones"), T0[:, 512 * j:512 * j + 512], True, True, done=True)
            E.wait(*B2.free)
            mm(B2.t[:, 0:8], C("upper"), g_, True, True)
            t2 = mm(B2.t[:, 8:16], C("chunk"), g_, True, True, done=True)
            yield
            d1 = V.copy(SM[:, 48:64], B2.t[:, 0:16], t2)
            B2.free = (d1,)
            G_, GL = SM[:, 48:56], SM[:, 56:64]
            w = V.tt(kx, GL, G_, OP.subtract, d1)
            e3 = A.act(eg, G_, AF.Exp, d1)
            e4 = A.act(kx, kx, AF.Exp, w)
            w3 = V.tt(eg, eg, be, OP.mult, e3, bdone)
            for j in range(2):
                c = slice(512 * j, 512 * j + 512)
                a = A.act(EG[:, c], bk(banks[j]), AF.Exp, t)
                b = V.tt(DT[:, c].rearrange("p (b t) -> p b t", t=128), bk(banks[j]).rearrange("p (b t) -> p b t", t=128),
                         wide(G_[:, 4 * j:4 * j + 4], 2, 128), OP.subtract, a, d1)
                banks[j].free = (b,)
            b = V.tt(v3(DT, 128), v3(DT, 128), wide(C("upper"), 1, 8), OP.mult, b)
            b = A.act(DT[:, :], DT[:, :], AF.Exp, b)
            dt = V.tt(v3(DT, 128), v3(DT, 128), wide(C("upper"), 1, 8), OP.mult, b)
            yield
            kb3 = lambda t, b: t[:, 128 * b:128 * b + 128]
            E.wait(n1, n2)
            for j in range(2):
                E.wait(*banks[j].free)
                for b in range(4 * j, 4 * j + 4):
                    t = mm(banks[j].t[:, 128 * (b % 4):128 * (b % 4) + 128], kb3(Ak, b), kb3(Ak, b), True, True, done=b % 4 == 3)
            E.wait(dt)
            for j in range(2):
                E.wait(*banks[2 + j].free)
                for b in range(4 * j, 4 * j + 4):
                    fn = lambda e, o=banks[2 + j].t[:, 128 * (b % 4):128 * (b % 4) + 128], i=kb3(DT, b): e.transpose(o, i, C("eye", CONST1))
                    if b % 4 == 3:
                        tt_ = E.do(fn)
                    else:
                        E.quiet(fn)
            for j in range(2):
                c = slice(512 * j, 512 * j + 512)
                w = V.tt(M[:, c].rearrange("p (b t) -> p b t", t=128), bk(banks[j]).rearrange("p (b t) -> p b t", t=128),
                         wide(be[:, 4 * j:4 * j + 4], 2, 128), OP.mult, t, bdone)
                banks[j].free = (w,)
                w = V.tt(M[:, c], M[:, c], bk(banks[2 + j]), OP.mult, w, tt_)
                banks[2 + j].free = (w,)
            md = w
            yield
            def transposed(src, bb, *after):
                E.wait(*after)
                for j in range(2):
                    E.wait(*bb[j].free)
                    for b in range(4 * j, 4 * j + 4):
                        fn = lambda e, o=bb[j].t[:, 128 * (b % 4):128 * (b % 4) + 128], i=kb3(src, b): e.transpose(o, i, C("eye", CONST1))
                        if b % 4 == 3:
                            tok = E.do(fn)
                        else:
                            E.quiet(fn)
                return tok

            def scaled(dst, bb, by, tok, *after):
                for j in range(2):
                    w = V.tt(dst[:, 512 * j:512 * j + 512].rearrange("p (b t) -> p b t", t=128),
                             bk(bb[j]).rearrange("p (b t) -> p b t", t=128), wide(by[:, 4 * j:4 * j + 4], 2, 128), OP.mult, tok, *after)
                    bb[j].free = (w,)
                return w

            t = transposed(M, (B0, B1), md)
            for j in range(2):
                mt = A.copy(MT[:, 512 * j:512 * j + 512], bk(banks[j]), t)
                banks[j].free = (mt,)
            lev = lambda s, tr=False: C("levT" if tr else "lev")[:, 128 * s:128 * s + 128]
            w = V.tt(v3(X, 128), v3(M, 128), wide(lev(0), 1, 8), OP.mult, md)
            xd = V.stt(v3(X, 128), v3(X, 128), -1.0, wide(C("eye"), 1, 8), OP.mult, OP.add, w)
            w = V.tt(v3(Y, 128), v3(MT, 128), wide(lev(0, True), 1, 8), OP.mult, mt)
            yd = V.stt(v3(Y, 128), v3(Y, 128), -1.0, wide(C("eye"), 1, 8), OP.mult, OP.add, w)
            lt = G.tt(v3(LT, 128), v3(MT, 128), wide(lev(1, True), 1, 8), OP.mult, mt)
            yield
            for j in range(2):
                E.wait(*banks[2 + j].free)
                for b in range(4 * j, 4 * j + 4):
                    t = mm(banks[2 + j].t[:, 128 * (b % 4):128 * (b % 4) + 128], kb3(Ak, b), kb3(Aq, b), True, True, done=b % 4 == 3)
            for j in range(2):
                c = slice(512 * j, 512 * j + 512)
                atd = V.tt(AT[:, c], DT[:, c], bk(banks[2 + j]), OP.mult, t)
                banks[2 + j].free = (atd,)
            qd = G.tt(Aq[:, :], Aq[:, :], EG[:, :], OP.mult, t, a)
            yield
            side = [0]

            def extra():
                if side[0] == 0:
                    tk = transposed(Ak, (B2, B3))
                    w1 = scaled(KT, (B2, B3), kx, tk, e4)
                    side.append(w1)
                elif side[0] == 1:
                    tk = transposed(Ak, (B2, B3))
                    side.append(scaled(KB, (B2, B3), eg, tk, w3))
                elif side[0] == 2:
                    tk = transposed(Av, (B2, B3), *qkv)
                    side.append(scaled(VB, (B2, B3), be, tk, bdone))
                side[0] += 1

            for s_ in range(1, 6):
                E.wait(lt, xd, yd)
                for j in range(2):
                    E.wait(*banks[j].free)
                    for b in range(4 * j, 4 * j + 4):
                        t = mm(banks[j].t[:, 128 * (b % 4):128 * (b % 4) + 128], kb3(LT, b), kb3(X, b), True, True, done=b % 4 == 3)
                for j in range(2):
                    w = A.copy(T0[:, 512 * j:512 * j + 512], bk(banks[j]), t)
                    banks[j].free = (w,)
                if s_ < 5:
                    lt = G.tt(v3(LT, 128), v3(MT, 128), wide(lev(s_ + 1, True), 1, 8), OP.mult, t)
                yield
                E.wait(w)
                if s_ < 5:
                    for j in range(2):
                        E.wait(*banks[j].free)
                        for b in range(4 * j, 4 * j + 4):
                            t1 = mm(banks[j].t[:, 128 * (b % 4):128 * (b % 4) + 128], kb3(Y, b), kb3(T0, b), True, True, done=b % 4 == 3)
                for j in range(2):
                    E.wait(*banks[2 + j].free)
                    for b in range(4 * j, 4 * j + 4):
                        t2 = mm(banks[2 + j].t[:, 128 * (b % 4):128 * (b % 4) + 128], kb3(T0, b), kb3(Y, b), True, True, done=b % 4 == 3)
                for j in range(2):
                    c = slice(512 * j, 512 * j + 512)
                    if s_ < 5:
                        xd = V.tt(X[:, c], X[:, c], bk(banks[j]), OP.subtract, t1)
                        banks[j].free = (xd,)
                    yd = V.tt(Y[:, c], Y[:, c], bk(banks[2 + j]), OP.subtract, t2)
                    banks[2 + j].free = (yd,)
                extra()
                yield
            ktd, kbd, vbd = side[1:4]
            E.wait(kbd, vbd, yd)
            for j in range(2):
                E.wait(*banks[j].free)
                for b in range(4 * j, 4 * j + 4):
                    t = mm(banks[j].t[:, 128 * (b % 4):128 * (b % 4) + 128], kb3(KB, b), kb3(Y, b), True, True, done=b % 4 == 3)
            for j in range(2):
                E.wait(*banks[2 + j].free)
                for b in range(4 * j, 4 * j + 4):
                    t2 = mm(banks[2 + j].t[:, 128 * (b % 4):128 * (b % 4) + 128], kb3(Y, b), kb3(VB, b), True, True, done=b % 4 == 3)
            for j in range(2):
                c = slice(512 * j, 512 * j + 512)
                wt = A.copy(M[:, c], bk(banks[j]), t)
                banks[j].free = (wt,)
                ud = A.copy(MT[:, c], bk(banks[2 + j]), t2)
                banks[2 + j].free = (ud,)
            yield
            St, VN = SV[:, 0:512], SV[:, 512:1024]
            hv = lambda ap: ap.rearrange("p (h t) -> p h t", h=4)
            sd = None
            OB = (B2, B3)
            for n in range(4):
                half, q = n // 2, n % 2
                r = slice(64 * q, 64 * q + 64)
                u_c = hv(MT[:, :])[r, :, 128 * half:128 * half + 128]
                if n == 0:
                    vn = V.copy(hv(VN)[r], u_c, ud)
                else:
                    E.wait(sd, wt, *B0.free)
                    for h in range(4):
                        c0 = 256 * h + 128 * half + 64 * q
                        t = mm(B0.t[r, 128 * h:128 * h + 128], M[:, c0:c0 + 64], St[:, 128 * h:128 * h + 128], True, True, done=h == 3)
                    vn = V.stt(hv(VN)[r], hv(B0.t[r, :]), -1.0, u_c, OP.mult, OP.add, t, ud)
                    B0.free = (vn,)
                yield
                E.wait(vn, ktd, *B1.free)
                for h in range(4):
                    b = 2 * h + half
                    t = mm(B1.t[:, 128 * h:128 * h + 128], KT[r, 128 * b:128 * b + 128], hv(VN)[r, h, :], True, True, done=h == 3)
                E.wait(atd, qd, *(OB[0].free + OB[1].free if n == 0 else ()))
                for h in range(4):
                    b = 2 * h + half
                    o = OB[h // 2].t[:, 256 * (h % 2) + 64 * n:256 * (h % 2) + 64 * n + 64]
                    if n:
                        mm(o, St[:, 128 * h:128 * h + 128], Aq[:, 256 * h + 64 * n:256 * h + 64 * n + 64], True, False)
                    to = mm(o, hv(VN)[r, h, :], AT[r, 128 * b + 64 * q:128 * b + 64 * q + 64], n == 0, True, done=h == 3)
                if n < 3:
                    dl = wide(v3(EG)[:, :, 64 * n + 63], 2, 128)
                    if n == 0:
                        sd = V.copy(St, bk(B1), t)
                    else:
                        sd = V.tt(hv(St), hv(St), dl, OP.mult, t, to)
                        sd = V.tt(St, St, bk(B1), OP.add, sd)
                    B1.free = (sd,)
                yield
            for j in range(2):
                o = A.copy(OD[:, 512 * j:512 * j + 512], bk(OB[j]), to)
                OB[j].free = (o,)
            s = A.act(T0[:, :], OD[:, :], AF.Square, o)
            E.wait(s)
            for j in range(2):
                E.wait(*banks[j].free)
                t = mm(bk(banks[j]), C("ones"), T0[:, 512 * j:512 * j + 512], True, True, done=True)
                a = A.act(EG[:, 512 * j:512 * j + 512], bk(banks[j]), AF.Ln, t, to, sd, scale=1.0 / 128, bias=C("eps6"))
                banks[j].free = (a,)
            a = A.act(EG[:, :], EG[:, :], AF.Exp, a, scale=-0.5)
            z_ = A.act(Z[:, :], Z[:, :], AF.Silu, *z)
            w = V.stt(OD[:, :], OD[:, :], Q("dnout"), EG[:, :], OP.mult, OP.mult, a)
            w = V.tt(OD[:, :], OD[:, :], Z[:, :], OP.mult, w, z_)
            out.append(w)

        def pooling(pu, poolw, out):
            PU3, A3, B3_, C3 = v3(PU), v3(PA), v3(PB), v3(PC)
            w = G.copy(A3, PU3, *pu, *everything())
            w = G.tt(A3[:, :, 1:T], PU3[:, :, 1:T], PU3[:, :, 0:T - 1], OP.add, w)
            w = G.copy(B3_, A3, w)
            w = G.tt(B3_[:, 1:4, 2:T], A3[:, 1:4, 2:T], A3[:, 1:4, 0:T - 2], OP.add, w)
            w = G.copy(A3[:, 2:4, :], B3_[:, 2:4, :], w)
            w = G.tt(A3[:, 2:4, 4:T], B3_[:, 2:4, 4:T], B3_[:, 2:4, 0:T - 4], OP.add, w)
            w = G.copy(B3_[:, 2:4, :], A3[:, 2:4, :], w)
            w = G.tt(B3_[:, 3:4, 8:T], A3[:, 3:4, 8:T], A3[:, 3:4, 0:T - 8], OP.add, w)
            w = G.tt(PB[:, :], PB[:, :], C("cnt"), OP.mult, w)
            w = G.tt(PB[:, :], PB[:, :], PU[:, :], OP.subtract, w)
            yield
            b0, b1 = banks[2], banks[3]
            E.wait(w, poolw)
            for g in range(4):
                b = (b0, b1)[g // 2]
                E.wait(*b.free)
                t = mm(b.t[:, T * (g % 2):T * (g % 2) + T], small[:, 64 + 128 * g:64 + 128 * g + 128], PB[:, T * g:T * g + T], True, True, done=True)
            for g in range(4):
                b = (b0, b1)[g // 2]
                o = A.act(PC[:, T * g:T * g + T], b.t[:, T * (g % 2):T * (g % 2) + T], AF.Copy, t, scale=Q("pscale")[:, g:g + 1])
                b.free = (o,)
            out.append(o)
            yield

        def retention(rqk, rv, rg, out):
            start = everything()
            E.wait(*rqk)
            w0 = G.tt(v3(R0), v3(RQK), wide(C("cos"), 1, 8), OP.mult, *rqk, *start)
            for j in range(4):
                b = banks[j]
                E.wait(*b.free)
                t = mm(b.t[:, :], C("rot"), RQK[:, 512 * j:512 * j + 512], True, True, done=True)
                w = V.tt(R1[:, 512 * j:512 * j + 512].rearrange("p (m t) -> p m t", t=T), b.t[:, :].rearrange("p (m t) -> p m t", t=T),
                         wide(C("sin"), 1, 2), OP.mult, t, *start)
                b.free = (w,)
            rot = V.tt(RQK[:, :], R0[:, :], R1[:, :], OP.add, w, w0, t)
            yield
            kb3 = lambda t, b: t[:, 128 * b:128 * b + 128]
            E.wait(rot)
            for j in range(2):
                E.wait(*banks[j].free)
                for b in range(4 * j, 4 * j + 4):
                    fn = lambda e, o=banks[j].t[:, 128 * (b % 4):128 * (b % 4) + 128], i=kb3(RK, b): e.transpose(o, i, C("eye", CONST1))
                    tk = E.do(fn) if b % 4 == 3 else E.quiet(fn)
            for j in range(2):
                for hh_ in range(2):
                    h = 2 * j + hh_
                    kz = A.act(KZ[:, 256 * h:256 * h + 256], banks[j].t[:, 256 * hh_:256 * hh_ + 256], AF.Copy, tk, *start, scale=C("zeta")[:, h:h + 1])
                banks[j].free = (kz,)
            for j in range(2):
                E.wait(*banks[2 + j].free)
                for b in range(4 * j, 4 * j + 4):
                    t = mm(banks[2 + j].t[:, 128 * (b % 4):128 * (b % 4) + 128], kb3(RK, b), kb3(RQ, b), True, True, done=b % 4 == 3)
            for j in range(2):
                for h2 in range(2):
                    h = 2 * j + h2
                    st = V.tt(ST[:, 256 * h:256 * h + 256].rearrange("p (s t) -> p s t", s=2),
                              banks[2 + j].t[:, 256 * h2:256 * h2 + 256].rearrange("p (s t) -> p s t", s=2),
                              wide(C("rmask")[:, 128 * h:128 * h + 128], 1, 2), OP.mult, t, *start)
                banks[2 + j].free = (st,)
            qx = G.tt(RQ[:, :], RQ[:, :], C("xi"), OP.mult, t)
            yield
            rr = lambda n, h: RR[:, 512 * (n - 1) + 128 * h:512 * (n - 1) + 128 * h + 128]
            E.wait(kz, *rv)
            rd = None
            for n in range(3):
                half, q = n // 2, n % 2
                r = slice(64 * q, 64 * q + 64)
                b = banks[n % 2]
                E.wait(*b.free)
                for h in range(4):
                    t = mm(b.t[:, 128 * h:128 * h + 128], KZ[r, 256 * h + 128 * half:256 * h + 128 * half + 128],
                           RV[r, 512 * half + 128 * h:512 * half + 128 * h + 128], True, True, done=h == 3)
                for h in range(4):
                    src = b.t[:, 128 * h:128 * h + 128]
                    if n == 0:
                        rd = V.copy(rr(1, h), src, t, *start)
                    else:
                        rd = V.stt(rr(n + 1, h), rr(n, h), CHUNK_DECAY[h], src, OP.mult, OP.add, t, rd)
                b.free = (rd,)
                yield
            E.wait(st, qx, rd)
            for j in range(2):
                E.wait(*banks[2 + j].free)
                for b in range(4 * j, 4 * j + 4):
                    h, half = b // 2, b % 2
                    o = banks[2 + j].t[:, 128 * (b % 4):128 * (b % 4) + 128]
                    mm(o, RV[:, 512 * half + 128 * h:512 * half + 128 * h + 128], kb3(ST, b), True, False, skip=True)
                    for q in range(2):
                        n = 2 * half + q
                        if n:
                            t = mm(banks[2 + j].t[:, 128 * (b % 4) + 64 * q:128 * (b % 4) + 64 * q + 64], rr(n, h),
                                   RQ[:, 256 * h + 64 * n:256 * h + 64 * n + 64], False, q == 1, skip=True, done=b % 4 == 3 and q == 1)
            for j in range(2):
                o = A.copy(OR[:, 512 * j:512 * j + 512], banks[2 + j].t[:, :], t, *start)
                banks[2 + j].free = (o,)
            yield
            E.wait(o)
            for j in range(2):
                E.wait(*banks[j].free)
                t = mm(banks[j].t[:, :], C("ones"), OR[:, 512 * j:512 * j + 512], True, True, done=True)
                w = V.stt(OR[:, 512 * j:512 * j + 512], banks[j].t[:, :], -1.0 / 128, OR[:, 512 * j:512 * j + 512], OP.mult, OP.add, t)
                banks[j].free = (w,)
            s = A.act(O2[:, :], OR[:, :], AF.Square, w)
            E.wait(s)
            for j in range(2):
                E.wait(*banks[j].free)
                t = mm(banks[j].t[:, :], C("ones"), O2[:, 512 * j:512 * j + 512], True, True, done=True)
                a = A.act(SR[:, 512 * j:512 * j + 512], banks[j].t[:, :], AF.Ln, t, *start, scale=1.0 / 128, bias=C("eps5"))
                banks[j].free = (a,)
            a = A.act(SR[:, :], SR[:, :], AF.Exp, a, scale=-0.5)
            z_ = A.act(RG[:, :], RG[:, :], AF.Silu, *rg)
            for h in range(4):
                c = slice(T * h, T * h + T)
                w = V.stt(OR[:, c], OR[:, c], Q("retout")[:, h:h + 1], SR[:, c], OP.mult, OP.mult, a)
            w = V.tt(OR[:, :], OR[:, :], RG[:, :], OP.mult, w, z_)
            out.append(w)

        def first_layer(l, xready):
            start = everything()
            cl = load(cst[:, 0:N_CONST1], ins["const1"], *start) if l == 0 else None
            pl = load(par[:, 0:N_PAR1], ins["par1"][l], *start)
            sl = load(small[:, :], ins["small"][l], *start)
            if cl:
                pl = sl
            for e in (A, V, G, E):
                e.wait(sl)
            h = split_norm(Q("mixpre"), MSQ, MR[:, 0:T], xready, start)
            cw = Q("conv").rearrange("p (m i) -> p m i", i=4)
            U3, A3 = v3(U), v3(QKV)
            conv = []

            def conv_evac(m0, n, b, tok):
                for m in range(m0, m0 + n):
                    a = A.act(A3[:, m, :], b.t[:, (m - m0) * T:(m - m0 + 1) * T], AF.Copy, tok, *h, scale=cw[:, m, 3:4])
                t = A.copy(U[:, m0 * T:(m0 + n) * T], b.t[:, 0:n * T], tok)
                b.free = (t,)
                for m in range(m0, m0 + n):
                    w = t
                    for j in range(1, 4):
                        w = V.stt(A3[:, m, j:T], U3[:, m, 0:T - j], cw[:, m, 3 - j:4 - j], A3[:, m, j:T], OP.mult, OP.add, w, a)
                conv.append(w)

            run(project(("qkv", l), 12, (hh, hl), 8, h, conv_evac))
            sq = A.act(QKV[:, :], QKV[:, :], AF.Silu, *conv)
            b = next_bank()
            E.wait(*b.free)
            for s in range(2):
                for k in range(8):
                    for n, x in enumerate((hh, hl)):
                        t = mm(b.t[:, 8 * s:8 * s + 8], x[:, k, 128 * s:128 * s + 128].bitcast(F32), small[:, 8 * k:8 * k + 8],
                               k == 0 and n == 0, k == 7 and n == 1, done=(s, k, n) == (1, 7, 1))
            ab = A.copy(SM[:, 192:208], b.t[:, 0:16], t)
            b.free = (ab,)
            z, rqk, rv, rg, pu, g0, g1, g2, od, oo, op_, yd = ([] for _ in range(12))

            def rv_evac(s, b, tok):
                t = A.copy(RV[:, 512 * s:512 * s + 512], b.t[:, :], tok)
                b.free = (t,)
                rv.append(t)

            fill = chain(project(("z", l), 4, (hh, hl), 8, h, copy_to(Z, z)),
                         project(("rqk", l), 8, (hh, hl), 8, h, copy_to(RQK, rqk)),
                         by_token(("rv", l), h, rv_evac),
                         project(("rg", l), 4, (hh, hl), 8, h, copy_to(RG, rg)),
                         project(("pu", l), 4, (hh, hl), 8, h, copy_to(PU, pu)),
                         project(("gate0", l), 8, (hh, hl), 8, h, copy_to(GT, g0)))
            next(fill)
            next(fill)
            run(delta_rule((sq,), z, (ab, sl), od), fill)
            run(fill)
            run(branch(("wdn", l), OD[:, :], od, 4, GT, g0, True, yd, everything()))
            gready = (V.done(),)

            def gate_evac(toks, ready):
                def evac(m0, n, b, tok):
                    t = A.copy(GT[:, m0 * T:(m0 + n) * T], b.t[:, 0:n * T], tok, *ready)
                    b.free = (t,)
                    toks.append(t)
                return evac

            fill = project(("gate1", l), 8, (hh, hl), 8, h, gate_evac(g1, gready))
            run(pooling(pu, sl, op_), fill)
            run(fill)
            run(branch(("wpool", l), PC[:, :], op_, 4, GT, g1, False, yd, everything()))
            gready = (V.done(),)
            fill = project(("gate2", l), 8, (hh, hl), 8, h, gate_evac(g2, gready))
            run(retention(rqk, rv, rg, oo), fill)
            run(fill)
            run(branch(("wret", l), OR[:, :], oo, 4, GT, g2, False, yd, everything()))
            yh = split(hh[:, :, :].rearrange("p k t -> p (k t)"), hl[:, :, :].rearrange("p k t -> p (k t)"), YY[:, :], (yd[-1], E.done()))
            mo = []
            run(project(("wout", l), 8, (hh, hl), 8, yh, copy_to(MO, mo)))
            x1 = post_norm(MO, Q("mixpost"), MSQ, MR[:, 0:T], mo)
            h2 = split_norm(Q("ffnpre"), MSQ, MR[:, 0:T], (x1,), everything())
            ready = []

            def ffn_evac(m0, n, b, tok):
                i = m0 // 2
                f = FT[:, 256 * (i % 4):256 * (i % 4) + 256]
                free = ready[i - 4] if i >= 4 else h2
                a = A.act(f, b.t[:, 0:T], AF.Silu, tok, *free)
                w = V.tt(f, b.t[:, T:2 * T], f, OP.mult, a, tok)
                b.free = (w,)
                hi = A.copy(FH[:, i, :], f, w)
                lo = V.tt(FL[:, i, :], f, FH[:, i, :].bitcast(F32), OP.subtract, hi)
                ready.append((hi, lo))

            run(project(("gu", l), 44, (hh, hl), 8, h2, ffn_evac))
            dm = []
            down(("down", l), 22, FH, FL, ready, copy_to(NM, dm))
            return post_norm(NM, Q("ffnpost"), NSQ, NR[:, 0:T], dm)


        QF = slot("QF", 0, 7)
        CS = slot("CS", 7)
        VT = slot("VT", 8, 3)
        LG = slot("LG", 11, 2)
        PT = slot("PT", 13, 2)
        OO = slot("OO", 15, 3)
        REL = slot("REL", 18, 2)
        SC = slot("SC", 20)
        SS = slot("SS", 21)
        RT = slot("RT", 22)
        QF3, OO3 = v3(QF), v3(OO)
        COS, SIN = CS[:, 0:256], CS[:, 256:512]
        AM = CS[:, 512:896]
        ROPE = slot("ROPE", 18)
        POS = slot("POS", 19, dt=I32)
        IW = SS[:, 0:16]

        def rope_tables():
            ld = load(POS[:, 0:T], ins["positions"])
            a, n = ROPE[:, 0:256], ROPE[:, 256:512]
            w = V.copy(a, POS[:, 0:T], ld)
            w = V.ts(a, a, C("inv"), None, OP.mult, None, w)
            big, two_pi = 12582912.0, 2.0 * np.pi
            c1 = 6.28125
            c2, c3 = SPLIT_PI
            for dst, turn in ((SIN, 0.0), (COS, 0.25)):
                u = V.ts(n, a, 1.0 / two_pi, turn, OP.mult, OP.add, w)
                u = V.ts(n, n, big, None, OP.add, None, u)
                u = V.ts(n, n, big, None, OP.subtract, None, u)
                u = V.stt(dst, n, -c1, a, OP.mult, OP.add, u)
                u = V.stt(dst, n, -c2, dst, OP.mult, OP.add, u)
                u = V.stt(dst, n, -c3, dst, OP.mult, OP.add, u)
                if turn:
                    u = V.ts(dst, dst, float(np.float32(np.pi / 2)), None, OP.add, None, u)
                u = V.ts(dst, dst, 3.1415925, -3.1415925, OP.min, OP.max, u)
                w = A.act(dst, dst, AF.Sin, u)
            return w

        def second_layer(l, xready):
            start = everything()
            pl = load(par[:, 0:N_PAR2], ins["par2"][l], *start)
            if l == 0:
                pl = load(cst[:, 0:N_CONST2], ins["const2"], *start)
            for e in (A, V, G, E):
                e.wait(pl)
            cs = rope_tables()
            start = everything()
            h = split_norm(Q("attn"), MSQ, MR[:, 0:T], xready, start)
            ring[0], ring[1] = 0, [6, 7]
            roped = {}

            def rope(m0, n, ready):
                b = next_bank()
                E.wait(*ready, *b.free)
                w_ = n * T
                f = QF[:, m0 * T:m0 * T + w_]
                t = mm(b.t[:, 0:w_], C("rot2"), f, True, True, done=True)
                tmp = RT[:, 0:w_] if m0 // 2 % 2 else RT[:, 512:512 + w_]
                w = V.tt(tmp.rearrange("p (m t) -> p m t", t=T), b.t[:, 0:w_].rearrange("p (m t) -> p m t", t=T), wide(SIN, 1, n), OP.mult, t, cs)
                b.free = (w,)
                g = G.tt(f.rearrange("p (m t) -> p m t", t=T), f.rearrange("p (m t) -> p m t", t=T), wide(COS, 1, n), OP.mult, t, cs, *ready)
                w = V.tt(f, f, tmp, OP.add, w, g)
                for m in range(m0, m0 + n):
                    roped[m] = w

            pend = []

            def flush():
                while pend:
                    rope(*pend.pop(0))

            def evac_from(base):
                def evac(m0, n, b, tok):
                    m0 += base
                    t = A.copy(QF[:, m0 * T:(m0 + n) * T], b.t[:, 0:n * T], tok, *h)
                    b.free = (t,)
                    flush()
                    if m0 == 8:
                        f = QF[:, 8 * T:9 * T]
                        s = A.act(REL[:, 0:T], f, AF.Square, t)
                        bb = next_bank()
                        E.wait(s, *bb.free)
                        t2 = mm(bb.t[:, 0:T], C("half"), REL[:, 0:T], True, True, done=True)
                        r = rstd_of(bb, T, 1.0 / 64, C("eps6"), REL[:, 256:512], t2)
                        t = V.stt(f, f, Q("idxk"), REL[:, 256:512], OP.mult, OP.mult, r)
                    pend.append((m0, n, (t,)))
                return evac

            vt = []
            cvd = lambda half, kv: VT[:, 1152 * half + 768 + 128 * kv:1152 * half + 896 + 128 * kv]
            avd = lambda half: VT[:, 1152 * half + 1024:1152 * half + 1152]
            bvd = lambda half, t: VT[:, 1152 * half + 128 * t:1152 * half + 128 * t + 128]

            def v_evac(group):
                def evac(s, b, tok):
                    if group == 0:
                        t = A.copy(VT[:, 1152 * s:1152 * s + 512], b.t[:, :], tok)
                    else:
                        A.copy(VT[:, 1152 * s + 512:1152 * s + 768], b.t[:, 0:256], tok)
                        for c in range(2):
                            A.copy(VT[:, 1152 * s + 768:1152 * s + 1024].rearrange("p (k c d) -> p k c d", k=2, c=2)[:, :, c, :],
                                   b.t[:, 256:384].rearrange("p (k d) -> p k d", k=2), tok)
                            A.copy(VT[:, 1152 * s + 1024 + 64 * c:1152 * s + 1088 + 64 * c], b.t[:, 384:448], tok)
                        t = A.act(IW[:, 8 * s:8 * s + 8], b.t[:, 448:456], AF.Copy, tok, scale=8.0 ** -0.5)
                    b.free = (t,)
                    vt.append(t)
                return evac

            run(project(("q2a", l), 11, (hh, hl), 8, h, evac_from(0)))
            run(by_token(("v2a", l), h, v_evac(0)))
            flush()
            run(by_token(("v2b", l), h, v_evac(1)))

            def index(half):
                nk = 128 * (half + 1)
                per = 512 // nk
                qs = slice(128 * half, 128 * half + 128)
                E.wait(roped[7], roped[8])
                rel = REL[:, 0:8 * nk].rearrange("p (c n t) -> p c n t", c=2, t=nk)
                toks = {}
                for par_ in range(2):
                    r = slice(64 * par_, 64 * par_ + 64)
                    for j in range(4):
                        b = banks[2 * par_ + j // per]
                        if j % per == 0:
                            E.wait(*b.free)
                        t = mm(b.t[:, nk * (j % per):nk * (j % per) + nk], QF3[r, 4 + j, qs], QF3[r, 8, 0:nk], True, True,
                               done=j % per == per - 1 or j == 3)
                        toks[par_, j // per] = t
                for par_ in range(2):
                    for k in range((4 + per - 1) // per):
                        b = banks[2 * par_ + k]
                        n = min(per, 4 - k * per)
                        w = A.act(rel[:, par_, k * per:k * per + n, :], b.t[:, 0:n * nk].rearrange("p (n t) -> p n t", t=nk), AF.Relu,
                                  toks[par_, k], *relfree, scale=0.125)
                        b.free = (w,)
                relfree.clear()
                sc = [SC[:, 0:nk], SC[:, 256:256 + nk]]
                causal = C(f"mA{half}", CONST2)
                first = True
                for par_ in range(2):
                    for j in range(4):
                        w = V.stt(sc[0], rel[:, par_, j, :], IW[:, 8 * half + 2 * j + par_:8 * half + 2 * j + par_ + 1],
                                  causal if first else sc[0], OP.mult, OP.add, w, vt[-1], vt[-2])
                        first = False
                relfree.append(w)
                yield
                m8 = SS[:, 16:24]
                for r in range(8):
                    w = V.do(lambda e, i=sc[0]: e.max(m8, i), w)
                    w = V.do(lambda e, i=sc[0], o=sc[1]: e.match_replace(o, m8, i, TAKEN), w)
                    sc = sc[::-1]
                    if r % 2:
                        yield
                am = AM[:, 128 * half:128 * half + nk]
                w = V.ts(am, sc[0], -2.0e38, NEG, OP.is_gt, OP.mult, w)
                w = V.tt(am, am, causal, OP.add, w)
                amask[half] = w
                yield

            relfree = []
            amask = {}
            lfree = []

            def attend(half, n, qtile, ktile, mask, mready, joint, sink, values, vready, dst, tiles, otoks):
                nk = 128 * (half + 1)
                per = 512 // nk
                nb = (n + per - 1) // per
                qs = slice(128 * half, 128 * half + 128)
                E.wait(*(roped[qtile(i)] for i in range(n)), *(roped[ktile(i)] for i in range(n)))
                L = LG[:, 0:2 * n * nk].rearrange("p (c n t) -> p c n t", c=2, t=nk)
                toks = {}
                for c in range(2):
                    r = slice(64 * c, 64 * c + 64)
                    for i in range(n):
                        b = banks[2 * c + i // per]
                        if i % per == 0:
                            E.wait(*b.free)
                        toks[c, i // per] = mm(b.t[:, nk * (i % per):nk * (i % per) + nk], QF3[r, qtile(i), qs], QF3[r, ktile(i), 0:nk],
                                               True, True, done=i % per == per - 1 or i == n - 1)
                for c in range(2):
                    for k in range(nb):
                        b = banks[2 * c + k]
                        m = min(per, n - k * per)
                        w = V.tt(L[:, c, k * per:k * per + m, :], b.t[:, 0:m * nk].rearrange("p (n t) -> p n t", t=nk),
                                 mask(k * per, m), OP.add, toks[c, k], *mready, *lfree)
                        b.free = (w,)
                lfree.clear()
                st = SS[:, 32:40], SS[:, 48:56], SS[:, 64:72]
                ng = 2 if joint else 2 * n
                Lg = LG[:, 0:2 * n * nk].rearrange("p (g t) -> p g t", g=ng)
                mx, den, ex = (x[:, 0:ng] for x in st)
                w = V.red(mx, Lg, OP.max, w)
                if sink is None:
                    w = V.ts(mx, mx, -0.125, None, OP.mult, None, w)
                else:
                    w = V.stt(mx, mx, 0.125, sink, OP.mult, OP.max, w)
                    w = V.tt(ex, sink, mx, OP.subtract, w)
                    se = A.act(ex, ex, AF.Exp, w)
                    w = V.ts(mx, mx, -1.0, None, OP.mult, None, w)
                for g in range(ng):
                    a = A.act(Lg[:, g, :], Lg[:, g, :], AF.Exp, w, scale=0.125, bias=mx[:, g:g + 1], accum=den[:, g:g + 1])
                if sink is not None:
                    a = V.tt(den, den, ex, OP.add, a, se)
                w = V.recip(den, den, a)
                w = V.tt(Lg, Lg, wide(den, 2, Lg.shape[2]), OP.mult, w, a)
                yield
                E.wait(w)
                for kb in range(half + 1):
                    for k in range((2 * n + 3) // 4):
                        b = banks[4 + k]
                        E.wait(*b.free)
                        m = min(4, 2 * n - 4 * k)
                        for j in range(4 * k, 4 * k + m):
                            fn = lambda e, o=b.t[:, 128 * (j % 4):128 * (j % 4) + 128], i=L[:, j % 2, j // 2, 128 * kb:128 * kb + 128]: e.transpose(o, i, C("eye", CONST2))
                            t = E.do(fn) if j == 4 * k + m - 1 else E.quiet(fn)
                        p = A.copy(PT[:, 768 * kb + 512 * k:768 * kb + 512 * k + 128 * m], b.t[:, 0:128 * m], t)
                        b.free = (p,)
                lfree.append(t)
                yield
                E.wait(p, *vready)
                nout = 1 if joint else n
                for o in range(nout):
                    b = banks[o // 2]
                    if o % 2 == 0:
                        E.wait(*b.free)
                    terms = [(i, kb) for i in (range(n) if joint else [o]) for kb in range(half + 1)]
                    for q, (i, kb) in enumerate(terms):
                        t = mm(b.t[:, 256 * (o % 2):256 * (o % 2) + 256], values(kb, i), PT[:, 768 * kb + 256 * i:768 * kb + 256 * i + 256],
                               q == 0, q == len(terms) - 1, done=q == len(terms) - 1)
                for k in range((nout + 1) // 2):
                    b = banks[k]
                    m = min(2, nout - 2 * k)
                    src = b.t[:, 0:256 * m].rearrange("p (o c t) -> p o c t", c=2, t=128)
                    for c in range(2):
                        r = slice(64 * c, 64 * c + 64)
                        w = V.copy(OO3[r, dst + 2 * k:dst + 2 * k + m, qs], src[r, :, c, :], t)
                    b.free = (w,)
                otoks.append(w)
                yield

            oa, ob, oc, g0, g1, g2, yd = ([] for _ in range(7))
            mA = lambda half: lambda i, m: wide(AM[:, 128 * half:128 * half + 128 * (half + 1)], 1, m)
            mB = lambda half: lambda i, m: C(f"mB{half}", CONST2).rearrange("p (g t) -> p g t", g=3)[:, i:i + m, :]
            mC = lambda half: lambda i, m: wide(C(f"mC{half}", CONST2), 1, m)

            def mix_a():
                yield from index(0)
                yield from index(1)
                for half in range(2):
                    yield from attend(half, 3, lambda i: i, lambda i: 3, mA(half), (amask[half],), False, None,
                                      lambda kb, i: avd(kb), vt, 0, 3, oa)

            def mix_c():
                for half in range(2):
                    for r in range(2):
                        yield from attend(half, 2, lambda i, r=r: 11 + 2 * r + i, lambda i, r=r: 9 + r, mC(half), (), False,
                                          Q("sinks", PAR2)[:, 4 * r:4 * r + 4], lambda kb, i, r=r: cvd(kb, r), vt, 5 + 2 * r, 2, oc)

            def mix_b():
                for half in range(2):
                    for jp in range(2):
                        yield from attend(half, 3, lambda i, jp=jp: 15 + 2 * i + jp, lambda i, jp=jp: 21 + 2 * i + jp, mB(half), (), True,
                                          None, lambda kb, i, jp=jp: bvd(kb, 2 * i + jp), vt, 3 + jp, 1, ob)

            def flushing():
                flush()
                yield

            fill = chain(project(("q2b", l), 16, (hh, hl), 8, h, evac_from(11)), flushing(),
                         project(("gate0", 2 + l), 8, (hh, hl), 8, h, copy_to(GT, g0)))
            run(mix_a(), fill)
            run(fill)
            run(branch(("wa", l), OO[:, 0:768], oa, 3, GT, g0, True, yd, everything()))

            def gate_evac(toks, ready):
                def evac(m0, n, b, tok):
                    t = A.copy(GT[:, m0 * T:(m0 + n) * T], b.t[:, 0:n * T], tok, *ready)
                    b.free = (t,)
                    toks.append(t)
                return evac

            fill = project(("gate1", 2 + l), 8, (hh, hl), 8, h, gate_evac(g1, (V.done(),)))
            run(mix_b(), fill)
            run(fill)
            run(branch(("wb", l), OO[:, 768:1280], ob, 2, GT, g1, False, yd, everything()))
            fill = project(("gate2", 2 + l), 8, (hh, hl), 8, h, gate_evac(g2, (V.done(),)))
            run(mix_c(), fill)
            run(fill)
            run(branch(("wc", l), OO[:, 1280:2304], oc, 4, GT, g2, False, yd, everything()))
            ring[0], ring[1] = 0, [4, 5, 6, 7]
            yh = split(hh[:, :, :].rearrange("p k t -> p (k t)"), hl[:, :, :].rearrange("p k t -> p (k t)"), YY[:, :], (yd[-1], E.done()))
            xs = []

            def add_evac(m0, n, b, tok):
                t = V.tt(xT[:, m0:m0 + n, :].rearrange("p m t -> p (m t)"), xT[:, m0:m0 + n, :].rearrange("p m t -> p (m t)"), b.t[:, 0:n * T], OP.add, tok)
                b.free = (t,)
                xs.append(t)

            run(project(("wo", l), 8, (hh, hl), 8, yh, add_evac))
            h2 = split_norm(Q("mlp"), MSQ, MR[:, 0:T], xs, everything())
            ready = []

            def mlp_evac(m0, n, b, tok):
                for i in range(m0, m0 + n):
                    f = FT[:, 256 * (i % 4):256 * (i % 4) + 256]
                    free = ready[i - 4] if i >= 4 else h2
                    src = b.t[:, (i - m0) * T:(i - m0 + 1) * T]
                    a = A.act(f, src, AF.Relu, tok, *free)
                    hi = A.act(FS[:, 256 * (i % 4):256 * (i % 4) + 256], f, AF.Square, a, *free)
                    f2 = FS[:, 256 * (i % 4):256 * (i % 4) + 256]
                    h_ = A.copy(FH[:, i, :], f2, hi)
                    lo = V.tt(FL[:, i, :], f2, FH[:, i, :].bitcast(F32), OP.subtract, h_)
                    ready.append((h_, lo))
                b.free = (a,)

            run(project(("up", l), 32, (hh, hl), 8, h2, mlp_evac))
            down(("down2", l), 32, FH, FL, ready, add_evac)
            return xs[-1]

        FS = slot("FS", 17)

        def second_block(x):
            consts[0], pars[0] = CONST2, PAR2
            for l in range(DEPTH):
                x = second_layer(l, (x,))
            r = norm_stats(xT[:, :, :], (x,), MSQ, MR[:, 0:T])
            for k in range(8):
                x = V.stt(xT[:, k, :], xT[:, k, :], Q("final")[:, k:k + 1], MR[:, 0:T], OP.mult, OP.mult, r)
            return x

        x0 = load(xT[:, :, :], ins["x"])
        for _ in range(RAW):
            fetch()
        x = x0
        for l in range(DEPTH):
            x = first_layer(l, (x,))
        x = second_block(x)
        last = everything()
        S.wait(*last)
        for i in range(fetched[0]):
            if i >= fetched[0] - RAW:
                S.wait((s_raw[i % RAW], 16 * (i // RAW + 1)))
        S.queue.append(lambda e: e.dma_start(out, xT[:, :, :]).then_inc(s_out, 16))
        S.wait((s_out, 16))
        assert len(order) == NCHUNK, len(order)
        block = ctx.enter_context(nc.Block())
        block.sync(S.play)
        block.scalar(A.play)
        block.vector(V.play)
        block.gpsimd(G.play)
        block.tensor(E.play)
    return order


LOG_GAMMA = [np.log1p(-np.exp2(np.float32(-5.0 - h))) for h in range(4)]
CHUNK_DECAY = [float(np.exp(np.float32(64.0 * g))) for g in LOG_GAMMA]


def constants1():
    c = np.zeros((P, N_CONST1), np.float32)

    def put(name, a):
        o, w = CONST1[name]
        c[:, o:o + w] = a

    p = np.arange(P)[:, None]
    f = np.arange(P)[None, :]
    same = p // 64 == f // 64
    put("ones", 1.0)
    put("eye", p == f)
    put("eps6", 1e-6)
    put("eps5", 1e-5)
    put("one", 1.0)
    put("upper", same & (p <= f))
    put("chunk", same)
    lev = [(p // (2 << s) == f // (2 << s)) & (p // (1 << s) % 2 == 1) & (f // (1 << s) % 2 == 0) for s in range(6)]
    put("lev", np.concatenate(lev, 1))
    put("levT", np.concatenate([a.T for a in lev], 1))
    rot = np.zeros((P, P))
    for i in range(64):
        rot[i + 64, i] = -1.0
        rot[i, i + 64] = 1.0
    put("rot", rot)
    inv = np.float32(10000.0) ** (-np.arange(64, dtype=np.float32) / 64)
    ang = inv.astype(np.float32)[:, None] * np.arange(T, dtype=np.float32)[None, :]
    put("cos", np.tile(np.cos(ang.astype(np.float64)), (2, 1)))
    put("sin", np.tile(np.sin(ang.astype(np.float64)), (2, 1)))
    lg = [float(g) for g in LOG_GAMMA]
    put("rmask", np.concatenate([np.where(same, np.exp(np.abs(p - f) * g), 0) * 128 ** -0.5 for g in lg], 1))
    t = np.arange(T)[None, :]
    put("xi", np.concatenate([np.exp((t % 64 + 1) * g) for g in lg], 1))
    put("zeta", np.concatenate([np.exp((63 - p % 64) * g) * 128 ** -0.5 for g in lg], 1))
    put("cnt", np.concatenate([1.0 / np.minimum(t + 1, w) for w in (2, 4, 8, 16)], 1))
    return c


def _split_pi():
    rest = 2.0 * np.pi - 6.28125
    c2 = round(rest * 2.0 ** 21) / 2.0 ** 21
    return c2, float(np.float32(rest - c2))


SPLIT_PI = _split_pi()


def constants2():
    c = np.zeros((P, N_CONST2), np.float32)

    def put(name, a):
        o, w = CONST2[name]
        c[:, o:o + w] = a

    p = np.arange(P)[:, None]
    f = np.arange(P)[None, :]
    put("ones", 1.0)
    put("eye", p == f)
    put("eps6", 1e-6)
    put("eps5", 1e-5)
    put("one", 1.0)
    put("half", p // 64 == f // 64)
    rot = np.zeros((P, P))
    for b in range(0, P, 64):
        for i in range(32):
            rot[b + i + 32, b + i] = -1.0
            rot[b + i, b + i + 32] = 1.0
    put("rot2", rot)
    inv = np.float32(10000.0) ** (-np.arange(32, dtype=np.float32) / 32)
    put("inv", np.tile(inv, 4)[:, None])
    for half in range(2):
        t = p + 128 * half
        s = np.arange(128 * (half + 1))[None, :]
        neg = lambda ok: np.where(ok, 0.0, NEG)
        put(f"mA{half}", neg(s <= t))
        put(f"mC{half}", neg((s <= t) & (s > t - 128)))
        put(f"mB{half}", np.concatenate([neg((s <= t) & (t - s <= w) & ((t - s) % d == 0)) for w, d in ((128, 1), (512, 4), (2048, 16))], 1))
    return c


S1 = dict(qkv=(0, 1536), z=(1536, 512), ab=(2048, 8), rqk=(2056, 1024), rv=(3080, 512), rg=(3592, 512), pu=(4104, 512), gate=(4616, 3072))
S2 = {}
_at = 0
for _n, _w in (("aq", 384), ("ak", 64), ("av", 64), ("iq", 512), ("ik", 64), ("iw", 8), ("bq", 768), ("bk", 768), ("bv", 768),
               ("cq", 512), ("ck", 128), ("cv", 128), ("gate", 3072)):
    S2[_n] = (_at, _w)
    _at += _w


def pack(order, inputs):
    w = {k: np.asarray(inputs[k]) for k in ("w_in", "w_branch_dn", "w_branch_ret", "w_branch_pool", "w_out", "ffn_gate", "ffn_up", "ffn_down",
                                            "w_in_2", "w_a_2", "w_b_2", "w_c_2", "w_o_2", "w_up_2", "w_down_2")}
    made = {}

    def cols(a, at, n):
        return a[:, at:at + n]

    def tiles(a):
        k, m = a.shape[0] // P, a.shape[1] // P
        t = a.reshape(k, P, m, P).transpose(2, 0, 1, 3).reshape(-1, 8, P, P)
        return t.transpose(0, 2, 1, 3).reshape(-1, P, 1024)

    def rows(a):
        return a.reshape(-1, P, 1024)

    def moving(a):
        return a.reshape(4, 2, P, 512).transpose(0, 2, 1, 3).reshape(4, P, 1024)

    def make(name, l):
        if name in ("qkv", "z", "rqk", "rg", "pu"):
            return tiles(cols(w["w_in"][l], *S1[name]))
        if name == "rv":
            return moving(cols(w["w_in"][l], *S1["rv"]))
        if name in ("gate0", "gate1", "gate2"):
            a, s = (w["w_in"][l], S1) if l < 2 else (w["w_in_2"][l - 2], S2)
            return tiles(cols(a, s["gate"][0] + 1024 * int(name[4]), 1024))
        if name == "gu":
            g, u = w["ffn_gate"][l], w["ffn_up"][l]
            return tiles(np.stack([g.reshape(D, 22, P), u.reshape(D, 22, P)], 2).reshape(D, 2 * FF1))
        direct = dict(wdn="w_branch_dn", wpool="w_branch_pool", wret="w_branch_ret", wout="w_out", wa="w_a_2", wb="w_b_2", wc="w_c_2",
                      wo="w_o_2", up="w_up_2")
        if name == "wb":
            return tiles(w["w_b_2"][l])
        if name in direct:
            return tiles(w[direct[name]][l])
        if name == "down":
            return rows(w["ffn_down"][l])
        if name == "down2":
            return rows(w["w_down_2"][l])
        a = w["w_in_2"][l]
        c = lambda n, lo=0, m=None: a[:, S2[n][0] + lo:S2[n][0] + (lo + m if m else S2[n][1])]
        if name == "q2a":
            return tiles(np.concatenate([c("aq"), c("ak"), c("ak"), c("iq"), c("ik"), c("ik"),
                                         c("ck", 0, 64), c("ck", 0, 64), c("ck", 64, 64), c("ck", 64, 64)], 1))
        if name == "q2b":
            return tiles(np.concatenate([c("cq"), c("bq"), c("bk")], 1))
        if name == "v2a":
            return moving(c("bv", 0, 512))
        if name == "v2b":
            return moving(np.concatenate([c("bv", 512, 256), c("cv"), c("av"), c("iw"), np.zeros((D, 56), np.float32)], 1))
        raise ValueError(name)

    out = np.zeros((NCHUNK, P, 1024), np.float32)
    for i, (name, l, n) in enumerate(order):
        if (name, l) not in made:
            made = {(name, l): make(name, l)}
        out[i] = made[name, l][n]
    return out


def feature_rows(a, n):
    return np.asarray(a).reshape(n, P).T


def parameters(inputs):
    x = {k: np.asarray(v) for k, v in inputs.items()}
    par1 = np.zeros((DEPTH, P, N_PAR1), np.float32)
    par2 = np.zeros((DEPTH, P, N_PAR2), np.float32)
    small = np.zeros((DEPTH, P, N_SMALL), np.float32)
    for l in range(DEPTH):
        def put(table, dst, name, a):
            o, n = table[name]
            dst[l][:, o:o + n] = a
        put(PAR1, par1, "mixpre", feature_rows(x["mix_pre_norm"][l], 8))
        put(PAR1, par1, "mixpost", feature_rows(x["mix_post_norm"][l], 8))
        put(PAR1, par1, "ffnpre", feature_rows(x["ffn_pre_norm"][l], 8))
        put(PAR1, par1, "ffnpost", feature_rows(x["ffn_post_norm"][l], 8))
        put(PAR1, par1, "conv", x["dn_conv"][l].reshape(4, 12, P).transpose(2, 1, 0).reshape(P, 48))
        put(PAR1, par1, "dnout", feature_rows(x["dn_out_norm"][l], 1))
        put(PAR1, par1, "retout", feature_rows(x["ret_out_norm"][l], 4))
        put(PAR1, par1, "pscale", feature_rows(x["pool_scale"][l], 4))
        put(PAR1, par1, "alog", np.repeat(x["dn_A_log"][l], 2)[None, :])
        put(PAR1, par1, "dtb", np.repeat(x["dn_dt_bias"][l], 2)[None, :])
        put(PAR2, par2, "attn", feature_rows(x["attn_norm_2"][l], 8))
        put(PAR2, par2, "mlp", feature_rows(x["mlp_norm_2"][l], 8))
        put(PAR2, par2, "final", feature_rows(x["final_norm_2"], 8))
        put(PAR2, par2, "idxk", np.concatenate([x["idx_k_norm_2"][l]] * 2)[:, None])
        put(PAR2, par2, "sinks", x["sinks_2"][l].reshape(2, 2, 2).transpose(0, 2, 1).reshape(1, 8))
        small[l][:, 0:64] = x["w_in"][l][:, 2048:2056].reshape(8, P, 8).transpose(1, 0, 2).reshape(P, 64)
        small[l][:, 64:576] = x["pool_w"][l].transpose(1, 0, 2).reshape(P, 512)
    return par1, par2, small


def declare(nc):
    d = lambda n, s, t=F32: nc.dram_tensor(f"in_{n}", s, t, kind="ExternalInput").ap()
    ins = {
        "weights": d("weights", (NCHUNK, P, 1024)), "x": d("x", (P, 8, T)), "positions": d("positions", (P, T), I32),
        "const1": d("const1", (P, N_CONST1)), "const2": d("const2", (P, N_CONST2)),
        "par1": d("par1", (DEPTH, P, N_PAR1)), "par2": d("par2", (DEPTH, P, N_PAR2)), "small": d("small", (DEPTH, P, N_SMALL)),
    }
    return ins, nc.dram_tensor("out", (P, 8, T), F32, kind="ExternalOutput").ap()


def lay_out(order, inputs):
    par1, par2, small = parameters(inputs)
    x = np.asarray(inputs["x"])[0]
    return {
        "in_weights": pack(order, inputs),
        "in_x": np.ascontiguousarray(x.T.reshape(8, P, T).transpose(1, 0, 2)),
        "in_positions": np.ascontiguousarray(np.broadcast_to(np.asarray(inputs["positions_2"])[0][None, :], (P, T))),
        "in_const1": constants1(), "in_const2": constants2(),
        "in_par1": par1, "in_par2": par2, "in_small": small,
    }


def kernel(**inputs):
    from concourse import bacc
    from concourse.bass_utils import run_bass_kernel_spmd

    nc = bacc.Bacc("TRN2", target_bir_lowering=False, num_devices=1)
    ins, out = declare(nc)
    order = program(nc, ins, out)
    r = run_bass_kernel_spmd(nc, [lay_out(order, inputs)], core_ids=[0])
    got = np.asarray(r.results[0]["out"])
    return np.ascontiguousarray(got.transpose(1, 0, 2).reshape(D, T).T)[None]
```

```python
from contextlib import ExitStack

import numpy as np
import concourse.bass as bass
from concourse import mybir

F32 = mybir.dt.float32
F32R = mybir.dt.float32r
I32 = mybir.dt.int32
OP = mybir.AluOpType
AF = mybir.ActivationFunctionType
AX = mybir.AxisListType.X

P = 128
T = 256
D = 1024
DEPTH = 2
FF1 = 2816
FF2 = 4096
NEG = -1.0e30
BLOCKED = -1
TAKEN = -3.0e38
RAW = 4
RING = 3
NCHUNK = 572
EXPLN = "natural_log_exp_and_others"

CONST1 = {}
CONST2 = {}


def _columns(table, widths):
    at = 0
    for name, w in widths:
        table[name] = (at, w)
        at += w
    return at


N_CONST1 = _columns(CONST1, [
    ("ones", 128), ("eye", 128), ("eps6", 1), ("eps5", 1), ("one", 1), ("pad", 1),
    ("upper", 128), ("chunk", 128), ("lev", 6 * 128), ("levT", 6 * 128), ("rot", 128),
    ("cos", 256), ("sin", 256), ("rmask", 4 * 128), ("xi", 4 * 64), ("zeta", 4), ("cnt", 4 * 256)])
N_CONST2 = _columns(CONST2, [
    ("ones", 128), ("eye", 128), ("eps6", 1), ("eps5", 1), ("one", 1), ("pad", 1),
    ("half", 128), ("rot2", 128), ("inv", 1), ("mB0", 3 * 128), ("mB1", 3 * 256),
    ("mA0", 128), ("mA1", 256), ("mC0", 128), ("mC1", 256)])
N_CONST = max(N_CONST1, N_CONST2)
HEAD = CONST1["pad"][0] + 1

PAR1 = {}
PAR2 = {}
N_PAR1 = _columns(PAR1, [("mixpre", 8), ("mixpost", 8), ("ffnpre", 8), ("ffnpost", 8), ("conv", 48),
                         ("dnout", 1), ("retout", 4), ("pscale", 4), ("alog", 8), ("dtb", 8)])
N_PAR2 = _columns(PAR2, [("attn", 8), ("mlp", 8), ("final", 8), ("idxk", 1), ("sinks", 8)])
N_PAR = DEPTH * (N_PAR1 + N_PAR2)
N_SMALL = 64 + 512


class Engine:

    def __init__(self, sem):
        self.sem, self.queue, self.count, self.seen = sem, [], 0, {}

    def wait(self, *tokens):
        for sem, value in tokens:
            if self.seen.get(id(sem), 0) < value:
                self.seen[id(sem)] = value
                self.queue.append(lambda e, s=sem, v=value: e.wait_ge(s, v))

    def do(self, fn, *after):
        self.wait(*after)
        self.count += 1
        self.queue.append(lambda e, s=self.sem: fn(e).then_inc(s, 1))
        return (self.sem, self.count)

    def quiet(self, fn, *after):
        self.wait(*after)
        self.queue.append(fn)

    def done(self):
        return (self.sem, self.count)

    def play(self, e):
        for fn in self.queue:
            fn(e)


class Vec(Engine):
    def tt(self, out, a, b, op, *after):
        return self.do(lambda e: e.tensor_tensor(out, a, b, op), *after)

    def ts(self, out, a, s1, s2, op0, op1, *after):
        if op1 is None:
            return self.do(lambda e: e.tensor_scalar(out, a, s1, None, op0), *after)
        return self.do(lambda e: e.tensor_scalar(out, a, s1, s2, op0, op1), *after)

    def stt(self, out, a, s, b, op0, op1, *after):
        return self.do(lambda e: e.scalar_tensor_tensor(out=out, in0=a, scalar=s, in1=b, op0=op0, op1=op1), *after)

    def copy(self, out, a, *after):
        return self.do(lambda e: e.tensor_copy(out, a), *after)

    def red(self, out, a, op, *after):
        return self.do(lambda e: e.tensor_reduce(out, a, AX, op), *after)

    def recip(self, out, a, *after):
        return self.do(lambda e: e.reciprocal(out, a), *after)


class Act(Engine):
    table = None

    def act(self, out, a, fn, *after, scale=1.0, bias=None, accum=None):
        if fn in (AF.Exp, AF.Ln):
            want = EXPLN
        elif fn in (AF.Silu, AF.Sigmoid, AF.Sin):
            want = str(fn)
        else:
            want = None
        if want and want != self.table:
            self.table = want
            if want == EXPLN:
                self.queue.append(lambda e: e.preload_act_table_set(EXPLN))
        kw = {"scale": scale}
        if bias is not None:
            kw["bias"] = bias
        if accum is not None:
            kw["accum_out"] = accum
        return self.do(lambda e: e.activation(out, a, fn, **kw), *after)

    def copy(self, out, a, *after):
        return self.do(lambda e: e.copy(out, a), *after)


class Bank:

    def __init__(self, t):
        self.t, self.free = t, ()


def wide(ap, axis, n):
    shape = list(ap.shape)
    shape.insert(axis, n)
    return ap.unsqueeze(axis).broadcast_to(shape)


def program(nc, ins, out):
    ctx = ExitStack()
    with ctx:
        sem = lambda name: ctx.enter_context(nc.semaphore(name))
        S, A, V, G, E = Engine(sem("sp")), Act(sem("act")), Vec(sem("dve")), Vec(sem("pool")), Engine(sem("pe"))
        s_raw = [sem(f"raw{i}") for i in range(RAW)]
        s_x, s_par, s_small, s_head, s_c1, s_c2, s_pos = (sem(n) for n in ("ldx", "ldpar", "ldsmall", "ldhead", "ldc1", "ldc2", "ldpos"))
        s_out = sem("out")

        at = [16640]

        def sb(name, shape, dt=F32, offset=None):
            n = 4
            for x in shape[1:]:
                n *= x
            if offset is None:
                offset = at[0]
                at[0] += (n + 31) // 32 * 32
            return nc.alloc_sbuf_tensor_at(name, shape, dt, offset=offset)

        xT = sb("xT", [P, 8, T])
        hh = sb("hh", [P, 8, T], F32R)
        hl = sb("hl", [P, 8, T], F32R)
        raw = sb("raw", [P, RAW, 1024])
        whi = sb("whi", [P, RING, 1024], F32R)
        wlo = sb("wlo", [P, RING, 1024], F32R)
        cst = sb("cst", [P, N_CONST])
        par = sb("par", [P, N_PAR])
        small = sb("small", [P, DEPTH * N_SMALL])
        region = at[0]
        nslots = (nc.sbuf_usable_end - region) // 4096
        assert nslots >= 30, nslots

        area = nc.alloc_sbuf_tensor_at("area", [P, 30 * 1024], F32, offset=region)

        def slot(name, i, n=1, dt=F32, shape=None):
            if dt == F32R:
                return sb(name, shape, dt, offset=region + 4096 * i)
            v = area[:, 1024 * i:1024 * (i + n)]
            return v.bitcast(dt) if dt != F32 else v

        banks = [Bank(ctx.enter_context(nc.psum_tensor(f"bank{i}", [P, 512], F32))) for i in range(8)]

        def C(name, table=None):
            o, w = (table or consts[0])[name]
            return cst[:, o:o + w]

        def Q(name, layer):
            first = layer < DEPTH
            o, w = (PAR1 if first else PAR2)[name]
            o += layer * N_PAR1 if first else DEPTH * N_PAR1 + (layer - DEPTH) * N_PAR2
            return par[:, o:o + w]

        consts = [CONST1]

        def load(dst, src, s, *after):
            S.wait(*after)
            S.queue.append(lambda e: e.dma_start(dst, src).then_inc(s, 16))
            return (s, 16)

        order = []
        hi_done, lo_done, used = {}, {}, {}
        staged = [0]
        fetched = [0]

        def fetch():
            i = fetched[0]
            if i >= NCHUNK:
                return
            fetched[0] += 1
            if i >= RAW:
                S.wait(hi_done[i - RAW], lo_done[i - RAW])
            r = i % RAW
            S.queue.append(lambda e: e.dma_start(raw[:, r, :], ins["weights"][i]).then_inc(s_raw[r], 16))

        def stage():
            i = staged[0]
            if i >= NCHUNK:
                return
            staged[0] += 1
            r, h = i % RAW, i % RING
            landed = (s_raw[r], 16 * (i // RAW + 1))
            free = [used[i - RING]] if i >= RING else []
            hi_done[i] = A.copy(whi[:, h, :], raw[:, r, :], landed, *free)
            lo_done[i] = V.tt(wlo[:, h, :], raw[:, r, :], whi[:, h, :].bitcast(F32), OP.subtract, hi_done[i], landed, *free)
            fetch()

        def chunk(what, ahead=RING):
            i = len(order)
            order.append(what)
            while staged[0] < min(i + ahead, NCHUNK):
                stage()
            E.wait(hi_done[i], lo_done[i])
            return i, whi[:, i % RING, :], wlo[:, i % RING, :]

        def mm(ps, l, r, first, last, *after, skip=False, done=False):
            fn = lambda e: e.matmul(ps, l, r, start=first, stop=last, skip_group_check=skip)
            return E.do(fn, *after) if done else E.quiet(fn, *after)

        def mm3(ps, w, x, first, last, wstat=True, skip=False, done=False):
            (wh, wl), (xh, xl) = w, x
            tok = None
            for n, (a, b) in enumerate(((wh, xh), (wh, xl), (wl, xh))):
                if not wstat:
                    a, b = b, a
                tok = mm(ps, a, b, first and n == 0, last and n == 2, skip=skip, done=done and n == 2)
            return tok

        ring = [0, [4, 5, 6, 7]]

        def next_bank():
            b = banks[ring[1][ring[0] % len(ring[1])]]
            ring[0] += 1
            return b

        def project(what, ntile, xs, nk, xtok, evac):
            at_, cur = 0, None
            for m0 in range(0, ntile, 2):
                b = next_bank()
                E.wait(*b.free)
                n = min(2, ntile - m0)
                for m in range(m0, m0 + n):
                    for k in range(nk):
                        E.wait(*xtok[k // 2])
                        if at_ % 8 == 0:
                            if at_:
                                yield
                            cur = chunk((*what, at_ // 8))
                        i, wh, wl = cur
                        c = at_ % 8 * 128
                        at_ += 1
                        tok = mm3(b.t[:, (m - m0) * T:(m - m0 + 1) * T], (wh[:, c:c + 128], wl[:, c:c + 128]),
                                  (xs[0][:, k, :], xs[1][:, k, :]), k == 0, k == nk - 1,
                                  done=(at_ % 8 == 0 or k == nk - 1))
                        if at_ % 8 == 0:
                            used[i] = tok
                evac(m0, n, b, tok)
            yield

        def by_token(what, xtok, evac):
            for x in xtok:
                E.wait(*x)
            bb = [next_bank(), next_bank()]
            for b in bb:
                E.wait(*b.free)
            for c in range(4):
                i, wh, wl = chunk((*what, c))
                for j in range(2):
                    k = 2 * c + j
                    w = (wh[:, 512 * j:512 * j + 512], wl[:, 512 * j:512 * j + 512])
                    for s in range(2):
                        x = (hh[:, k, 128 * s:128 * s + 128], hl[:, k, 128 * s:128 * s + 128])
                        tok = mm3(bb[s].t[:, :], w, x, k == 0, k == 7, wstat=False, done=(j == 1 and s == 1))
                used[i] = tok
                if c < 3:
                    yield
            for s in range(2):
                evac(s, bb[s], tok)
            yield

        def down(what, nk, ah, al, ready, evac):
            bb = banks[0:4]
            for b in bb:
                E.wait(*b.free)

            def term(k, m, w, done):
                wh, wl = w
                return mm3(bb[m // 2].t[:, (m % 2) * T:(m % 2 + 1) * T], (wh[:, 128 * m:128 * m + 128], wl[:, 128 * m:128 * m + 128]),
                           (ah[:, k, :], al[:, k, :]), k == 0 and m % 2 == 0, k == nk - 1, skip=True, done=done)

            for k in range(nk - RING):
                E.wait(*ready[k])
                i, wh, wl = chunk((*what, k))
                for m in range(8):
                    tok = term(k, m, (wh, wl), m == 7)
                used[i] = tok
            tail = []
            for k in range(nk - RING, nk):
                E.wait(*ready[k])
                tail.append((k, *chunk((*what, k), nk - k)))
            for j, b in enumerate(bb):
                for k, i, wh, wl in tail:
                    for m in (2 * j, 2 * j + 1):
                        tok = term(k, m, (wh, wl), m % 2 == 1)
                    used[i] = tok
                evac(2 * j, 2, b, tok)
            for _ in range(RING - 1):
                stage()

        def run(gen, fill=None):
            for n in gen:
                for _ in range(n or 1 if fill is not None else 0):
                    if next(fill, BLOCKED) == BLOCKED:
                        break

        def chain(*gens):
            for g in gens:
                yield from g

        def rstd_of(bank, n, scale, eps, out_ap, *after):
            a = A.act(out_ap, bank.t[:, 0:n], AF.Ln, *after, scale=scale, bias=eps)
            r = A.act(out_ap, out_ap, AF.Exp, a, scale=-0.5)
            bank.free = (a,)
            return r

        def split(h, l, src, ready):
            a = A.copy(h, src, *ready)
            b = V.tt(l, src, h.bitcast(F32), OP.subtract, a)
            return (a, b)

        pair = lambda t, j: t[:, 512 * j:512 * j + 512]
        x_ = lambda j: xT[:, 2 * j:2 * j + 2, :].rearrange("p k t -> p (k t)")

        class Stats:

            def __init__(self, bank):
                self.bank, self.late, self.n = bank, [], 0
                E.wait(*bank.free)

            def square(self, j, src, *ready):
                s = A.act(pair(SQ2, j), src, AF.Square, *ready)
                self.late.append((j, s))
                return s

            def flush(self):
                tok = None
                while self.late:
                    j, s = self.late.pop(0)
                    for k in range(2):
                        self.n += 1
                        tok = mm(self.bank.t[:, 0:T], C("ones"), pair(SQ2, j)[:, k * T:(k + 1) * T], self.n == 1, self.n == 8, s, done=k == 1)
                return tok

            def rstd(self):
                t = self.flush()
                return rstd_of(self.bank, T, 1.0 / D, C("eps6"), RS[:, 0:T], t)

        def normalised(gain, r):
            toks = []
            for j in range(4):
                for k in (2 * j, 2 * j + 1):
                    t = V.stt(SQ2[:, k * T:(k + 1) * T], xT[:, k, :], gain[:, k:k + 1], RS[:, 0:T], OP.mult, OP.mult, r)
                h, l = (x[:, 2 * j:2 * j + 2, :].rearrange("p k t -> p (k t)") for x in (hh, hl))
                a = A.copy(h, pair(SQ2, j), t)
                b = (V if j % 2 == 0 else G).tt(l, pair(SQ2, j), h.bitcast(F32), OP.subtract, a)
                toks.append((a, b))
            return toks

        def norm_x(gain, ready, bank):
            st = Stats(bank)
            for j in range(4):
                st.square(j, x_(j), *ready)
            return normalised(gain, st.rstd())

        class PostNorm:

            def __init__(self, gain, bank):
                self.gain, self.st, self.toks = gain, Stats(bank), []

            def evac(self, m0, n, b, tok):
                j = m0 // 2
                self.st.flush()
                s = self.st.square(j, b.t[:, :], tok)
                for m in (m0, m0 + 1):
                    v = V.ts(MG[:, m * T:(m + 1) * T], b.t[:, (m - m0) * T:(m - m0 + 1) * T], self.gain[:, m:m + 1], None, OP.mult, None, s)
                b.free = (v,)
                self.toks.append(v)

            def finish(self, gain, bank):
                r = self.st.rstd()
                st = Stats(bank)
                for j in range(4):
                    e = G if j == 2 else V
                    w = e.tt(pair(MG, j).rearrange("p (m t) -> p m t", t=T), pair(MG, j).rearrange("p (m t) -> p m t", t=T),
                             wide(RS[:, 0:T], 1, 2), OP.mult, r, self.toks[j])
                    self.toks[j] = w
                for j in (0, 1, 3, 2):
                    w = V.tt(x_(j), x_(j), pair(MG, j), OP.add, self.toks[j])
                    st.square(j, x_(j), w)
                return normalised(gain, st.rstd()) if gain is not None else (w, st)

        class Residual:

            def __init__(self, bank):
                self.st = Stats(bank)

            def evac(self, m0, n, b, tok):
                self.st.flush()
                t = V.tt(x_(m0 // 2), x_(m0 // 2), b.t[:, :], OP.add, tok)
                b.free = (t,)
                self.st.square(m0 // 2, x_(m0 // 2), t)

            def finish(self, gain):
                return normalised(gain, self.st.rstd())

        def everything():
            return tuple(x.done() for x in (A, V, G, E))

        U = slot("U", 0, 3)
        KT, KB, VB = slot("KT", 0), slot("KB", 1), slot("VB", 2)
        Aq, Ak, Av = slot("Aq", 3), slot("Ak", 4), slot("Av", 5)
        QKV = slot("QKV", 3, 3)
        QK = slot("QK", 3, 2)
        SQ = slot("SQ", 6, 2)
        T0, EG, DT, M, MT, AT = (slot(n, 6 + i) for i, n in enumerate(("T0", "EG", "DT", "M", "MT", "AT")))
        X, Y, LT = slot("X", 12), slot("Y", 13), slot("LT", 14)
        SV = slot("SV", 15)
        SM = slot("SM", 16)
        Z = slot("Z", 17)
        RQ, RK, RV, RG, PU = (slot(n, 18 + i) for i, n in enumerate(("RQ", "RK", "RV", "RG", "PU")))
        RQK = slot("RQK", 18, 2)
        GT = slot("GT", 23, 2)
        YY = slot("YY", 25, 2)
        OD = slot("OD", 27)
        BH, BL = slot("BH", 28, dt=F32R, shape=[P, 4, T]), slot("BL", 29, dt=F32R, shape=[P, 4, T])
        R0, R1 = slot("R0", 0, 2), slot("R1", 2, 2)
        KZ, ST, RR, OR, SR, O2 = slot("KZ", 4), slot("ST", 5), slot("RR", 6, 2), slot("OR", 8), slot("SR", 9), slot("O2", 10)
        PA, PB, PC = slot("PA", 25), slot("PB", 26), slot("PC", 22)
        FH, FL = slot("FH", 0, dt=F32R, shape=[P, 32, T]), slot("FL", 8, dt=F32R, shape=[P, 32, T])
        FT, FS = slot("FT", 16), slot("FS", 17)
        SQ2, MG, RS = slot("SQ2", 18, 2), slot("MG", 20, 2), slot("RS", 22)

        def v3(t, n=T):
            return t[:, :].rearrange("p (m t) -> p m t", t=n)

        def copy_to(dst, toks):
            def evac(m0, n, b, tok):
                t = A.copy(dst[:, m0 * T:(m0 + n) * T], b.t[:, 0:n * T], tok)
                b.free = (t,)
                toks.append(t)
            return evac

        def branch(what, src, ready, nready, nk, gate, gready, ngate, first, ydone, *after):
            while len(ready) < nready:
                yield BLOCKED
            assert len(gready) == ngate
            s = split(BH[:, 0:nk, :].rearrange("p k t -> p (k t)"), BL[:, 0:nk, :].rearrange("p k t -> p (k t)"), src, (*ready, *after))
            g = A.act(gate[:, :], gate[:, :], AF.Sigmoid, *gready)

            def evac(m0, n, b, tok):
                c = slice(m0 * T, (m0 + n) * T)
                if first:
                    t = V.tt(YY[:, c], b.t[:, 0:n * T], gate[:, c], OP.mult, tok, g, *after)
                    b.free = (t,)
                else:
                    u = V.tt(gate[:, c], b.t[:, 0:n * T], gate[:, c], OP.mult, tok, g)
                    b.free = (u,)
                    t = V.tt(YY[:, c], YY[:, c], gate[:, c], OP.add, u)
                ydone.append(t)
            yield from project(what, 8, (BH, BL), nk, [s] * 4, evac)

        def gate_evac(toks, ydone, n):
            def evac(m0, n_, b, tok):
                assert len(ydone) == n
                t = A.copy(GT[:, m0 * T:(m0 + n_) * T], b.t[:, 0:n_ * T], tok, *ydone[-1:])
                b.free = (t,)
                toks.append(t)
            return evac

        def delta_rule(l, qkv, z, abtok, out):
            B0, B1, B2, B3 = banks[0:4]
            bk = lambda b: b.t[:, :]
            s = A.act(SQ[:, :], QK[:, :], AF.Square, *qkv)
            for j in range(4):
                E.wait(s, *banks[j].free)
                t = mm(bk(banks[j]), C("ones"), SQ[:, 512 * j:512 * j + 512], True, True, done=True)
                r = A.act(SQ[:, 512 * j:512 * j + 512], bk(banks[j]), AF.Ln, t, bias=C("eps6"))
                banks[j].free = (r,)
            r = A.act(SQ[:, :], SQ[:, :], AF.Exp, r, scale=-0.5)
            n1 = V.stt(Aq[:, :], Aq[:, :], 128.0 ** -0.5, SQ[:, 0:1024], OP.mult, OP.mult, r)
            n2 = V.tt(Ak[:, :], Ak[:, :], SQ[:, 1024:2048], OP.mult, r)
            yield 2
            a_, be, g_, G_, eg, kx = (SM[:, 16 * i:16 * i + 8] for i in range(6))
            u1, u2 = SM[:, 128:136], SM[:, 144:152]
            AB = SM[:, 192:208].rearrange("p (s c) -> p c s", s=2)
            hs = lambda ap: ap.rearrange("p (h s) -> p h s", s=2)
            e1 = A.act(hs(be), AB[:, 0:4, :], AF.Exp, *abtok, scale=-1.0)
            w = V.ts(be, be, 1.0, None, OP.add, None, e1)
            bdone = V.recip(be, be, w)
            w = V.tt(hs(a_), AB[:, 4:8, :], hs(Q("dtb", l)), OP.add, *abtok)
            w1 = V.ts(u1, a_, -1.0, None, OP.mult, None, w)
            w1 = V.tt(u1, u1, a_, OP.max, w1)
            e1 = A.act(u1, u1, AF.Exp, w1, scale=-1.0)
            e1 = A.act(u1, u1, AF.Ln, e1, bias=C("one"))
            w = V.stt(a_, a_, 0.0, u1, OP.max, OP.add, e1)
            e2 = A.act(u2, Q("alog", l), AF.Exp, abtok[0])
            gd = V.stt(g_, a_, -1.0, u2, OP.mult, OP.mult, w, e2)
            rg = V.tt(v3(T0, 128), wide(C("upper"), 1, 8), wide(g_, 2, 128), OP.mult, gd, s, r, n1, n2)
            E.wait(rg)
            for j in range(2):
                E.wait(*banks[j].free)
                t = mm(bk(banks[j]), C("ones"), T0[:, 512 * j:512 * j + 512], True, True, done=True)
            E.wait(*B2.free)
            mm(B2.t[:, 0:8], C("upper"), g_, True, True)
            t2 = mm(B2.t[:, 8:16], C("chunk"), g_, True, True, done=True)
            yield
            d1 = V.copy(SM[:, 48:64], B2.t[:, 0:16], t2)
            B2.free = (d1,)
            G_, GL = SM[:, 48:56], SM[:, 56:64]
            w = V.tt(kx, GL, G_, OP.subtract, d1)
            e3 = A.act(eg, G_, AF.Exp, d1)
            e4 = A.act(kx, kx, AF.Exp, w)
            w3 = V.tt(eg, eg, be, OP.mult, e3, bdone)
            for j in range(2):
                c = slice(512 * j, 512 * j + 512)
                a = A.act(EG[:, c], bk(banks[j]), AF.Exp, t)
                b = V.tt(DT[:, c].rearrange("p (b t) -> p b t", t=128), bk(banks[j]).rearrange("p (b t) -> p b t", t=128),
                         wide(G_[:, 4 * j:4 * j + 4], 2, 128), OP.subtract, a, d1)
                banks[j].free = (b,)
            b = V.tt(v3(DT, 128), v3(DT, 128), wide(C("upper"), 1, 8), OP.mult, b)
            b = A.act(DT[:, :], DT[:, :], AF.Exp, b)
            dt = V.tt(v3(DT, 128), v3(DT, 128), wide(C("upper"), 1, 8), OP.mult, b)
            yield 2
            kb3 = lambda t, b: t[:, 128 * b:128 * b + 128]
            E.wait(n1, n2)
            for j in range(2):
                E.wait(*banks[j].free)
                for b in range(4 * j, 4 * j + 4):
                    t = mm(banks[j].t[:, 128 * (b % 4):128 * (b % 4) + 128], kb3(Ak, b), kb3(Ak, b), True, True, done=b % 4 == 3)
            E.wait(dt)
            for j in range(2):
                E.wait(*banks[2 + j].free)
                for b in range(4 * j, 4 * j + 4):
                    fn = lambda e, o=banks[2 + j].t[:, 128 * (b % 4):128 * (b % 4) + 128], i=kb3(DT, b): e.transpose(o, i, C("eye", CONST1))
                    if b % 4 == 3:
                        tt_ = E.do(fn)
                    else:
                        E.quiet(fn)
            for j in range(2):
                c = slice(512 * j, 512 * j + 512)
                w = V.tt(M[:, c].rearrange("p (b t) -> p b t", t=128), bk(banks[j]).rearrange("p (b t) -> p b t", t=128),
                         wide(be[:, 4 * j:4 * j + 4], 2, 128), OP.mult, t, bdone)
                banks[j].free = (w,)
                w = V.tt(M[:, c], M[:, c], bk(banks[2 + j]), OP.mult, w, tt_)
                banks[2 + j].free = (w,)
            md = w
            yield
            def transposed(src, bb, *after):
                E.wait(*after)
                for j in range(2):
                    E.wait(*bb[j].free)
                    for b in range(4 * j, 4 * j + 4):
                        fn = lambda e, o=bb[j].t[:, 128 * (b % 4):128 * (b % 4) + 128], i=kb3(src, b): e.transpose(o, i, C("eye", CONST1))
                        if b % 4 == 3:
                            tok = E.do(fn)
                        else:
                            E.quiet(fn)
                return tok

            def scaled(dst, bb, by, tok, *after):
                for j in range(2):
                    w = V.tt(dst[:, 512 * j:512 * j + 512].rearrange("p (b t) -> p b t", t=128),
                             bk(bb[j]).rearrange("p (b t) -> p b t", t=128), wide(by[:, 4 * j:4 * j + 4], 2, 128), OP.mult, tok, *after)
                    bb[j].free = (w,)
                return w

            t = transposed(M, (B0, B1), md)
            for j in range(2):
                mt = A.copy(MT[:, 512 * j:512 * j + 512], bk(banks[j]), t)
                banks[j].free = (mt,)
            lev = lambda s, tr=False: C("levT" if tr else "lev")[:, 128 * s:128 * s + 128]
            w = V.tt(v3(X, 128), v3(M, 128), wide(lev(0), 1, 8), OP.mult, md)
            xd = V.stt(v3(X, 128), v3(X, 128), -1.0, wide(C("eye"), 1, 8), OP.mult, OP.add, w)
            w = V.tt(v3(Y, 128), v3(MT, 128), wide(lev(0, True), 1, 8), OP.mult, mt)
            yd = V.stt(v3(Y, 128), v3(Y, 128), -1.0, wide(C("eye"), 1, 8), OP.mult, OP.add, w)
            lt = G.tt(v3(LT, 128), v3(MT, 128), wide(lev(1, True), 1, 8), OP.mult, mt)
            yield
            for j in range(2):
                E.wait(*banks[2 + j].free)
                for b in range(4 * j, 4 * j + 4):
                    t = mm(banks[2 + j].t[:, 128 * (b % 4):128 * (b % 4) + 128], kb3(Ak, b), kb3(Aq, b), True, True, done=b % 4 == 3)
            for j in range(2):
                c = slice(512 * j, 512 * j + 512)
                atd = V.tt(AT[:, c], DT[:, c], bk(banks[2 + j]), OP.mult, t)
                banks[2 + j].free = (atd,)
            qd = G.tt(Aq[:, :], Aq[:, :], EG[:, :], OP.mult, t, a)
            yield
            side = [0]

            def extra():
                if side[0] == 0:
                    tk = transposed(Ak, (B2, B3))
                    w1 = scaled(KT, (B2, B3), kx, tk, e4)
                    side.append(w1)
                elif side[0] == 1:
                    tk = transposed(Ak, (B2, B3))
                    side.append(scaled(KB, (B2, B3), eg, tk, w3))
                elif side[0] == 2:
                    tk = transposed(Av, (B2, B3), *qkv)
                    side.append(scaled(VB, (B2, B3), be, tk, bdone))
                side[0] += 1

            for s_ in range(1, 6):
                E.wait(lt, xd, yd)
                for j in range(2):
                    E.wait(*banks[j].free)
                    for b in range(4 * j, 4 * j + 4):
                        t = mm(banks[j].t[:, 128 * (b % 4):128 * (b % 4) + 128], kb3(LT, b), kb3(X, b), True, True, done=b % 4 == 3)
                for j in range(2):
                    w = A.copy(T0[:, 512 * j:512 * j + 512], bk(banks[j]), t)
                    banks[j].free = (w,)
                if s_ < 5:
                    lt = G.tt(v3(LT, 128), v3(MT, 128), wide(lev(s_ + 1, True), 1, 8), OP.mult, t)
                yield
                E.wait(w)
                if s_ < 5:
                    for j in range(2):
                        E.wait(*banks[j].free)
                        for b in range(4 * j, 4 * j + 4):
                            t1 = mm(banks[j].t[:, 128 * (b % 4):128 * (b % 4) + 128], kb3(Y, b), kb3(T0, b), True, True, done=b % 4 == 3)
                for j in range(2):
                    E.wait(*banks[2 + j].free)
                    for b in range(4 * j, 4 * j + 4):
                        t2 = mm(banks[2 + j].t[:, 128 * (b % 4):128 * (b % 4) + 128], kb3(T0, b), kb3(Y, b), True, True, done=b % 4 == 3)
                for j in range(2):
                    c = slice(512 * j, 512 * j + 512)
                    if s_ < 5:
                        xd = V.tt(X[:, c], X[:, c], bk(banks[j]), OP.subtract, t1)
                        banks[j].free = (xd,)
                    yd = V.tt(Y[:, c], Y[:, c], bk(banks[2 + j]), OP.subtract, t2)
                    banks[2 + j].free = (yd,)
                extra()
                yield
            ktd, kbd, vbd = side[1:4]
            E.wait(kbd, vbd, yd)
            for j in range(2):
                E.wait(*banks[j].free)
                for b in range(4 * j, 4 * j + 4):
                    t = mm(banks[j].t[:, 128 * (b % 4):128 * (b % 4) + 128], kb3(KB, b), kb3(Y, b), True, True, done=b % 4 == 3)
            for j in range(2):
                E.wait(*banks[2 + j].free)
                for b in range(4 * j, 4 * j + 4):
                    t2 = mm(banks[2 + j].t[:, 128 * (b % 4):128 * (b % 4) + 128], kb3(Y, b), kb3(VB, b), True, True, done=b % 4 == 3)
            for j in range(2):
                c = slice(512 * j, 512 * j + 512)
                wt = A.copy(M[:, c], bk(banks[j]), t)
                banks[j].free = (wt,)
                ud = A.copy(MT[:, c], bk(banks[2 + j]), t2)
                banks[2 + j].free = (ud,)
            yield
            St, VN = SV[:, 0:512], SV[:, 512:1024]
            hv = lambda ap: ap.rearrange("p (h t) -> p h t", h=4)
            sd = None
            OB = (B2, B3)
            for n in range(4):
                half, q = n // 2, n % 2
                r = slice(64 * q, 64 * q + 64)
                u_c = hv(MT[:, :])[r, :, 128 * half:128 * half + 128]
                if n == 0:
                    vn = V.copy(hv(VN)[r], u_c, ud)
                else:
                    E.wait(sd, wt, *B0.free)
                    for h in range(4):
                        c0 = 256 * h + 128 * half + 64 * q
                        t = mm(B0.t[r, 128 * h:128 * h + 128], M[:, c0:c0 + 64], St[:, 128 * h:128 * h + 128], True, True, done=h == 3)
                    vn = V.stt(hv(VN)[r], hv(B0.t[r, :]), -1.0, u_c, OP.mult, OP.add, t, ud)
                    B0.free = (vn,)
                yield
                E.wait(vn, ktd, *B1.free)
                for h in range(4):
                    b = 2 * h + half
                    t = mm(B1.t[:, 128 * h:128 * h + 128], KT[r, 128 * b:128 * b + 128], hv(VN)[r, h, :], True, True, done=h == 3)
                E.wait(atd, qd, *(OB[0].free + OB[1].free if n == 0 else ()))
                for h in range(4):
                    b = 2 * h + half
                    o = OB[h // 2].t[:, 256 * (h % 2) + 64 * n:256 * (h % 2) + 64 * n + 64]
                    if n:
                        mm(o, St[:, 128 * h:128 * h + 128], Aq[:, 256 * h + 64 * n:256 * h + 64 * n + 64], True, False)
                    to = mm(o, hv(VN)[r, h, :], AT[r, 128 * b + 64 * q:128 * b + 64 * q + 64], n == 0, True, done=h == 3)
                if n < 3:
                    dl = wide(v3(EG)[:, :, 64 * n + 63], 2, 128)
                    if n == 0:
                        sd = V.copy(St, bk(B1), t)
                    else:
                        sd = V.tt(hv(St), hv(St), dl, OP.mult, t, to)
                        sd = V.tt(St, St, bk(B1), OP.add, sd)
                    B1.free = (sd,)
                yield
            for j in range(2):
                o = A.copy(OD[:, 512 * j:512 * j + 512], bk(OB[j]), to)
                OB[j].free = (o,)
            s = A.act(T0[:, :], OD[:, :], AF.Square, o)
            yield
            E.wait(s)
            for j in range(2):
                E.wait(*banks[j].free)
                t = mm(bk(banks[j]), C("ones"), T0[:, 512 * j:512 * j + 512], True, True, done=True)
                a = A.act(EG[:, 512 * j:512 * j + 512], bk(banks[j]), AF.Ln, t, to, sd, scale=1.0 / 128, bias=C("eps6"))
                banks[j].free = (a,)
            a = A.act(EG[:, :], EG[:, :], AF.Exp, a, scale=-0.5)
            z_ = A.act(Z[:, :], Z[:, :], AF.Silu, *z)
            w = V.stt(OD[:, :], OD[:, :], Q("dnout", l), EG[:, :], OP.mult, OP.mult, a)
            w = V.tt(OD[:, :], OD[:, :], Z[:, :], OP.mult, w, z_)
            out.append(w)

        def pooling(l, pu, out, *after):
            PU3, A3, B3_, C3 = v3(PU), v3(PA), v3(PB), v3(PC)
            w = G.copy(A3, PU3, *pu, *after)
            w = G.tt(A3[:, :, 1:T], PU3[:, :, 1:T], PU3[:, :, 0:T - 1], OP.add, w)
            w = G.copy(B3_, A3, w)
            w = G.tt(B3_[:, 1:4, 2:T], A3[:, 1:4, 2:T], A3[:, 1:4, 0:T - 2], OP.add, w)
            w = G.copy(A3[:, 2:4, :], B3_[:, 2:4, :], w)
            w = G.tt(A3[:, 2:4, 4:T], B3_[:, 2:4, 4:T], B3_[:, 2:4, 0:T - 4], OP.add, w)
            w = G.copy(B3_[:, 2:4, :], A3[:, 2:4, :], w)
            w = G.tt(B3_[:, 3:4, 8:T], A3[:, 3:4, 8:T], A3[:, 3:4, 0:T - 8], OP.add, w)
            w = G.tt(PB[:, :], PB[:, :], C("cnt"), OP.mult, w)
            w = G.tt(PB[:, :], PB[:, :], PU[:, :], OP.subtract, w)
            for _ in range(7):
                yield
            E.wait(w)
            for j in range(2):
                b = next_bank()
                E.wait(*b.free)
                for g in (2 * j, 2 * j + 1):
                    c = l * N_SMALL + 64 + 128 * g
                    t = mm(b.t[:, T * (g % 2):T * (g % 2) + T], small[:, c:c + 128], PB[:, T * g:T * g + T], True, True, done=True)
                for g in (2 * j, 2 * j + 1):
                    o = A.act(PC[:, T * g:T * g + T], b.t[:, T * (g % 2):T * (g % 2) + T], AF.Copy, t, w, scale=Q("pscale", l)[:, g:g + 1])
                b.free = (o,)
            out.append(o)
            yield

        def retention(l, rqk, rv, rg, out):
            start = everything()
            E.wait(*rqk)
            w0 = G.tt(v3(R0), v3(RQK), wide(C("cos"), 1, 8), OP.mult, *rqk, *start)
            for j in range(4):
                b = banks[j]
                E.wait(*b.free)
                t = mm(b.t[:, :], C("rot"), RQK[:, 512 * j:512 * j + 512], True, True, done=True)
                w = V.tt(R1[:, 512 * j:512 * j + 512].rearrange("p (m t) -> p m t", t=T), b.t[:, :].rearrange("p (m t) -> p m t", t=T),
                         wide(C("sin"), 1, 2), OP.mult, t, *start)
                b.free = (w,)
            rot = V.tt(RQK[:, :], R0[:, :], R1[:, :], OP.add, w, w0, t)
            yield 3
            kb3 = lambda t, b: t[:, 128 * b:128 * b + 128]
            E.wait(rot)
            for j in range(2):
                E.wait(*banks[j].free)
                for b in range(4 * j, 4 * j + 4):
                    fn = lambda e, o=banks[j].t[:, 128 * (b % 4):128 * (b % 4) + 128], i=kb3(RK, b): e.transpose(o, i, C("eye", CONST1))
                    tk = E.do(fn) if b % 4 == 3 else E.quiet(fn)
            for j in range(2):
                for hh_ in range(2):
                    h = 2 * j + hh_
                    kz = A.act(KZ[:, 256 * h:256 * h + 256], banks[j].t[:, 256 * hh_:256 * hh_ + 256], AF.Copy, tk, *start, scale=C("zeta")[:, h:h + 1])
                banks[j].free = (kz,)
            for j in range(2):
                E.wait(*banks[2 + j].free)
                for b in range(4 * j, 4 * j + 4):
                    t = mm(banks[2 + j].t[:, 128 * (b % 4):128 * (b % 4) + 128], kb3(RK, b), kb3(RQ, b), True, True, done=b % 4 == 3)
            for j in range(2):
                for h2 in range(2):
                    h = 2 * j + h2
                    st = V.tt(ST[:, 256 * h:256 * h + 256].rearrange("p (s t) -> p s t", s=2),
                              banks[2 + j].t[:, 256 * h2:256 * h2 + 256].rearrange("p (s t) -> p s t", s=2),
                              wide(C("rmask")[:, 128 * h:128 * h + 128], 1, 2), OP.mult, t, *start)
                banks[2 + j].free = (st,)
            qx = [G.tt(v3(RQ, 64)[:, 4 * h:4 * h + 4, :], v3(RQ, 64)[:, 4 * h:4 * h + 4, :], wide(C("xi")[:, 64 * h:64 * h + 64], 1, 4), OP.mult, t)
                  for h in range(4)][-1]
            yield 3
            rr = lambda n, h: RR[:, 512 * (n - 1) + 128 * h:512 * (n - 1) + 128 * h + 128]
            E.wait(kz, *rv)
            rd = None
            for n in range(3):
                half, q = n // 2, n % 2
                r = slice(64 * q, 64 * q + 64)
                b = banks[n % 2]
                E.wait(*b.free)
                for h in range(4):
                    t = mm(b.t[:, 128 * h:128 * h + 128], KZ[r, 256 * h + 128 * half:256 * h + 128 * half + 128],
                           RV[r, 512 * half + 128 * h:512 * half + 128 * h + 128], True, True, done=h == 3)
                for h in range(4):
                    src = b.t[:, 128 * h:128 * h + 128]
                    if n == 0:
                        rd = V.copy(rr(1, h), src, t, *start)
                    else:
                        rd = V.stt(rr(n + 1, h), rr(n, h), CHUNK_DECAY[h], src, OP.mult, OP.add, t, rd)
                b.free = (rd,)
                yield 2
            E.wait(st, qx, rd)
            for j in range(2):
                E.wait(*banks[2 + j].free)
                for b in range(4 * j, 4 * j + 4):
                    h, half = b // 2, b % 2
                    o = banks[2 + j].t[:, 128 * (b % 4):128 * (b % 4) + 128]
                    mm(o, RV[:, 512 * half + 128 * h:512 * half + 128 * h + 128], kb3(ST, b), True, False, skip=True)
                    for q in range(2):
                        n = 2 * half + q
                        if n:
                            t = mm(banks[2 + j].t[:, 128 * (b % 4) + 64 * q:128 * (b % 4) + 64 * q + 64], rr(n, h),
                                   RQ[:, 256 * h + 64 * n:256 * h + 64 * n + 64], False, q == 1, skip=True, done=b % 4 == 3 and q == 1)
            for j in range(2):
                o = A.copy(OR[:, 512 * j:512 * j + 512], banks[2 + j].t[:, :], t, *start)
                banks[2 + j].free = (o,)
            yield 3
            E.wait(o)
            for j in range(2):
                E.wait(*banks[j].free)
                t = mm(banks[j].t[:, :], C("ones"), OR[:, 512 * j:512 * j + 512], True, True, done=True)
                w = V.stt(OR[:, 512 * j:512 * j + 512], banks[j].t[:, :], -1.0 / 128, OR[:, 512 * j:512 * j + 512], OP.mult, OP.add, t)
                banks[j].free = (w,)
            s = A.act(O2[:, :], OR[:, :], AF.Square, w)
            yield 2
            E.wait(s)
            for j in range(2):
                E.wait(*banks[j].free)
                t = mm(banks[j].t[:, :], C("ones"), O2[:, 512 * j:512 * j + 512], True, True, done=True)
                a = A.act(SR[:, 512 * j:512 * j + 512], banks[j].t[:, :], AF.Ln, t, *start, scale=1.0 / 128, bias=C("eps5"))
                banks[j].free = (a,)
            a = A.act(SR[:, :], SR[:, :], AF.Exp, a, scale=-0.5)
            z_ = A.act(RG[:, :], RG[:, :], AF.Silu, *rg)
            for h in range(4):
                c = slice(T * h, T * h + T)
                w = V.stt(OR[:, c], OR[:, c], Q("retout", l)[:, h:h + 1], SR[:, c], OP.mult, OP.mult, a)
            w = V.tt(OR[:, :], OR[:, :], RG[:, :], OP.mult, w, z_)
            out.append(w)

        def first_layer(l, h):
            flat = [t for p in h for t in p]
            cw = Q("conv", l).rearrange("p (m i) -> p m i", i=4)
            U3, A3 = v3(U), v3(QKV)
            conv = []

            def conv_evac(m0, n, b, tok):
                for m in range(m0, m0 + n):
                    a = A.act(A3[:, m, :], b.t[:, (m - m0) * T:(m - m0 + 1) * T], AF.Copy, tok, scale=cw[:, m, 3:4])
                t = A.copy(U[:, m0 * T:(m0 + n) * T], b.t[:, 0:n * T], tok)
                b.free = (t,)
                for m in range(m0, m0 + n):
                    w = t
                    for j in range(1, 4):
                        w = V.stt(A3[:, m, j:T], U3[:, m, 0:T - j], cw[:, m, 3 - j:4 - j], A3[:, m, j:T], OP.mult, OP.add, w, a)
                conv.append(w)

            run(project(("qkv", l), 12, (hh, hl), 8, h, conv_evac))
            E.wait(small_ready)
            b = next_bank()
            E.wait(*b.free)
            for s in range(2):
                for k in range(8):
                    for n, x in enumerate((hh, hl)):
                        c = l * N_SMALL + 8 * k
                        t = mm(b.t[:, 8 * s:8 * s + 8], x[:, k, 128 * s:128 * s + 128].bitcast(F32), small[:, c:c + 8],
                               k == 0 and n == 0, k == 7 and n == 1, done=(s, k, n) == (1, 7, 1))
            ab = A.copy(SM[:, 192:208], b.t[:, 0:16], t)
            b.free = (ab,)
            for e in (A, V, G, E):
                e.wait(c1_ready)
            sq = A.act(QKV[:, :], QKV[:, :], AF.Silu, *conv)
            z, rqk, rv, rg, pu, g0, g1, g2, od, oo, op_, yd = ([] for _ in range(12))

            def rv_evac(s, b, tok):
                t = A.copy(RV[:, 512 * s:512 * s + 512], b.t[:, :], tok)
                b.free = (t,)
                rv.append(t)

            fill = chain(project(("pu", l), 4, (hh, hl), 8, h, copy_to(PU, pu)),
                         project(("z", l), 4, (hh, hl), 8, h, copy_to(Z, z)),
                         project(("rqk", l), 8, (hh, hl), 8, h, copy_to(RQK, rqk)),
                         by_token(("rv", l), h, rv_evac),
                         project(("rg", l), 4, (hh, hl), 8, h, copy_to(RG, rg)),
                         project(("gate0", l), 8, (hh, hl), 8, h, copy_to(GT, g0)))

            def first_mixers():
                dn = delta_rule(l, (sq,), z, (ab,), od)
                pool = None
                for n in dn:
                    yield n
                    if pool is None and len(pu) == 2:
                        pool = pooling(l, pu, op_)
                    if pool is not None:
                        next(pool, None)

            run(first_mixers(), fill)
            fill = chain(fill, branch(("wdn", l), OD, od, 1, 4, GT, g0, 4, True, yd, *op_),
                         project(("gate1", l), 8, (hh, hl), 8, h, gate_evac(g1, yd, 4)),
                         branch(("wpool", l), PC, op_, 1, 4, GT, g1, 4, False, yd, *flat),
                         project(("gate2", l), 8, (hh, hl), 8, h, gate_evac(g2, yd, 8)))
            run(retention(l, rqk, rv, rg, oo), fill)
            run(fill)
            run(branch(("wret", l), OR, oo, 1, 4, GT, g2, 4, False, yd))
            yh = split(hh[:, :, :].rearrange("p k t -> p (k t)"), hl[:, :, :].rearrange("p k t -> p (k t)"), YY[:, :], (yd[-1], E.done()))
            pn = PostNorm(Q("mixpost", l), banks[0])
            run(project(("wout", l), 8, (hh, hl), 8, [yh] * 4, pn.evac))
            h2 = pn.finish(Q("ffnpre", l), banks[1])
            ready = []

            def ffn_evac(m0, n, b, tok):
                i = m0 // 2
                f = FT[:, 256 * (i % 4):256 * (i % 4) + 256]
                free = ready[i - 4] if i >= 4 else ()
                a = A.act(f, b.t[:, 0:T], AF.Silu, tok, *free)
                w = V.tt(f, b.t[:, T:2 * T], f, OP.mult, a, tok)
                b.free = (w,)
                hi = A.copy(FH[:, i, :], f, w)
                lo = V.tt(FL[:, i, :], f, FH[:, i, :].bitcast(F32), OP.subtract, hi)
                ready.append((hi, lo))

            gu = project(("gu", l), 44, (hh, hl), 8, h2, ffn_evac)
            if l == DEPTH - 1:
                for _ in range(8):
                    next(gu)
                rope_tables()
            run(gu)
            pn = PostNorm(Q("ffnpost", l), banks[7])
            down(("down", l), 22, FH, FL, ready, pn.evac)
            return pn.finish(Q("mixpre", l + 1) if l + 1 < DEPTH else Q("attn", DEPTH), banks[6])

        QF = slot("QF", 0, 7)
        VT = slot("VT", 7, 2)
        LG = [slot("LG", 9, 3)[:, 1536 * i:1536 * i + 1536] for i in range(2)]
        PT = slot("PT", 12, 2)
        OO = slot("OO", 14, 3)
        REL = slot("REL", 17, 2)
        SC = slot("SC", 19)
        SS = slot("SS", 20)
        RT = slot("RT", 21)
        OTK, AM = slot("OTK", 22)[:, 0:384], slot("OTK", 22)[:, 512:896]
        CS = slot("CS", 27)
        ROPE, POS = slot("ROPE", 23), slot("POS", 24, dt=I32)
        QF3, OO3 = v3(QF), v3(OO)
        COS, SIN = CS[:, 0:256], CS[:, 256:512]
        IW = SS[:, 0:16]

        def rope_tables():
            mixed = everything()
            ready = load(cst[:, HEAD:N_CONST2], ins["const2"][:, HEAD:N_CONST2], s_c2, *mixed)
            for e in (A, V, G, E):
                c2_ready.append(ready)
            ld = load(POS[:, 0:T], ins["positions"], s_pos, *mixed)
            a, n = ROPE[:, 0:256], ROPE[:, 256:512]
            w = V.copy(a, POS[:, 0:T], ld)
            w = V.ts(a, a, C("inv", CONST2), None, OP.mult, None, w, ready)
            big, two_pi = 12582912.0, 2.0 * np.pi
            c1 = 6.28125
            c2, c3 = SPLIT_PI
            for dst, turn in ((SIN, 0.0), (COS, 0.25)):
                u = V.ts(n, a, 1.0 / two_pi, turn, OP.mult, OP.add, w)
                u = V.ts(n, n, big, None, OP.add, None, u)
                u = V.ts(n, n, big, None, OP.subtract, None, u)
                u = V.stt(dst, n, -c1, a, OP.mult, OP.add, u)
                u = V.stt(dst, n, -c2, dst, OP.mult, OP.add, u)
                u = V.stt(dst, n, -c3, dst, OP.mult, OP.add, u)
                if turn:
                    u = V.ts(dst, dst, float(np.float32(np.pi / 2)), None, OP.add, None, u)
                u = V.ts(dst, dst, 3.1415925, -3.1415925, OP.min, OP.max, u)
                w = A.act(dst, dst, AF.Sin, u)
            roping.append(w)

        c2_ready, roping = [], []

        def second_layer(l, h):
            cs = roping[0]
            ring[0], ring[1] = 0, [6, 7]
            roped = {}

            def rope(m0, n, ready):
                b = next_bank()
                E.wait(*ready, *b.free)
                w_ = n * T
                f = QF[:, m0 * T:m0 * T + w_]
                t = mm(b.t[:, 0:w_], C("rot2"), f, True, True, done=True)
                tmp = RT[:, 0:w_] if m0 // 2 % 2 else RT[:, 512:512 + w_]
                w = V.tt(tmp.rearrange("p (m t) -> p m t", t=T), b.t[:, 0:w_].rearrange("p (m t) -> p m t", t=T), wide(SIN, 1, n), OP.mult, t, cs)
                b.free = (w,)
                g = G.tt(f.rearrange("p (m t) -> p m t", t=T), f.rearrange("p (m t) -> p m t", t=T), wide(COS, 1, n), OP.mult, t, cs, *ready)
                w = V.tt(f, f, tmp, OP.add, w, g)
                for m in range(m0, m0 + n):
                    roped[m] = w

            pend = []

            def flush():
                while pend:
                    rope(*pend.pop(0))

            def evac_from(base):
                def evac(m0, n, b, tok):
                    m0 += base
                    t = A.copy(QF[:, m0 * T:(m0 + n) * T], b.t[:, 0:n * T], tok)
                    b.free = (t,)
                    flush()
                    if m0 == 8:
                        f = QF[:, 8 * T:9 * T]
                        s = A.act(REL[:, 0:T], f, AF.Square, t)
                        bb = next_bank()
                        E.wait(s, *bb.free)
                        t2 = mm(bb.t[:, 0:T], C("half"), REL[:, 0:T], True, True, done=True)
                        r = rstd_of(bb, T, 1.0 / 64, C("eps6"), REL[:, 256:512], t2)
                        t = V.stt(f, f, Q("idxk", DEPTH + l), REL[:, 256:512], OP.mult, OP.mult, r)
                    pend.append((m0, n, (t,)))
                return evac

            vt = []
            bv = lambda half, head: VT[:, 960 * half + 64 * head:960 * half + 64 * head + 64]
            cv = lambda half, kv: VT[:, 960 * half + 768 + 64 * kv:960 * half + 832 + 64 * kv]
            av = lambda half: VT[:, 960 * half + 896:960 * half + 960]

            def v_evac(group):
                def evac(s, b, tok):
                    if group == 0:
                        t = A.copy(VT[:, 960 * s:960 * s + 512], b.t[:, :], tok)
                    else:
                        A.copy(VT[:, 960 * s + 512:960 * s + 960], b.t[:, 0:448], tok)
                        t = A.act(IW[:, 8 * s:8 * s + 8], b.t[:, 448:456], AF.Copy, tok, scale=8.0 ** -0.5)
                    b.free = (t,)
                    vt.append(t)
                return evac

            run(project(("q2a", l), 11, (hh, hl), 8, h, evac_from(0)))
            run(by_token(("v2a", l), h, v_evac(0)))
            flush()
            run(by_token(("v2b", l), h, v_evac(1)))

            def index(half):
                nk = 128 * (half + 1)
                per = 512 // nk
                qs = slice(128 * half, 128 * half + 128)
                E.wait(roped[7], roped[8])
                rel = REL[:, 0:8 * nk].rearrange("p (c n t) -> p c n t", c=2, t=nk)
                toks = {}
                for par_ in range(2):
                    r = slice(64 * par_, 64 * par_ + 64)
                    for j in range(4):
                        b = banks[2 * par_ + j // per]
                        if j % per == 0:
                            E.wait(*b.free)
                        t = mm(b.t[:, nk * (j % per):nk * (j % per) + nk], QF3[r, 4 + j, qs], QF3[r, 8, 0:nk], True, True,
                               done=j % per == per - 1 or j == 3)
                        toks[par_, j // per] = t
                for par_ in range(2):
                    for k in range((4 + per - 1) // per):
                        b = banks[2 * par_ + k]
                        n = min(per, 4 - k * per)
                        w = A.act(rel[:, par_, k * per:k * per + n, :], b.t[:, 0:n * nk].rearrange("p (n t) -> p n t", t=nk), AF.Relu,
                                  toks[par_, k], *relfree, scale=0.125)
                        b.free = (w,)
                relfree.clear()
                sc = [SC[:, 0:nk], SC[:, 256:256 + nk]]
                causal = C(f"mA{half}", CONST2)
                first = True
                for par_ in range(2):
                    for j in range(4):
                        w = V.stt(sc[0], rel[:, par_, j, :], IW[:, 8 * half + 2 * j + par_:8 * half + 2 * j + par_ + 1],
                                  causal if first else sc[0], OP.mult, OP.add, w, vt[-1], vt[-2])
                        first = False
                relfree.append(w)
                yield
                m8 = SS[:, 16:24]
                for r in range(8):
                    w = V.do(lambda e, i=sc[0]: e.max(m8, i), w)
                    w = V.do(lambda e, i=sc[0], o=sc[1]: e.match_replace(o, m8, i, TAKEN), w)
                    sc = sc[::-1]
                    if r % 2:
                        yield
                am = AM[:, 128 * half:128 * half + nk]
                w = V.ts(am, sc[0], -2.0e38, NEG, OP.is_gt, OP.mult, w)
                w = V.tt(am, am, causal, OP.add, w)
                amask[half] = w
                yield

            relfree = []
            amask = {}
            lfree = {0: [], 1: []}

            def attend(turn, half, n, qtile, ktile, mask, mready, joint, sink, values, dst, otoks):
                nk = 128 * (half + 1)
                per = 512 // nk
                qs = slice(128 * half, 128 * half + 128)
                mready = (mready(),) if mready else ()
                E.wait(*(roped[qtile(i)] for i in range(n)), *(roped[ktile(i)] for i in range(n)))
                LB, free = LG[turn % 2][:, 0:2 * n * nk], lfree[turn % 2]
                L = LB.rearrange("p (c n t) -> p c n t", c=2, t=nk)
                if half == 0:
                    plan = [(0, [(0, i) for i in range(n)]), (2, [(1, i) for i in range(n)])]
                elif n == 2:
                    plan = [(0, [(0, 0), (0, 1)]), (2, [(1, 0), (1, 1)])]
                else:
                    plan = [(1, [(0, 2)]), (0, [(0, 0), (0, 1)]), (2, [(1, 0), (1, 1)]), (1, [(1, 2)])]
                where = {}
                for q, (bk, heads) in enumerate(plan):
                    b = banks[bk]
                    E.wait(*b.free)
                    if q == 3:
                        E.wait(where[0][3])
                    c0 = nk if q == 3 else 0
                    for m, (c, i) in enumerate(heads):
                        r = slice(64 * c, 64 * c + 64)
                        t = mm(b.t[:, c0 + nk * m:c0 + nk * m + nk], QF3[r, qtile(i), qs], QF3[r, ktile(i), 0:nk], True, True,
                               done=m == len(heads) - 1)
                    where[q] = (b, c0, heads, t)
                if len(plan) == 4:
                    where[0] = (*where[0][:3], where[3][3])
                for q in ((1, 2, 0, 3) if len(plan) == 4 else (0, 1)):
                    b, c0, heads, t = where[q]
                    (c, i), m = heads[0], len(heads)
                    w = V.tt(L[:, c, i:i + m, :], b.t[:, c0:c0 + m * nk].rearrange("p (n t) -> p n t", t=nk), mask(i, m), OP.add,
                             t, *mready, *free)
                    b.free = (w,)
                free.clear()
                st = [SS[:, 32 + 64 * (turn % 2) + 16 * i:40 + 64 * (turn % 2) + 16 * i] for i in range(3)]
                ng = 2 if joint else 2 * n
                Lg = LB.rearrange("p (g t) -> p g t", g=ng)
                mx, den, ex = (x[:, 0:ng] for x in st)
                w = V.red(mx, Lg, OP.max, w)
                if sink is None:
                    w = V.ts(mx, mx, -0.125, None, OP.mult, None, w)
                else:
                    w = V.stt(mx, mx, 0.125, sink, OP.mult, OP.max, w)
                    w = V.tt(ex, sink, mx, OP.subtract, w)
                    se = A.act(ex, ex, AF.Exp, w)
                    w = V.ts(mx, mx, -1.0, None, OP.mult, None, w)
                for g in range(ng):
                    a = A.act(Lg[:, g, :], Lg[:, g, :], AF.Exp, w, scale=0.125, bias=mx[:, g:g + 1], accum=den[:, g:g + 1])
                yield
                w = a
                if sink is not None:
                    w = V.tt(den, den, ex, OP.add, a, se)
                rd = V.recip(den, den, w)
                E.wait(a)
                for kb in range(half + 1):
                    for k in range((2 * n + 3) // 4):
                        b = banks[3 + k]
                        E.wait(*b.free)
                        m = min(4, 2 * n - 4 * k)
                        for j in range(4 * k, 4 * k + m):
                            fn = lambda e, o=b.t[:, 128 * (j % 4):128 * (j % 4) + 128], i=L[:, j % 2, j // 2, 128 * kb:128 * kb + 128]: e.transpose(o, i, C("eye", CONST2))
                            t = E.do(fn) if j == 4 * k + m - 1 else E.quiet(fn)
                        p = A.copy(PT[:, 768 * kb + 512 * k:768 * kb + 512 * k + 128 * m], b.t[:, 0:128 * m], t)
                        b.free = (p,)
                free.append(t)
                yield
                E.wait(p, *vt)
                b = banks[5]
                E.wait(*b.free)
                heads = [(0, c) for c in range(2)] if joint else [(i, c) for i in range(n) for c in range(2)]
                for q, (i0, c) in enumerate(heads):
                    terms = [(i, kb) for i in (range(n) if joint else [i0]) for kb in range(half + 1)]
                    for u, (i, kb) in enumerate(terms):
                        t = mm(b.t[:, 64 * q:64 * q + 64], PT[:, 768 * kb + 128 * (2 * i + c):768 * kb + 128 * (2 * i + c) + 128],
                               values(kb, i, c), u == 0, u == len(terms) - 1, done=(q, u) == (len(heads) - 1, len(terms) - 1))
                nh = len(heads)
                by = (den if joint else den.rearrange("p (c n) -> p n c", c=2))
                src = b.t[:, 0:64 * nh]
                o4 = OTK[:, 0:64 * nh]
                if joint:
                    w = V.tt(o4.rearrange("p (h d) -> p h d", d=64), src.rearrange("p (h d) -> p h d", d=64), wide(by, 2, 64), OP.mult, t, rd)
                else:
                    w = V.tt(o4.rearrange("p (n c d) -> p n c d", c=2, d=64), src.rearrange("p (n c d) -> p n c d", c=2, d=64),
                             wide(by, 3, 64), OP.mult, t, rd)
                b.free = (w,)
                yield
                b = banks[3]
                E.wait(w, *b.free)
                for q in range(nh // 2):
                    fn = lambda e, o=b.t[:, 128 * q:128 * q + 128], i=OTK[:, 128 * q:128 * q + 128]: e.transpose(o, i, C("eye", CONST2))
                    t = E.do(fn) if q == nh // 2 - 1 else E.quiet(fn)
                w = A.copy(OO3[:, dst:dst + nh // 2, qs], b.t[:, 0:64 * nh].rearrange("p (n t) -> p n t", t=128), t)
                b.free = (w,)
                otoks.append(w)

            oa, ob, oc, g0, g1, g2, yd = ([] for _ in range(7))
            mA = lambda half: lambda i, m: wide(AM[:, 128 * half:128 * half + 128 * (half + 1)], 1, m)
            mB = lambda half: lambda i, m: C(f"mB{half}", CONST2).rearrange("p (g t) -> p g t", g=3)[:, i:i + m, :]
            mC = lambda half: lambda i, m: wide(C(f"mC{half}", CONST2), 1, m)
            rounds = []
            for half in range(2):
                rounds.append((half, 3, lambda i: i, lambda i: 3, mA(half), lambda half=half: amask[half], False, None,
                               lambda kb, i, c: av(kb), 0, oa))
            for half in range(2):
                for r in range(2):
                    rounds.append((half, 2, lambda i, r=r: 11 + 2 * r + i, lambda i, r=r: 9 + r, mC(half), None, False,
                                   Q("sinks", DEPTH + l)[:, 4 * r:4 * r + 4], lambda kb, i, c, r=r: cv(kb, r), 5 + 2 * r, oc))
            for half in range(2):
                for jp in range(2):
                    rounds.append((half, 3, lambda i, jp=jp: 15 + 2 * i + jp, lambda i, jp=jp: 21 + 2 * i + jp, mB(half), None, True,
                                   None, lambda kb, i, c, jp=jp: bv(kb, 4 * i + 2 * jp + c), 3 + jp, ob))

            def attention():
                yield from index(0)
                yield from index(1)
                before = None
                for turn, r in enumerate(rounds):
                    g = attend(turn, *r)
                    next(g)
                    yield
                    if before is not None:
                        for _ in before:
                            yield
                    before = g
                for _ in before:
                    yield

            def flushing():
                flush()
                yield

            fill = chain(project(("q2b", l), 16, (hh, hl), 8, h, evac_from(11)), flushing(),
                         project(("gate0", 2 + l), 8, (hh, hl), 8, h, copy_to(GT, g0)),
                         branch(("wa", l), OO[:, 0:768], oa, 2, 3, GT, g0, 4, True, yd),
                         project(("gate2", 2 + l), 8, (hh, hl), 8, h, gate_evac(g2, yd, 4)),
                         branch(("wc", l), OO[:, 1280:2304], oc, 4, 4, GT, g2, 4, False, yd),
                         project(("gate1", 2 + l), 8, (hh, hl), 8, h, gate_evac(g1, yd, 8)),
                         branch(("wb", l), OO[:, 768:1280], ob, 4, 2, GT, g1, 4, False, yd))
            run(attention(), fill)
            run(fill)
            ring[0], ring[1] = 0, [4, 5, 6, 7]
            yh = split(hh[:, :, :].rearrange("p k t -> p (k t)"), hl[:, :, :].rearrange("p k t -> p (k t)"), YY[:, :], (yd[-1], E.done()))
            rs = Residual(banks[0])
            run(project(("wo", l), 8, (hh, hl), 8, [yh] * 4, rs.evac))
            h2 = rs.finish(Q("mlp", DEPTH + l))
            ready = []

            def mlp_evac(m0, n, b, tok):
                for i in range(m0, m0 + n):
                    f = FT[:, 256 * (i % 4):256 * (i % 4) + 256]
                    f2 = FS[:, 256 * (i % 4):256 * (i % 4) + 256]
                    free = ready[i - 4] if i >= 4 else ()
                    a = A.act(f, b.t[:, (i - m0) * T:(i - m0 + 1) * T], AF.Relu, tok, *free)
                    if i == m0 + n - 1:
                        b.free = (a,)
                    s = A.act(f2, f, AF.Square, a, *free)
                    hi = A.copy(FH[:, i, :], f2, s)
                    lo = V.tt(FL[:, i, :], f2, FH[:, i, :].bitcast(F32), OP.subtract, hi)
                    ready.append((hi, lo))

            run(project(("up", l), 32, (hh, hl), 8, h2, mlp_evac))
            rs = Residual(banks[7])
            down(("down2", l), 32, FH, FL, ready, rs.evac)
            if l + 1 < DEPTH:
                return rs.finish(Q("attn", DEPTH + l + 1))
            r = rs.st.rstd()
            for k in range(8):
                x = V.stt(xT[:, k, :], xT[:, k, :], Q("final", DEPTH + l)[:, k:k + 1], RS[:, 0:T], OP.mult, OP.mult, r)
            return x

        x_ready = load(xT[:, :, :], ins["x"], s_x)
        head_ready = load(cst[:, 0:HEAD], ins["const1"][:, 0:HEAD], s_head)
        par_ready = load(par[:, :], ins["par"], s_par)
        for _ in range(RAW):
            fetch()
        small_ready = load(small[:, :], ins["small"], s_small)
        c1_ready = load(cst[:, HEAD:N_CONST1], ins["const1"][:, HEAD:N_CONST1], s_c1)
        for e in (A, V, G, E):
            e.wait(head_ready, par_ready, x_ready)
        h = norm_x(Q("mixpre", 0), (x_ready,), banks[0])
        for l in range(DEPTH):
            h = first_layer(l, h)
        for e in (A, V, G, E):
            e.wait(*c2_ready)
        consts[0] = CONST2
        for l in range(DEPTH):
            h = second_layer(l, h)
        last = everything()
        S.wait(*last)
        for i in range(fetched[0]):
            if i >= fetched[0] - RAW:
                S.wait((s_raw[i % RAW], 16 * (i // RAW + 1)))
        S.queue.append(lambda e: e.dma_start(out, xT[:, :, :]).then_inc(s_out, 16))
        S.wait((s_out, 16))
        assert len(order) == NCHUNK, len(order)
        block = ctx.enter_context(nc.Block())
        block.sync(S.play)
        block.scalar(A.play)
        block.vector(V.play)
        block.gpsimd(G.play)
        block.tensor(E.play)
    return order


LOG_GAMMA = [np.log1p(-np.exp2(np.float32(-5.0 - h))) for h in range(4)]
CHUNK_DECAY = [float(np.exp(np.float32(64.0 * g))) for g in LOG_GAMMA]


def constants1():
    c = np.zeros((P, N_CONST1), np.float32)

    def put(name, a):
        o, w = CONST1[name]
        c[:, o:o + w] = a

    p = np.arange(P)[:, None]
    f = np.arange(P)[None, :]
    same = p // 64 == f // 64
    put("ones", 1.0)
    put("eye", p == f)
    put("eps6", 1e-6)
    put("eps5", 1e-5)
    put("one", 1.0)
    put("upper", same & (p <= f))
    put("chunk", same)
    lev = [(p // (2 << s) == f // (2 << s)) & (p // (1 << s) % 2 == 1) & (f // (1 << s) % 2 == 0) for s in range(6)]
    put("lev", np.concatenate(lev, 1))
    put("levT", np.concatenate([a.T for a in lev], 1))
    rot = np.zeros((P, P))
    for i in range(64):
        rot[i + 64, i] = -1.0
        rot[i, i + 64] = 1.0
    put("rot", rot)
    inv = np.float32(10000.0) ** (-np.arange(64, dtype=np.float32) / 64)
    ang = inv.astype(np.float32)[:, None] * np.arange(T, dtype=np.float32)[None, :]
    put("cos", np.tile(np.cos(ang.astype(np.float64)), (2, 1)))
    put("sin", np.tile(np.sin(ang.astype(np.float64)), (2, 1)))
    lg = [float(g) for g in LOG_GAMMA]
    put("rmask", np.concatenate([np.where(same, np.exp(np.abs(p - f) * g), 0) * 128 ** -0.5 for g in lg], 1))
    t = np.arange(T)[None, :]
    put("xi", np.concatenate([np.exp((t[:, 0:64] + 1) * g) for g in lg], 1))
    put("zeta", np.concatenate([np.exp((63 - p % 64) * g) * 128 ** -0.5 for g in lg], 1))
    put("cnt", np.concatenate([1.0 / np.minimum(t + 1, w) for w in (2, 4, 8, 16)], 1))
    return c


def _split_pi():
    rest = 2.0 * np.pi - 6.28125
    c2 = round(rest * 2.0 ** 21) / 2.0 ** 21
    return c2, float(np.float32(rest - c2))


SPLIT_PI = _split_pi()


def constants2():
    c = np.zeros((P, N_CONST2), np.float32)

    def put(name, a):
        o, w = CONST2[name]
        c[:, o:o + w] = a

    p = np.arange(P)[:, None]
    f = np.arange(P)[None, :]
    put("ones", 1.0)
    put("eye", p == f)
    put("eps6", 1e-6)
    put("eps5", 1e-5)
    put("one", 1.0)
    put("half", p // 64 == f // 64)
    rot = np.zeros((P, P))
    for b in range(0, P, 64):
        for i in range(32):
            rot[b + i + 32, b + i] = -1.0
            rot[b + i, b + i + 32] = 1.0
    put("rot2", rot)
    inv = np.float32(10000.0) ** (-np.arange(32, dtype=np.float32) / 32)
    put("inv", np.tile(inv, 4)[:, None])
    for half in range(2):
        t = p + 128 * half
        s = np.arange(128 * (half + 1))[None, :]
        neg = lambda ok: np.where(ok, 0.0, NEG)
        put(f"mA{half}", neg(s <= t))
        put(f"mC{half}", neg((s <= t) & (s > t - 128)))
        put(f"mB{half}", np.concatenate([neg((s <= t) & (t - s <= w) & ((t - s) % d == 0)) for w, d in ((128, 1), (512, 4), (2048, 16))], 1))
    return c


S1 = dict(qkv=(0, 1536), z=(1536, 512), ab=(2048, 8), rqk=(2056, 1024), rv=(3080, 512), rg=(3592, 512), pu=(4104, 512), gate=(4616, 3072))
S2 = {}
_at = 0
for _n, _w in (("aq", 384), ("ak", 64), ("av", 64), ("iq", 512), ("ik", 64), ("iw", 8), ("bq", 768), ("bk", 768), ("bv", 768),
               ("cq", 512), ("ck", 128), ("cv", 128), ("gate", 3072)):
    S2[_n] = (_at, _w)
    _at += _w


def pack(order, inputs):
    w = {k: np.asarray(inputs[k]) for k in ("w_in", "w_branch_dn", "w_branch_ret", "w_branch_pool", "w_out", "ffn_gate", "ffn_up", "ffn_down",
                                            "w_in_2", "w_a_2", "w_b_2", "w_c_2", "w_o_2", "w_up_2", "w_down_2")}
    made = {}

    def cols(a, at, n):
        return a[:, at:at + n]

    def tiles(a):
        k, m = a.shape[0] // P, a.shape[1] // P
        t = a.reshape(k, P, m, P).transpose(2, 0, 1, 3).reshape(-1, 8, P, P)
        return t.transpose(0, 2, 1, 3).reshape(-1, P, 1024)

    def rows(a):
        return a.reshape(-1, P, 1024)

    def moving(a):
        return a.reshape(4, 2, P, 512).transpose(0, 2, 1, 3).reshape(4, P, 1024)

    def make(name, l):
        if name in ("qkv", "z", "rqk", "rg", "pu"):
            return tiles(cols(w["w_in"][l], *S1[name]))
        if name == "rv":
            return moving(cols(w["w_in"][l], *S1["rv"]))
        if name in ("gate0", "gate1", "gate2"):
            a, s = (w["w_in"][l], S1) if l < 2 else (w["w_in_2"][l - 2], S2)
            return tiles(cols(a, s["gate"][0] + 1024 * int(name[4]), 1024))
        if name == "gu":
            g, u = w["ffn_gate"][l], w["ffn_up"][l]
            return tiles(np.stack([g.reshape(D, 22, P), u.reshape(D, 22, P)], 2).reshape(D, 2 * FF1))
        direct = dict(wdn="w_branch_dn", wpool="w_branch_pool", wret="w_branch_ret", wout="w_out", wa="w_a_2", wb="w_b_2", wc="w_c_2",
                      wo="w_o_2", up="w_up_2")
        if name == "wb":
            return tiles(w["w_b_2"][l])
        if name in direct:
            return tiles(w[direct[name]][l])
        if name == "down":
            return rows(w["ffn_down"][l])
        if name == "down2":
            return rows(w["w_down_2"][l])
        a = w["w_in_2"][l]
        c = lambda n, lo=0, m=None: a[:, S2[n][0] + lo:S2[n][0] + (lo + m if m else S2[n][1])]
        if name == "q2a":
            return tiles(np.concatenate([c("aq"), c("ak"), c("ak"), c("iq"), c("ik"), c("ik"),
                                         c("ck", 0, 64), c("ck", 0, 64), c("ck", 64, 64), c("ck", 64, 64)], 1))
        if name == "q2b":
            return tiles(np.concatenate([c("cq"), c("bq"), c("bk")], 1))
        if name == "v2a":
            return moving(c("bv", 0, 512))
        if name == "v2b":
            return moving(np.concatenate([c("bv", 512, 256), c("cv"), c("av"), c("iw"), np.zeros((D, 56), np.float32)], 1))
        raise ValueError(name)

    out = np.zeros((NCHUNK, P, 1024), np.float32)
    for i, (name, l, n) in enumerate(order):
        if (name, l) not in made:
            made = {(name, l): make(name, l)}
        out[i] = made[name, l][n]
    return out


def feature_rows(a, n):
    return np.asarray(a).reshape(n, P).T


def parameters(inputs):
    x = {k: np.asarray(v) for k, v in inputs.items()}
    par1 = np.zeros((DEPTH, P, N_PAR1), np.float32)
    par2 = np.zeros((DEPTH, P, N_PAR2), np.float32)
    small = np.zeros((DEPTH, P, N_SMALL), np.float32)
    for l in range(DEPTH):
        def put(table, dst, name, a):
            o, n = table[name]
            dst[l][:, o:o + n] = a
        put(PAR1, par1, "mixpre", feature_rows(x["mix_pre_norm"][l], 8))
        put(PAR1, par1, "mixpost", feature_rows(x["mix_post_norm"][l], 8))
        put(PAR1, par1, "ffnpre", feature_rows(x["ffn_pre_norm"][l], 8))
        put(PAR1, par1, "ffnpost", feature_rows(x["ffn_post_norm"][l], 8))
        put(PAR1, par1, "conv", x["dn_conv"][l].reshape(4, 12, P).transpose(2, 1, 0).reshape(P, 48))
        put(PAR1, par1, "dnout", feature_rows(x["dn_out_norm"][l], 1))
        put(PAR1, par1, "retout", feature_rows(x["ret_out_norm"][l], 4))
        put(PAR1, par1, "pscale", feature_rows(x["pool_scale"][l], 4))
        put(PAR1, par1, "alog", np.repeat(x["dn_A_log"][l], 2)[None, :])
        put(PAR1, par1, "dtb", np.repeat(x["dn_dt_bias"][l], 2)[None, :])
        put(PAR2, par2, "attn", feature_rows(x["attn_norm_2"][l], 8))
        put(PAR2, par2, "mlp", feature_rows(x["mlp_norm_2"][l], 8))
        put(PAR2, par2, "final", feature_rows(x["final_norm_2"], 8))
        put(PAR2, par2, "idxk", np.concatenate([x["idx_k_norm_2"][l]] * 2)[:, None])
        put(PAR2, par2, "sinks", x["sinks_2"][l].reshape(2, 2, 2).transpose(0, 2, 1).reshape(1, 8))
        small[l][:, 0:64] = x["w_in"][l][:, 2048:2056].reshape(8, P, 8).transpose(1, 0, 2).reshape(P, 64)
        small[l][:, 64:576] = x["pool_w"][l].transpose(1, 0, 2).reshape(P, 512)
    return par1, par2, small


def declare(nc):
    d = lambda n, s, t=F32: nc.dram_tensor(f"in_{n}", s, t, kind="ExternalInput").ap()
    ins = {
        "weights": d("weights", (NCHUNK, P, 1024)), "x": d("x", (P, 8, T)), "positions": d("positions", (P, T), I32),
        "const1": d("const1", (P, N_CONST1)), "const2": d("const2", (P, N_CONST2)),
        "par": d("par", (P, N_PAR)), "small": d("small", (P, DEPTH * N_SMALL)),
    }
    return ins, nc.dram_tensor("out", (P, 8, T), F32, kind="ExternalOutput").ap()


def lay_out(order, inputs):
    par1, par2, small = parameters(inputs)
    x = np.asarray(inputs["x"])[0]
    return {
        "in_weights": pack(order, inputs),
        "in_x": np.ascontiguousarray(x.T.reshape(8, P, T).transpose(1, 0, 2)),
        "in_positions": np.ascontiguousarray(np.broadcast_to(np.asarray(inputs["positions_2"])[0][None, :], (P, T))),
        "in_const1": constants1(), "in_const2": constants2(),
        "in_par": np.concatenate([*par1, *par2], 1), "in_small": np.concatenate([*small], 1),
    }


def kernel(**inputs):
    from concourse import bacc
    from concourse.bass_utils import run_bass_kernel_spmd

    nc = bacc.Bacc("TRN2", target_bir_lowering=False, num_devices=1)
    ins, out = declare(nc)
    order = program(nc, ins, out)
    r = run_bass_kernel_spmd(nc, [lay_out(order, inputs)], core_ids=[0])
    got = np.asarray(r.results[0]["out"])
    return np.ascontiguousarray(got.transpose(1, 0, 2).reshape(D, T).T)[None]
```

```python
from contextlib import ExitStack

import numpy as np
import concourse.bass as bass
from concourse import mybir

F32 = mybir.dt.float32
F32R = mybir.dt.float32r
I32 = mybir.dt.int32
OP = mybir.AluOpType
AF = mybir.ActivationFunctionType
AX = mybir.AxisListType.X

P = 128
T = 256
D = 1024
DEPTH = 2
FF1 = 2816
FF2 = 4096
NEG = -1.0e30
BLOCKED = -1
TAKEN = -3.0e38
RAW = 4
RING = 4
TAIL = 2
NCHUNK = 572
EXPLN = "natural_log_exp_and_others"

CONST1 = {}
CONST2 = {}


def _columns(table, widths):
    at = 0
    for name, w in widths:
        table[name] = (at, w)
        at += w
    return at


N_CONST1 = _columns(CONST1, [
    ("ones", 128), ("eye", 128), ("eps6", 1), ("eps5", 1), ("one", 1), ("pad", 1),
    ("upper", 128), ("chunk", 128), ("levT", 6 * 128), ("rot", 128),
    ("cos", 256), ("sin", 256), ("rmask", 4 * 128), ("xi", 4 * 64), ("zeta", 4), ("cnt", 4 * 16), ("cntw", 4)])
N_CONST2 = _columns(CONST2, [
    ("ones", 128), ("eye", 128), ("eps6", 1), ("eps5", 1), ("one", 1), ("pad", 1),
    ("half", 128), ("rot2", 128), ("inv", 1), ("mB0", 3 * 128), ("mB1", 3 * 256),
    ("mA0", 128), ("mA1", 256), ("mC0", 128), ("mC1", 256)])
N_CONST = max(N_CONST1, N_CONST2)
HEAD = CONST1["pad"][0] + 1

PAR1 = {}
PAR2 = {}
N_PAR1 = _columns(PAR1, [("mixpre", 8), ("mixpost", 8), ("ffnpre", 8), ("ffnpost", 8), ("conv", 48),
                         ("dnout", 1), ("retout", 4), ("pscale", 4), ("alog", 8), ("dtb", 8)])
N_PAR2 = _columns(PAR2, [("attn", 8), ("mlp", 8), ("final", 8), ("idxk", 1), ("sinks", 8)])
N_PAR = DEPTH * (N_PAR1 + N_PAR2)
N_SMALL = 64 + 512


class Engine:

    def __init__(self, sem):
        self.sem, self.queue, self.count, self.seen = sem, [], 0, {}

    def wait(self, *tokens):
        for sem, value in tokens:
            if self.seen.get(id(sem), 0) < value:
                self.seen[id(sem)] = value
                self.queue.append(lambda e, s=sem, v=value: e.wait_ge(s, v))

    def do(self, fn, *after):
        self.wait(*after)
        self.count += 1
        self.queue.append(lambda e, s=self.sem: fn(e).then_inc(s, 1))
        return (self.sem, self.count)

    def quiet(self, fn, *after):
        self.wait(*after)
        self.queue.append(fn)

    def done(self):
        return (self.sem, self.count)

    def play(self, e):
        for fn in self.queue:
            fn(e)


class Vec(Engine):
    def tt(self, out, a, b, op, *after):
        return self.do(lambda e: e.tensor_tensor(out, a, b, op), *after)

    def ts(self, out, a, s1, s2, op0, op1, *after):
        if op1 is None:
            return self.do(lambda e: e.tensor_scalar(out, a, s1, None, op0), *after)
        return self.do(lambda e: e.tensor_scalar(out, a, s1, s2, op0, op1), *after)

    def stt(self, out, a, s, b, op0, op1, *after):
        return self.do(lambda e: e.scalar_tensor_tensor(out=out, in0=a, scalar=s, in1=b, op0=op0, op1=op1), *after)

    def copy(self, out, a, *after):
        return self.do(lambda e: e.tensor_copy(out, a), *after)

    def red(self, out, a, op, *after):
        return self.do(lambda e: e.tensor_reduce(out, a, AX, op), *after)

    def recip(self, out, a, *after):
        return self.do(lambda e: e.reciprocal(out, a), *after)


class Act(Engine):
    table = None

    def preload(self):
        if self.table != EXPLN:
            self.table = EXPLN
            self.queue.append(lambda e: e.preload_act_table_set(EXPLN))

    def act(self, out, a, fn, *after, scale=1.0, bias=None, accum=None):
        if fn in (AF.Exp, AF.Ln):
            want = EXPLN
        elif fn in (AF.Silu, AF.Sigmoid, AF.Sin):
            want = str(fn)
        else:
            want = None
        if want == EXPLN:
            self.preload()
        elif want:
            self.table = want
        kw = {"scale": scale}
        if bias is not None:
            kw["bias"] = bias
        if accum is not None:
            kw["accum_out"] = accum
        return self.do(lambda e: e.activation(out, a, fn, **kw), *after)

    def copy(self, out, a, *after):
        return self.do(lambda e: e.copy(out, a), *after)


class Bank:

    def __init__(self, t):
        self.t, self.free = t, ()


def wide(ap, axis, n):
    shape = list(ap.shape)
    shape.insert(axis, n)
    return ap.unsqueeze(axis).broadcast_to(shape)


def program(nc, ins, out):
    ctx = ExitStack()
    with ctx:
        sem = lambda name: ctx.enter_context(nc.semaphore(name))
        S, A, V, G, E = Engine(sem("sp")), Act(sem("act")), Vec(sem("dve")), Vec(sem("pool")), Engine(sem("pe"))
        s_raw = [sem(f"raw{i}") for i in range(RAW)]
        s_par, s_small, s_head, s_c1, s_c2, s_pos, s_small2 = (sem(n) for n in ("ldpar", "ldsmall", "ldhead", "ldc1", "ldc2", "ldpos", "ldsmall2"))
        s_lev = [sem(f"ldlev{i}") for i in range(DEPTH)]
        s_x4 = [sem(f"ldx{i}") for i in range(4)]
        s_out = sem("out")

        at = [16640]

        def sb(name, shape, dt=F32, offset=None):
            n = 4
            for x in shape[1:]:
                n *= x
            if offset is None:
                offset = at[0]
                at[0] += (n + 31) // 32 * 32
            return nc.alloc_sbuf_tensor_at(name, shape, dt, offset=offset)

        xT = sb("xT", [P, 8, T])
        hh = sb("hh", [P, 8, T], F32R)
        hl = sb("hl", [P, 8, T], F32R)
        raw = sb("raw", [P, RAW, 1024])
        whi = sb("whi", [P, RING, 1024], F32R)
        wlo = sb("wlo", [P, RING, 1024], F32R)
        cst = sb("cst", [P, N_CONST])
        par = sb("par", [P, N_PAR])
        small = sb("small", [P, N_SMALL])
        RSB = sb("RSB", [P, T])
        RST = sb("RST", [P, 2])
        SW = sb("SW", [P, 8, 16], F32R)
        region = at[0]
        nslots = (nc.sbuf_usable_end - region) // 4096
        assert nslots >= 30, nslots

        area = nc.alloc_sbuf_tensor_at("area", [P, 30 * 1024], F32, offset=region)

        def slot(name, i, n=1, dt=F32, shape=None):
            if dt == F32R:
                return sb(name, shape, dt, offset=region + 4096 * i)
            v = area[:, 1024 * i:1024 * (i + n)]
            return v.bitcast(dt) if dt != F32 else v

        banks = [Bank(ctx.enter_context(nc.psum_tensor(f"bank{i}", [P, 512], F32))) for i in range(8)]

        def C(name, table=None):
            o, w = (table or consts[0])[name]
            return cst[:, o:o + w]

        def Q(name, layer):
            first = layer < DEPTH
            o, w = (PAR1 if first else PAR2)[name]
            o += layer * N_PAR1 if first else DEPTH * N_PAR1 + (layer - DEPTH) * N_PAR2
            return par[:, o:o + w]

        consts = [CONST1]

        def load(dst, src, s, *after):
            S.wait(*after)
            S.queue.append(lambda e: e.dma_start(dst, src).then_inc(s, 16))
            return (s, 16)

        order = []
        hi_done, lo_done, used = {}, {}, {}
        staged = [0]
        helped = [0]
        fetched = [0]

        def fetch():
            i = fetched[0]
            if i >= NCHUNK:
                return
            fetched[0] += 1
            if i >= RAW:
                S.wait(hi_done[i - RAW], lo_done[i - RAW])
            r = i % RAW
            S.queue.append(lambda e: e.dma_start(raw[:, r, :], ins["weights"][i]).then_inc(s_raw[r], 16))

        def stage():
            i = staged[0]
            if i >= NCHUNK:
                return
            staged[0] += 1
            r, h = i % RAW, i % RING
            landed = (s_raw[r], 16 * (i // RAW + 1))
            free = [used[i - RING]] if i >= RING else []
            hi_done[i] = A.copy(whi[:, h, :], raw[:, r, :], landed, *free)
            e = G if helped[0] and i % helped[0] == 0 else V
            lo_done[i] = e.tt(wlo[:, h, :], raw[:, r, :], whi[:, h, :].bitcast(F32), OP.subtract, hi_done[i], landed, *free)
            fetch()

        def chunk(what, ahead=RING):
            i = len(order)
            order.append(what)
            while staged[0] < min(i + ahead, NCHUNK):
                stage()
            E.wait(lo_done[i])
            return i, whi[:, i % RING, :], wlo[:, i % RING, :]

        def mm(ps, l, r, first, last, *after, skip=False, done=False):
            fn = lambda e: e.matmul(ps, l, r, start=first, stop=last, skip_group_check=skip)
            return E.do(fn, *after) if done else E.quiet(fn, *after)

        def mm3(ps, w, x, first, last, wstat=True, skip=False, done=False):
            (wh, wl), (xh, xl) = w, x
            tok = None
            for n, (a, b) in enumerate(((wh, xh), (wh, xl), (wl, xh))):
                if not wstat:
                    a, b = b, a
                tok = mm(ps, a, b, first and n == 0, last and n == 2, skip=skip, done=done and n == 2)
            return tok

        ring = [0, [4, 5, 6, 7]]

        def next_bank():
            b = banks[ring[1][ring[0] % len(ring[1])]]
            ring[0] += 1
            return b

        def project(what, ntile, xs, nk, xtok, evac, hook=None, lead=False):
            at_, cur = 0, None
            m0 = 0
            if hook or lead:
                assert nk == 8
                b = next_bank()
                lead = [chunk((*what, 0)), chunk((*what, 1), RING - 1)]
                E.wait(*b.free)
                for j in range(4):
                    E.wait(*xtok[j])
                    for m, (i, wh, wl) in enumerate(lead):
                        for k in (2 * j, 2 * j + 1):
                            tok = mm3(b.t[:, m * T:(m + 1) * T], (wh[:, 128 * k:128 * k + 128], wl[:, 128 * k:128 * k + 128]),
                                      (xs[0][:, k, :], xs[1][:, k, :]), (m, k) == (0, 0), k == nk - 1, skip=True, done=k == nk - 1)
                        used[i] = tok
                m0, at_ = 2, 16
                if hook:
                    hook()
                evac(0, 2, b, tok)
            for m0 in range(m0, ntile, 2):
                b = next_bank()
                n = min(2, ntile - m0)
                for m in range(m0, m0 + n):
                    for k in range(nk):
                        if at_ % 8 == 0:
                            if at_:
                                yield
                            cur = chunk((*what, at_ // 8))
                        if m == m0 and k == 0:
                            E.wait(*b.free)
                        E.wait(*xtok[k // 2])
                        i, wh, wl = cur
                        c = at_ % 8 * 128
                        at_ += 1
                        tok = mm3(b.t[:, (m - m0) * T:(m - m0 + 1) * T], (wh[:, c:c + 128], wl[:, c:c + 128]),
                                  (xs[0][:, k, :], xs[1][:, k, :]), k == 0, k == nk - 1,
                                  done=(at_ % 8 == 0 or k == nk - 1))
                        if at_ % 8 == 0:
                            used[i] = tok
                evac(m0, n, b, tok)
            yield

        def by_token(what, xtok, evac):
            for x in xtok:
                E.wait(*x)
            bb = [next_bank(), next_bank()]
            for c in range(4):
                i, wh, wl = chunk((*what, c))
                if c == 0:
                    for b in bb:
                        E.wait(*b.free)
                for j in range(2):
                    k = 2 * c + j
                    w = (wh[:, 512 * j:512 * j + 512], wl[:, 512 * j:512 * j + 512])
                    for s in range(2):
                        x = (hh[:, k, 128 * s:128 * s + 128], hl[:, k, 128 * s:128 * s + 128])
                        tok = mm3(bb[s].t[:, :], w, x, k == 0, k == 7, wstat=False, done=(j == 1 and s == 1))
                used[i] = tok
                if c < 3:
                    yield
            for s in range(2):
                evac(s, bb[s], tok)
            yield

        def down(what, nk, ah, al, ready, evac, settle):
            bb = banks[0:4]
            for b in bb:
                E.wait(*b.free)

            def term(k, m, w, done):
                wh, wl = w
                return mm3(bb[m // 2].t[:, (m % 2) * T:(m % 2 + 1) * T], (wh[:, 128 * m:128 * m + 128], wl[:, 128 * m:128 * m + 128]),
                           (ah[:, k, :], al[:, k, :]), k == 0 and m % 2 == 0, k == nk - 1, skip=True, done=done)

            for k in range(nk - TAIL):
                E.wait(*ready[k])
                i, wh, wl = chunk((*what, k))
                for m in range(8):
                    tok = term(k, m, (wh, wl), m == 7)
                used[i] = tok
                if k < len(settle):
                    settle[k]()
            tail = []
            for k in range(nk - TAIL, nk):
                E.wait(*ready[k])
                tail.append((k, *chunk((*what, k), nk - TAIL + RING - k)))
            for j, b in enumerate(bb):
                for k, i, wh, wl in tail:
                    for m in (2 * j, 2 * j + 1):
                        tok = term(k, m, (wh, wl), m % 2 == 1)
                    used[i] = tok
                evac(2 * j, 2, b, tok)

        def run(gen, fill=None):
            for n in gen:
                for _ in range(n or 1 if fill is not None else 0):
                    if next(fill, BLOCKED) == BLOCKED:
                        break

        def chain(*gens):
            for g in gens:
                yield from g

        def rstd_of(bank, n, scale, eps, out_ap, *after):
            a = A.act(out_ap, bank.t[:, 0:n], AF.Ln, *after, scale=scale, bias=eps)
            r = A.act(out_ap, out_ap, AF.Exp, a, scale=-0.5)
            bank.free = (a,)
            return r

        def split(h, l, src, ready):
            a = A.copy(h, src, *ready)
            b = V.tt(l, src, h.bitcast(F32), OP.subtract, a)
            return (a, b)

        pair = lambda t, j: t[:, 512 * j:512 * j + 512]
        x_ = lambda j: xT[:, 2 * j:2 * j + 2, :].rearrange("p k t -> p (k t)")

        class Stats:

            def __init__(self, bank):
                self.bank, self.late, self.n = bank, [], 0

            def square(self, j, src, *ready):
                s = A.act(pair(SQ2, j), src, AF.Square, *ready)
                self.late.append((j, s))
                return s

            def flush(self):
                tok = None
                if self.late and self.n == 0:
                    E.wait(*self.bank.free)
                while self.late:
                    j, s = self.late.pop(0)
                    for k in range(2):
                        self.n += 1
                        tok = mm(self.bank.t[:, 0:T], C("ones"), pair(SQ2, j)[:, k * T:(k + 1) * T], self.n == 1, self.n == 8, s, done=k == 1)
                return tok

            def rstd(self):
                t = self.flush()
                return rstd_of(self.bank, T, 1.0 / D, C("eps6"), RS[:, 0:T], t)

        class Norm:

            def __init__(self, gain, bank, by_token=False):
                self.gain, self.bank, self.by_token = gain, bank, by_token
                self.toks, self.sq, self.r, self.rt = [], [], None, None
                self.before = (V.done(), G.done())

            def high(self, j, *ready):
                self.hi = [A.act(hh[:, k, :], xT[:, k, :], AF.Copy, *ready, scale=self.gain[:, k:k + 1]) for k in (2 * j, 2 * j + 1)]

            def low(self, j):
                for k, hi in zip((2 * j, 2 * j + 1), self.hi):
                    lo = V.stt(hl[:, k, :], xT[:, k, :], self.gain[:, k:k + 1], hh[:, k, :].bitcast(F32), OP.mult, OP.subtract, hi)
                self.toks.append((hi, lo))

            def parts(self, j, *ready):
                self.high(j, *ready)
                self.low(j)

            def square(self, j, *ready):
                s = A.act(pair(SQ2, j), x_(j), AF.Square, *ready)
                if j % 2:
                    s = G.tt(pair(SQ2, j), pair(SQ2, j), pair(SQ2, j - 1), OP.add, s)
                    self.sq.append((j, s))

            def late_pair(self, j, *ready):
                if j:
                    self.low(j - 1)
                self.high(j, *ready)
                self.square(j, *ready)
                if j == 3:
                    self.low(3)

            def finish(self):
                E.wait(*self.bank.free)
                for n, (j, s) in enumerate(self.sq):
                    for k in range(2):
                        t = mm(self.bank.t[:, 0:T], C("ones"), pair(SQ2, j)[:, k * T:(k + 1) * T], (n, k) == (0, 0), (n, k) == (1, 1), s, done=(n, k) == (1, 1))
                self.r = rstd_of(self.bank, T, 1.0 / D, C("eps6"), RSB[:, :], t, *self.before)
                if self.by_token:
                    w = V.tt(v3(SQ2[:, 0:T], 128), v3(RSB, 128), wide(C("eye"), 1, 2), OP.mult, self.r)
                    self.rt = V.red(RST[:, :], v3(SQ2[:, 0:T], 128), OP.add, w)

        def v3(t, n=T):
            return t[:, :].rearrange("p (m t) -> p m t", t=n)

        class PostNorm:

            def __init__(self, gain, bank):
                self.gain, self.st, self.toks = gain, Stats(bank), []

            def evac(self, m0, n, b, tok):
                j = m0 // 2
                self.st.flush()
                self.st.square(j, b.t[:, :], tok)
                for m in (m0, m0 + 1):
                    v = A.act(MG[:, m * T:(m + 1) * T], b.t[:, (m - m0) * T:(m - m0 + 1) * T], AF.Copy, tok, scale=self.gain[:, m:m + 1])
                b.free = (v,)
                self.toks.append(v)

            def finish(self, norm):
                r = self.st.rstd()

                def times(e, j):
                    return e.tt(v3(pair(MG, j)), v3(pair(MG, j)), wide(RS[:, 0:T], 1, 2), OP.mult, r, self.toks[j])

                w = [times(G if j % 2 else V, j) if j != 2 else None for j in range(4)]
                done = []
                for j in range(4):
                    if j == 2:
                        w[2] = times(V, 2)
                    if j > 1:
                        norm.low(j - 1)
                    done.append(V.tt(x_(j), x_(j), pair(MG, j), OP.add, w[j]))
                    if j == 1:
                        norm.low(0)
                    norm.high(j, done[j])
                norm.low(3)
                for j in range(4):
                    norm.square(j, done[j])
                return norm

        class Residual:

            def __init__(self, norm):
                self.norm = norm

            def evac(self, m0, n, b, tok):
                t = V.tt(x_(m0 // 2), x_(m0 // 2), b.t[:, :], OP.add, tok)
                b.free = (t,)
                self.norm.late_pair(m0 // 2, t)

        class Last:

            def __init__(self, bank):
                self.st = Stats(bank)

            def late_pair(self, j, *ready):
                self.st.flush()
                self.st.square(j, x_(j), *ready)

        def everything():
            return tuple(x.done() for x in (A, V, G, E))

        U = slot("U", 0, 3)
        KT, KB, VB = slot("KT", 0), slot("KB", 1), slot("VB", 2)
        Aq, Ak, Av = slot("Aq", 3), slot("Ak", 4), slot("Av", 5)
        QKV = slot("QKV", 3, 3)
        QK = slot("QK", 3, 2)
        SQ = slot("SQ", 6, 2)
        T0, EG, DT, M, MT, AT = (slot(n, 6 + i) for i, n in enumerate(("T0", "EG", "DT", "M", "MT", "AT")))
        X, Y, LT = slot("X", 12), slot("Y", 13), slot("LT", 14)
        SV = slot("SV", 15)
        SM = slot("SM", 16)
        LEV = SM[:, 256:1024]
        Z = slot("Z", 17)
        RQ, RK, RV, RG, PU = (slot(n, 18 + i) for i, n in enumerate(("RQ", "RK", "RV", "RG", "PU")))
        RQK = slot("RQK", 18, 2)
        GT = slot("GT", 23, 2)
        XY = slot("XY", 12, 2)
        RF = slot("RF", 15)[:, 0:512]
        YY = slot("YY", 25, 2)
        OD = slot("OD", 27)
        parts_at = lambda name, i, j: (slot(name + "H", i, dt=F32R, shape=[P, 4, T]), slot(name + "L", j, dt=F32R, shape=[P, 4, T]), [])
        BR0, BR1, BR2 = parts_at("B0", 28, 29), parts_at("B1", 11, 14), parts_at("B2", 11, 13)
        R0, R1 = slot("R0", 0, 2), slot("R1", 2, 2)
        KZ, ST, RR, OR, SR, O2 = slot("KZ", 4), slot("ST", 5), slot("RR", 6, 2), slot("OR", 8), slot("SR", 9), slot("O2", 10)
        PA, PB, PC = slot("PA", 25), slot("PB", 26), slot("PC", 22)
        FH, FL = slot("FH", 0, dt=F32R, shape=[P, 32, T]), slot("FL", 8, dt=F32R, shape=[P, 32, T])
        FT = slot("FT", 25, 2)
        COSR, SINR = RF[:, 0:T], RF[:, T:2 * T]
        SQ2, MG, RS = slot("SQ2", 18, 2), slot("MG", 20, 2), slot("RS", 22)

        def times_rms(dst, b, n, norm, tok, *after):
            t = V.tt(v3(dst), b.t[:, 0:n * T].rearrange("p (m t) -> p m t", t=T), wide(RSB[:, :], 1, n), OP.mult, tok, norm.r, *after)
            b.free = (t,)
            return t

        def copy_to(dst, toks, norm=None):
            def evac(m0, n, b, tok):
                if norm:
                    t = times_rms(dst[:, m0 * T:(m0 + n) * T], b, n, norm, tok)
                else:
                    t = A.copy(dst[:, m0 * T:(m0 + n) * T], b.t[:, 0:n * T], tok)
                    b.free = (t,)
                toks.append(t)
            return evac

        class Gate:

            def __init__(self, dst, norm, before=None, nbefore=0):
                self.dst, self.norm, self.before, self.nbefore = dst, norm, before, nbefore
                self.late, self.toks = [], []

            def finish(self):
                if not self.toks:
                    assert len(self.late) == 4
                    for j in (0, 2):
                        d = self.dst[:, 512 * j:512 * j + 1024]
                        self.toks += [A.act(d, d, AF.Sigmoid, self.late[j], self.late[j + 1])] * 2

            def evac(self, m0, n, b, tok):
                if self.before is not None:
                    assert len(self.before) >= self.nbefore
                d = self.dst[:, m0 * T:(m0 + n) * T]
                t = times_rms(d, b, n, self.norm, tok, *(self.before or [])[-1:])
                self.late.append(t)

        class Branch:

            def __init__(self, where, what, src, ready, nready, nk, gate, first, ydone, *after):
                self.bh, self.bl, self.bfree = where
                self.what, self.src, self.ready, self.nready, self.nk = what, src, ready, nready, nk
                self.gate, self.first, self.ydone, self.after = gate, first, ydone, after
                self.parts, self.over = None, False

            def prepare(self):
                if self.parts is None and len(self.ready) >= self.nready:
                    nk = self.nk
                    self.parts = split(self.bh[:, 0:nk, :].rearrange("p k t -> p (k t)"), self.bl[:, 0:nk, :].rearrange("p k t -> p (k t)"),
                                       self.src, (*self.ready, *self.after, *self.bfree))

            def evac(self, m0, n, b, tok):
                c = slice(m0 * T, (m0 + n) * T)
                gate = self.gate.dst
                g = self.gate.toks[m0 // 2]
                if self.first:
                    t = V.tt(YY[:, c], b.t[:, 0:n * T], gate[:, c], OP.mult, tok, g, *self.after)
                    b.free = (t,)
                else:
                    u = V.tt(gate[:, c], b.t[:, 0:n * T], gate[:, c], OP.mult, tok, g)
                    b.free = (u,)
                    t = (G if m0 < 6 else V).tt(YY[:, c], YY[:, c], gate[:, c], OP.add, u, *self.ydone[-4:-3])
                self.ydone.append(t)
                self.bfree[:] = [tok]

            def steps(self, evac=None):
                while self.parts is None:
                    self.prepare()
                    if self.parts is None:
                        yield BLOCKED
                self.gate.finish()
                yield from project(self.what, 8, (self.bh, self.bl), self.nk, [self.parts] * 4, evac or self.evac)
                self.over = True

        class Merged:

            def __init__(self, branch):
                self.branch, self.toks, self.late, self.early = branch, [None] * 4, [], []

            def low(self):
                while self.late:
                    j, a = self.late.pop()
                    self.toks[j] = (a, V.tt(FL[:, 2 * j:2 * j + 2, :], v3(pair(YY, j)), FH[:, 2 * j:2 * j + 2, :].bitcast(F32), OP.subtract, a))

            def high(self):
                while self.early:
                    j, t = self.early.pop()
                    self.late.append((j, A.copy(FH[:, 2 * j:2 * j + 2, :], v3(pair(YY, j)), t)))

            def evac(self, m0, n, b, tok):
                self.high()
                self.branch.evac(m0, n, b, tok)
                self.low()
                self.early.append((m0 // 2, self.branch.ydone[-1]))

            def flush(self):
                self.high()
                self.low()

        def one(fn):
            fn()
            yield from ()

        def before_end(gen, k, fn):
            for n, x in enumerate(gen):
                yield x
                if n == k:
                    fn()

        def delta_rule(l, squared, qkv, abtok, middle, zt, out):
            B0, B1, B2, B3 = banks[0:4]
            bk = lambda b: b.t[:, :]
            a_, be, g_, G_, eg, kx = (SM[:, 16 * i:16 * i + 8] for i in range(6))
            u1, u2 = SM[:, 128:136], SM[:, 144:152]
            AB = SM[:, 192:208].rearrange("p (s c) -> p c s", s=2)
            hs = lambda ap: ap.rearrange("p (h s) -> p h s", s=2)
            e1 = A.act(hs(be), AB[:, 0:4, :], AF.Exp, *abtok, scale=-1.0)
            w = V.ts(be, be, 1.0, None, OP.add, None, e1)
            bdone = V.recip(be, be, w)
            w = V.tt(hs(a_), AB[:, 4:8, :], hs(Q("dtb", l)), OP.add, *abtok)
            w1 = V.ts(u1, a_, -1.0, None, OP.mult, None, w)
            w1 = V.tt(u1, u1, a_, OP.max, w1)
            e1 = A.act(u1, u1, AF.Exp, w1, scale=-1.0)
            e1 = A.act(u1, u1, AF.Ln, e1, bias=C("one"))
            w = V.stt(a_, a_, 0.0, u1, OP.max, OP.add, e1)
            e2 = A.act(u2, Q("alog", l), AF.Exp, abtok[0])
            gd = V.stt(g_, a_, -1.0, u2, OP.mult, OP.mult, w, e2)
            yield
            rg = V.tt(v3(X, 128), wide(C("upper"), 1, 8), wide(g_, 2, 128), OP.mult, gd)
            for j in range(4):
                E.wait(*squared, *banks[j].free)
                t = mm(bk(banks[j]), C("ones"), SQ[:, 512 * j:512 * j + 512], True, True, done=True)
                r = A.act(SQ[:, 512 * j:512 * j + 512], bk(banks[j]), AF.Ln, t, bias=C("eps6"))
                banks[j].free = (r,)
            yield 2
            yield
            r = A.act(SQ[:, :], SQ[:, :], AF.Exp, r, scale=-0.5)
            n1 = V.stt(Aq[:, :], Aq[:, :], 128.0 ** -0.5, SQ[:, 0:1024], OP.mult, OP.mult, r)
            n2 = V.tt(Ak[:, :], Ak[:, :], SQ[:, 1024:2048], OP.mult, r)
            E.wait(rg)
            for j in range(2):
                E.wait(*banks[j].free)
                t = mm(bk(banks[j]), C("ones"), X[:, 512 * j:512 * j + 512], True, True, done=True)
            E.wait(*B2.free)
            mm(B2.t[:, 0:8], C("upper"), g_, True, True)
            t2 = mm(B2.t[:, 8:16], C("chunk"), g_, True, True, done=True)
            d1 = V.copy(SM[:, 48:64], B2.t[:, 0:16], t2)
            B2.free = (d1,)
            G_, GL = SM[:, 48:56], SM[:, 56:64]
            w = V.tt(kx, GL, G_, OP.subtract, d1)
            e3 = A.act(eg, G_, AF.Exp, d1)
            e4 = A.act(kx, kx, AF.Exp, w)
            w3 = V.tt(eg, eg, be, OP.mult, e3, bdone)
            yield
            for j in range(2):
                c = slice(512 * j, 512 * j + 512)
                a = A.act(EG[:, c], bk(banks[j]), AF.Exp, t, n1, n2)
                b = V.tt(DT[:, c].rearrange("p (b t) -> p b t", t=128), bk(banks[j]).rearrange("p (b t) -> p b t", t=128),
                         wide(G_[:, 4 * j:4 * j + 4], 2, 128), OP.subtract, a, d1)
                banks[j].free = (b,)
            b = V.tt(v3(DT, 128), v3(DT, 128), wide(C("upper"), 1, 8), OP.mult, b)
            b = A.act(DT[:, :], DT[:, :], AF.Exp, b)
            dt = V.tt(v3(DT, 128), v3(DT, 128), wide(C("upper"), 1, 8), OP.mult, b)
            yield 3
            kb3 = lambda t, b: t[:, 128 * b:128 * b + 128]
            E.wait(n1, n2)
            for j in range(2):
                E.wait(*banks[j].free)
                for b in range(4 * j, 4 * j + 4):
                    t = mm(banks[j].t[:, 128 * (b % 4):128 * (b % 4) + 128], kb3(Ak, b), kb3(Ak, b), True, True, done=b % 4 == 3)
            E.wait(dt)
            for j in range(2):
                E.wait(*banks[2 + j].free)
                for b in range(4 * j, 4 * j + 4):
                    fn = lambda e, o=banks[2 + j].t[:, 128 * (b % 4):128 * (b % 4) + 128], i=kb3(DT, b): e.transpose(o, i, C("eye", CONST1))
                    if b % 4 == 3:
                        tt_ = E.do(fn)
                    else:
                        E.quiet(fn)
            for j in range(2):
                c = slice(512 * j, 512 * j + 512)
                w = V.tt(M[:, c].rearrange("p (b t) -> p b t", t=128), bk(banks[j]).rearrange("p (b t) -> p b t", t=128),
                         wide(be[:, 4 * j:4 * j + 4], 2, 128), OP.mult, t, bdone)
                banks[j].free = (w,)
                w = V.tt(M[:, c], M[:, c], bk(banks[2 + j]), OP.mult, w, tt_)
                banks[2 + j].free = (w,)
            md = w
            yield
            def transposed(src, bb, *after):
                E.wait(*after)
                for j in range(2):
                    E.wait(*bb[j].free)
                    for b in range(4 * j, 4 * j + 4):
                        fn = lambda e, o=bb[j].t[:, 128 * (b % 4):128 * (b % 4) + 128], i=kb3(src, b): e.transpose(o, i, C("eye", CONST1))
                        if b % 4 == 3:
                            tok = E.do(fn)
                        else:
                            E.quiet(fn)
                return tok

            def scaled(dst, bb, by, tok, *after):
                for j in range(2):
                    w = V.tt(dst[:, 512 * j:512 * j + 512].rearrange("p (b t) -> p b t", t=128),
                             bk(bb[j]).rearrange("p (b t) -> p b t", t=128), wide(by[:, 4 * j:4 * j + 4], 2, 128), OP.mult, tok, *after)
                    bb[j].free = (w,)
                return w

            yield 2
            t = transposed(M, (B0, B1), md)
            for j in range(2):
                mt = A.copy(MT[:, 512 * j:512 * j + 512], bk(banks[j]), t)
                banks[j].free = (mt,)
            lev = lambda s, tr=False: (C("levT") if tr else LEV)[:, 128 * s:128 * s + 128]
            w = V.tt(v3(X, 128), v3(M, 128), wide(lev(0), 1, 8), OP.mult, md)
            xd = V.stt(v3(X, 128), v3(X, 128), -1.0, wide(C("eye"), 1, 8), OP.mult, OP.add, w)
            w = V.tt(v3(Y, 128), v3(MT, 128), wide(lev(0, True), 1, 8), OP.mult, mt)
            yd = V.stt(v3(Y, 128), v3(Y, 128), -1.0, wide(C("eye"), 1, 8), OP.mult, OP.add, w)
            lt = G.tt(v3(LT, 128), v3(MT, 128), wide(lev(1, True), 1, 8), OP.mult, mt)
            yield
            for j in range(2):
                E.wait(*banks[2 + j].free)
                for b in range(4 * j, 4 * j + 4):
                    t = mm(banks[2 + j].t[:, 128 * (b % 4):128 * (b % 4) + 128], kb3(Ak, b), kb3(Aq, b), True, True, done=b % 4 == 3)
            for j in range(2):
                c = slice(512 * j, 512 * j + 512)
                atd = V.tt(AT[:, c], DT[:, c], bk(banks[2 + j]), OP.mult, t)
                banks[2 + j].free = (atd,)
            qd = G.tt(Aq[:, :], Aq[:, :], EG[:, :], OP.mult, t, a)
            yield
            side = [0]

            def extra():
                if side[0] == 0:
                    tk = transposed(Ak, (B2, B3))
                    side.append(scaled(KT, (B2, B3), kx, tk, e4))
                    side.append(scaled(KB, (B2, B3), eg, tk, w3))
                elif side[0] == 2:
                    tk = transposed(Av, (B2, B3), *qkv)
                    side.append(scaled(VB, (B2, B3), be, tk, bdone))
                side[0] += 1

            for s_ in range(1, 6):
                E.wait(lt, xd, yd)
                for j in range(2):
                    E.wait(*banks[j].free)
                    for b in range(4 * j, 4 * j + 4):
                        t = mm(banks[j].t[:, 128 * (b % 4):128 * (b % 4) + 128], kb3(LT, b), kb3(X, b), True, True, done=b % 4 == 3)
                if s_ > 1:
                    t1 = transposed(X, (B2, B3), xd)
                for j in range(2):
                    w = A.copy(T0[:, 512 * j:512 * j + 512], bk(banks[j]), t)
                    banks[j].free = (w,)
                if s_ > 1:
                    for j in range(2):
                        w = yd = A.copy(Y[:, 512 * j:512 * j + 512], bk(banks[2 + j]), t1)
                        banks[2 + j].free = (w,)
                if s_ < 5:
                    lt = G.tt(v3(LT, 128), v3(MT, 128), wide(lev(s_ + 1, True), 1, 8), OP.mult, t)
                yield
                E.wait(w)
                fixed, moved, o = (Y, T0, 0) if s_ < 5 else (T0, Y, 2)
                for j in range(2):
                    E.wait(*banks[o + j].free)
                    for b in range(4 * j, 4 * j + 4):
                        t = mm(banks[o + j].t[:, 128 * (b % 4):128 * (b % 4) + 128], kb3(fixed, b), kb3(moved, b), True, True, done=b % 4 == 3)
                for j in range(2):
                    c = slice(512 * j, 512 * j + 512)
                    if s_ < 5:
                        w = xd = V.tt(X[:, c], X[:, c], bk(banks[j]), OP.subtract, t)
                    else:
                        w = yd = V.tt(Y[:, c], Y[:, c], bk(banks[2 + j]), OP.subtract, t)
                    banks[o + j].free = (w,)
                yield
                extra()
            ktd, kbd, vbd = side[1:4]
            E.wait(kbd, vbd, yd)
            for j in range(2):
                E.wait(*banks[j].free)
                for b in range(4 * j, 4 * j + 4):
                    t = mm(banks[j].t[:, 128 * (b % 4):128 * (b % 4) + 128], kb3(KB, b), kb3(Y, b), True, True, done=b % 4 == 3)
            for j in range(2):
                E.wait(*banks[2 + j].free)
                for b in range(4 * j, 4 * j + 4):
                    t2 = mm(banks[2 + j].t[:, 128 * (b % 4):128 * (b % 4) + 128], kb3(Y, b), kb3(VB, b), True, True, done=b % 4 == 3)
            for j in range(2):
                c = slice(512 * j, 512 * j + 512)
                wt = A.copy(M[:, c], bk(banks[j]), t)
                banks[j].free = (wt,)
                ud = A.copy(MT[:, c], bk(banks[2 + j]), t2)
                banks[2 + j].free = (ud,)
            yield
            St, VN = SV[:, 0:512], SV[:, 512:1024]
            hv = lambda ap: ap.rearrange("p (h t) -> p h t", h=4)
            sd = None
            OB = (B2, B3)
            for n in range(4):
                half, q = n // 2, n % 2
                r = slice(64 * q, 64 * q + 64)
                u_c = hv(MT[:, :])[r, :, 128 * half:128 * half + 128]
                if n == 0:
                    vn = V.copy(hv(VN)[r], u_c, ud)
                else:
                    E.wait(sd, wt, *B0.free)
                    for h in range(4):
                        c0 = 256 * h + 128 * half + 64 * q
                        t = mm(B0.t[r, 128 * h:128 * h + 128], M[:, c0:c0 + 64], St[:, 128 * h:128 * h + 128], True, True, done=h == 3)
                    vn = V.stt(hv(VN)[r], hv(B0.t[r, :]), -1.0, u_c, OP.mult, OP.add, t, ud)
                    B0.free = (vn,)
                yield
                E.wait(vn, ktd, *B1.free)
                for h in range(4):
                    b = 2 * h + half
                    t = mm(B1.t[:, 128 * h:128 * h + 128], KT[r, 128 * b:128 * b + 128], hv(VN)[r, h, :], True, True, done=h == 3)
                if n == 1:
                    middle()
                E.wait(atd, qd, *(OB[0].free + OB[1].free if n == 0 else ()))
                for h in range(4):
                    b = 2 * h + half
                    o = OB[h // 2].t[:, 256 * (h % 2) + 64 * n:256 * (h % 2) + 64 * n + 64]
                    if n:
                        mm(o, St[:, 128 * h:128 * h + 128], Aq[:, 256 * h + 64 * n:256 * h + 64 * n + 64], True, False)
                    to = mm(o, hv(VN)[r, h, :], AT[r, 128 * b + 64 * q:128 * b + 64 * q + 64], n == 0, True, done=h == 3)
                if n < 3:
                    dl = wide(v3(EG)[:, :, 64 * n + 63], 2, 128)
                    if n == 0:
                        sd = V.copy(St, bk(B1), t)
                    else:
                        sd = V.tt(hv(St), hv(St), dl, OP.mult, t, to)
                        sd = V.tt(St, St, bk(B1), OP.add, sd)
                    B1.free = (sd,)
                yield
            for j in range(2):
                o = A.copy(OD[:, 512 * j:512 * j + 512], bk(OB[j]), to)
                OB[j].free = (o,)
            s = A.act(T0[:, :], OD[:, :], AF.Square, o)
            yield
            E.wait(s)
            for j in range(2):
                E.wait(*banks[j].free)
                t = mm(bk(banks[j]), C("ones"), T0[:, 512 * j:512 * j + 512], True, True, done=True)
                a = A.act(EG[:, 512 * j:512 * j + 512], bk(banks[j]), AF.Ln, t, to, sd, scale=1.0 / 128, bias=C("eps6"))
                banks[j].free = (a,)
            a = A.act(EG[:, :], EG[:, :], AF.Exp, a, scale=-0.5)
            yield 2
            w = V.stt(OD[:, :], OD[:, :], Q("dnout", l), EG[:, :], OP.mult, OP.mult, a)
            w = V.tt(OD[:, :], OD[:, :], Z[:, :], OP.mult, w, *zt)
            out.append(w)

        def pooling(l, pu, out, *after):
            PU3, A3, B3_, C3 = v3(PU), v3(PA), v3(PB), v3(PC)
            w = G.copy(A3, PU3, *pu, *after)
            yield
            w = G.tt(A3[:, :, 1:T], PU3[:, :, 1:T], PU3[:, :, 0:T - 1], OP.add, w)
            yield
            w = G.copy(B3_, A3, w)
            w = G.tt(B3_[:, 1:4, 2:T], A3[:, 1:4, 2:T], A3[:, 1:4, 0:T - 2], OP.add, w)
            yield
            w = G.copy(A3[:, 2:4, :], B3_[:, 2:4, :], w)
            w = G.tt(A3[:, 2:4, 4:T], B3_[:, 2:4, 4:T], B3_[:, 2:4, 0:T - 4], OP.add, w)
            yield
            w = G.copy(B3_[:, 2:4, :], A3[:, 2:4, :], w)
            w = G.tt(B3_[:, 3:4, 8:T], A3[:, 3:4, 8:T], A3[:, 3:4, 0:T - 8], OP.add, w)
            yield
            w = G.tt(B3_[:, :, 0:16], B3_[:, :, 0:16], v3(C("cnt"), 16), OP.mult, w)
            w = G.tt(B3_[:, :, 16:T], B3_[:, :, 16:T], wide(C("cntw"), 2, T - 16), OP.mult, w)
            yield
            w = G.tt(PB[:, :], PB[:, :], PU[:, :], OP.subtract, w)
            for _ in range(4):
                yield
            E.wait(w)
            for j in range(2):
                b = next_bank()
                E.wait(*b.free)
                for g in (2 * j, 2 * j + 1):
                    c = 64 + 128 * g
                    t = mm(b.t[:, T * (g % 2):T * (g % 2) + T], small[:, c:c + 128], PB[:, T * g:T * g + T], True, True, done=True)
                for g in (2 * j, 2 * j + 1):
                    o = A.act(PC[:, T * g:T * g + T], b.t[:, T * (g % 2):T * (g % 2) + T], AF.Copy, t, w, scale=Q("pscale", l)[:, g:g + 1])
                b.free = (o,)
            out.append(o)
            yield

        def retention(l, norm, rqk, rv, zt, out):
            start = everything()
            cosr = V.tt(COSR, C("cos"), RSB[:, :], OP.mult, norm.r, *start)
            sinr = V.tt(SINR, C("sin"), RSB[:, :], OP.mult, norm.r)
            E.wait(*rqk)
            w0 = G.tt(v3(R0), v3(RQK), wide(COSR, 1, 8), OP.mult, *rqk, cosr, *start)
            for j in range(4):
                b = banks[j]
                E.wait(*b.free)
                t = mm(b.t[:, :], C("rot"), RQK[:, 512 * j:512 * j + 512], True, True, done=True)
                w = V.tt(R1[:, 512 * j:512 * j + 512].rearrange("p (m t) -> p m t", t=T), b.t[:, :].rearrange("p (m t) -> p m t", t=T),
                         wide(SINR, 1, 2), OP.mult, t, sinr, *start)
                b.free = (w,)
            yield 2
            rot = V.tt(RQK[:, :], R0[:, :], R1[:, :], OP.add, w, w0, t)
            yield 2
            kb3 = lambda t, b: t[:, 128 * b:128 * b + 128]
            E.wait(rot)
            for j in range(2):
                E.wait(*banks[j].free)
                for b in range(4 * j, 4 * j + 4):
                    fn = lambda e, o=banks[j].t[:, 128 * (b % 4):128 * (b % 4) + 128], i=kb3(RK, b): e.transpose(o, i, C("eye", CONST1))
                    tk = E.do(fn) if b % 4 == 3 else E.quiet(fn)
            for j in range(2):
                for hh_ in range(2):
                    h = 2 * j + hh_
                    kz = A.act(KZ[:, 256 * h:256 * h + 256], banks[j].t[:, 256 * hh_:256 * hh_ + 256], AF.Copy, tk, *start, scale=C("zeta")[:, h:h + 1])
                banks[j].free = (kz,)
            for j in range(2):
                E.wait(*banks[2 + j].free)
                for b in range(4 * j, 4 * j + 4):
                    t = mm(banks[2 + j].t[:, 128 * (b % 4):128 * (b % 4) + 128], kb3(RK, b), kb3(RQ, b), True, True, done=b % 4 == 3)
            for j in range(2):
                for h2 in range(2):
                    h = 2 * j + h2
                    st = V.tt(ST[:, 256 * h:256 * h + 256].rearrange("p (s t) -> p s t", s=2),
                              banks[2 + j].t[:, 256 * h2:256 * h2 + 256].rearrange("p (s t) -> p s t", s=2),
                              wide(C("rmask")[:, 128 * h:128 * h + 128], 1, 2), OP.mult, t, *start)
                banks[2 + j].free = (st,)
            qx = [G.tt(v3(RQ, 64)[:, 4 * h:4 * h + 4, :], v3(RQ, 64)[:, 4 * h:4 * h + 4, :], wide(C("xi")[:, 64 * h:64 * h + 64], 1, 4), OP.mult, t)
                  for h in range(4)][-1]
            yield 2
            rr = lambda n, h: RR[:, 512 * (n - 1) + 128 * h:512 * (n - 1) + 128 * h + 128]
            E.wait(kz, *rv)
            rd = None
            for n in range(3):
                half, q = n // 2, n % 2
                r = slice(64 * q, 64 * q + 64)
                b = banks[n % 2]
                E.wait(*b.free)
                for h in range(4):
                    t = mm(b.t[:, 128 * h:128 * h + 128], KZ[r, 256 * h + 128 * half:256 * h + 128 * half + 128],
                           RV[r, 512 * half + 128 * h:512 * half + 128 * h + 128], True, True, done=h == 3)
                for h in range(4):
                    src = b.t[:, 128 * h:128 * h + 128]
                    if n == 0:
                        rd = V.copy(rr(1, h), src, t, *start)
                    else:
                        rd = V.stt(rr(n + 1, h), rr(n, h), CHUNK_DECAY[h], src, OP.mult, OP.add, t, rd)
                b.free = (rd,)
                yield
            E.wait(st, qx, rd)
            for j in range(2):
                E.wait(*banks[2 + j].free)
                for b in range(4 * j, 4 * j + 4):
                    h, half = b // 2, b % 2
                    o = banks[2 + j].t[:, 128 * (b % 4):128 * (b % 4) + 128]
                    mm(o, RV[:, 512 * half + 128 * h:512 * half + 128 * h + 128], kb3(ST, b), True, False, skip=True)
                    for q in range(2):
                        n = 2 * half + q
                        if n:
                            t = mm(banks[2 + j].t[:, 128 * (b % 4) + 64 * q:128 * (b % 4) + 64 * q + 64], rr(n, h),
                                   RQ[:, 256 * h + 64 * n:256 * h + 64 * n + 64], False, q == 1, skip=True, done=b % 4 == 3 and q == 1)
            for j in range(2):
                o = A.copy(OR[:, 512 * j:512 * j + 512], banks[2 + j].t[:, :], t, *start)
                banks[2 + j].free = (o,)
            yield 2
            E.wait(o)
            for j in range(2):
                E.wait(*banks[j].free)
                t = mm(banks[j].t[:, :], C("ones"), OR[:, 512 * j:512 * j + 512], True, True, done=True)
                w = V.stt(OR[:, 512 * j:512 * j + 512], banks[j].t[:, :], -1.0 / 128, OR[:, 512 * j:512 * j + 512], OP.mult, OP.add, t)
                banks[j].free = (w,)
            s = A.act(O2[:, :], OR[:, :], AF.Square, w)
            yield 2
            E.wait(s)
            for j in range(2):
                E.wait(*banks[j].free)
                t = mm(banks[j].t[:, :], C("ones"), O2[:, 512 * j:512 * j + 512], True, True, done=True)
                a = A.act(SR[:, 512 * j:512 * j + 512], banks[j].t[:, :], AF.Ln, t, *start, scale=1.0 / 128, bias=C("eps5"))
                banks[j].free = (a,)
            a = A.act(SR[:, :], SR[:, :], AF.Exp, a, scale=-0.5)
            yield
            for h in range(4):
                c = slice(T * h, T * h + T)
                w = V.stt(OR[:, c], OR[:, c], Q("retout", l)[:, h:h + 1], SR[:, c], OP.mult, OP.mult, a)
            w = V.tt(OR[:, :], OR[:, :], RG[:, :], OP.mult, w, *zt)
            out.append(w)

        def first_layer(l, norm):
            cw = Q("conv", l).rearrange("p (m i) -> p m i", i=4)
            U3, A3 = v3(U), v3(QKV)
            sw_ready, lev_ready = small_ready[l], lev_loads[l]
            late, conv, squared = [], [], []

            def silu():
                while late:
                    m0, t = late.pop()
                    c = slice(m0 * T, (m0 + 2) * T)
                    t = A.act(QKV[:, c], QKV[:, c], AF.Silu, *t)
                    conv.append(t)
                    if m0 < 8:
                        squared.append(A.act(SQ[:, c], QKV[:, c], AF.Square, t))

            def conv_evac(m0, n, b, tok):
                t = times_rms(U[:, m0 * T:(m0 + n) * T], b, n, norm, tok)
                toks = []
                for m in range(m0, m0 + n):
                    w = A.act(A3[:, m, :], U3[:, m, :], AF.Copy, t, scale=cw[:, m, 3:4])
                    for j in range(1, 4):
                        w = V.stt(A3[:, m, j:T], U3[:, m, 0:T - j], cw[:, m, 3 - j:4 - j], A3[:, m, j:T], OP.mult, OP.add, w)
                    toks.append(w)
                silu()
                late.append((m0, toks))

            z, rqk, rv, rg, pu, od, oo, op_, yd, zt = ([] for _ in range(10))
            g0, g1, g2 = Gate(GT, norm), Gate(XY, norm), Gate(GT, norm, yd, 4)

            def middle():
                assert len(z) == 2 and len(rg) == 2
                A.act(Z[:, :], Z[:, :], AF.Silu, *z)
                zt.append(A.act(RG[:, :], RG[:, :], AF.Silu, *rg))
                A.preload()

            sm3 = small[:, 0:64].rearrange("p (k c) -> p k c", c=8)
            sw = []

            def qkv_hook():
                norm.finish()
                helped[0] = 4
                sw.append(A.copy(SW[:, :, 0:8], sm3, sw_ready))
                sw.append(V.tt(SW[:, :, 8:16], sm3, SW[:, :, 0:8].bitcast(F32), OP.subtract, *sw, sw_ready))

            qkv = project(("qkv", l), 12, (hh, hl), 8, norm.toks, conv_evac, qkv_hook)
            for _ in range(2):
                next(qkv)
            b = banks[1]
            E.wait(*sw, *b.free)
            for s in range(2):
                for k in range(8):
                    mm(b.t[:, 16 * s:16 * s + 16], hh[:, k, 128 * s:128 * s + 128], SW[:, k, :], k == 0, False, skip=True)
                    t = mm(b.t[:, 16 * s:16 * s + 8], hl[:, k, 128 * s:128 * s + 128], SW[:, k, 0:8], False, k == 7, skip=True, done=k == 7)
            two = b.t[:, 0:32].rearrange("p (s c) -> p s c", s=2)
            AB, tmp = (SM[:, c:c + 16].rearrange("p (s c) -> p s c", s=2) for c in (192, 224))
            ab = V.copy(tmp, two[:, :, 8:16], t)
            ab = V.tt(AB, two[:, :, 0:8], tmp, OP.add, ab)
            b.free = (ab,)
            ab = V.tt(AB, AB, wide(RST[:, :], 2, 8), OP.mult, ab, norm.rt)
            dn = delta_rule(l, squared, conv, (ab, par_ready), middle, zt, od)
            next(dn)
            run(qkv)
            helped[0] = 0
            silu()
            for e in (A, V, G, E):
                e.wait(c1_ready, lev_ready)

            def rv_evac(s, b, tok):
                t = A.act(RV[:, 512 * s:512 * s + 512], b.t[:, :], AF.Copy, tok, norm.rt, scale=RST[:, s:s + 1])
                b.free = (t,)
                rv.append(t)

            wdn = Branch(BR0, ("wdn", l), OD, od, 1, 4, g0, True, yd)
            wpool = Branch(BR1, ("wpool", l), PC, op_, 1, 4, g1, False, yd)
            wret = Branch(BR0, ("wret", l), OR, oo, 1, 4, g2, False, yd)
            fill = chain(project(("pu", l), 4, (hh, hl), 8, norm.toks, copy_to(PU, pu, norm)),
                         project(("z", l), 4, (hh, hl), 8, norm.toks, copy_to(Z, z, norm)),
                         project(("rqk", l), 8, (hh, hl), 8, norm.toks, copy_to(RQK, rqk)),
                         by_token(("rv", l), norm.toks, rv_evac),
                         project(("rg", l), 4, (hh, hl), 8, norm.toks, copy_to(RG, rg, norm)),
                         project(("gate0", l), 8, (hh, hl), 8, norm.toks, g0.evac),
                         before_end(project(("gate1", l), 8, (hh, hl), 8, norm.toks, g1.evac), 3, wdn.prepare),
                         wdn.steps(), one(wpool.prepare),
                         project(("gate2", l), 8, (hh, hl), 8, norm.toks, g2.evac),
                         wpool.steps())

            def first_mixers():
                pool = None
                yield
                for i, n in enumerate(dn):
                    yield n
                    if pool is None and len(pu) == 2 and i > 6:
                        pool = pooling(l, pu, op_)
                    if pool is not None:
                        next(pool, None)
                assert op_

            run(first_mixers(), fill)
            wdn.after = tuple(op_)
            helped[0] = 3
            run(retention(l, norm, rqk, rv, zt, oo), fill)
            helped[0] = 0
            while not wdn.over:
                next(fill)
            wret.prepare()
            run(fill)
            merged = Merged(wret)
            run(wret.steps(merged.evac))
            merged.flush()
            A.preload()
            settled = everything()
            pn = PostNorm(Q("mixpost", l), banks[0])
            run(project(("wout", l), 8, (FH, FL), 8, merged.toks, pn.evac, lead=True))
            norm = pn.finish(Norm(Q("ffnpre", l), banks[0]))
            ready, late1, late2 = [], [], []

            def parts():
                while late2:
                    i, hi, f = late2.pop()
                    ready.append((hi, V.tt(FL[:, i, :], f, FH[:, i, :].bitcast(F32), OP.subtract, hi)))

            def product():
                while late1:
                    i, a, f = late1.pop()
                    w = V.tt(f[:, 0:T], f[:, 0:T], f[:, T:2 * T], OP.mult, a)
                    late2.append((i, A.copy(FH[:, i, :], f[:, 0:T], w), f[:, 0:T]))

            def ffn_evac(m0, n, b, tok):
                i = m0 // 2
                f = FT[:, 512 * (i % 4):512 * (i % 4) + 512]
                w = times_rms(f, b, n, norm, tok, *(ready[i - 4] if i >= 4 else ()))
                parts()
                product()
                late1.append((i, A.act(f[:, 0:T], f[:, 0:T], AF.Silu, w), f))

            gu = project(("gu", l), 44, (hh, hl), 8, norm.toks, ffn_evac, norm.finish)
            for _ in range(8):
                next(gu)
            if l == 0:
                small_ready.append(load(small[:, :], ins["small"][:, N_SMALL:2 * N_SMALL], s_small2, *settled))
                lev_loads.append(load(LEV, ins["lev"], s_lev[1], *settled))
            if l == DEPTH - 1:
                run(rope_tables(settled), gu)
            run(gu)
            pn = PostNorm(Q("ffnpost", l), banks[7])
            down(("down", l), 22, FH, FL, ready, pn.evac, (parts, product, parts, A.preload))
            return pn.finish(Norm(Q("mixpre", l + 1) if l + 1 < DEPTH else Q("attn", DEPTH), banks[4], True))

        QF = slot("QF", 0, 7)
        VT = slot("VT", 7, 2)
        LG = [slot("LG", 9, 3)[:, 1536 * i:1536 * i + 1536] for i in range(2)]
        PT = slot("PT", 12, 2)
        OO = slot("OO", 14, 3)
        REL = slot("REL", 17, 2)
        SC = slot("SC", 19)
        SS = slot("SS", 20)
        RT = slot("RT", 21)
        OTK, AM = slot("OTK", 22)[:, 0:384], slot("OTK", 22)[:, 512:896]
        CS = slot("CS", 27)
        ROPE, POS = slot("ROPE", 23), slot("POS", 24, dt=I32)
        QF3, OO3 = v3(QF), v3(OO)
        COS, SIN = CS[:, 0:256], CS[:, 256:512]
        IW = SS[:, 0:16]

        def rope_tables(settled):
            ready = load(cst[:, HEAD:N_CONST2], ins["const2"][:, HEAD:N_CONST2], s_c2, *settled)
            for e in (A, V, G, E):
                c2_ready.append(ready)
            ld = load(POS[:, 0:T], ins["positions"], s_pos, *settled)
            a, n = ROPE[:, 0:256], ROPE[:, 256:512]
            for _ in range(4):
                yield
            w = V.copy(a, POS[:, 0:T], ld)
            w = V.ts(a, a, C("inv", CONST2), None, OP.mult, None, w, ready)
            big, two_pi = 12582912.0, 2.0 * np.pi
            c1 = 6.28125
            c2, c3 = SPLIT_PI
            for dst, turn in ((SIN, 0.0), (COS, 0.25)):
                u = V.ts(n, a, 1.0 / two_pi, turn, OP.mult, OP.add, w)
                u = V.ts(n, n, big, None, OP.add, None, u)
                u = V.ts(n, n, big, None, OP.subtract, None, u)
                yield
                u = V.stt(dst, n, -c1, a, OP.mult, OP.add, u)
                u = V.stt(dst, n, -c2, dst, OP.mult, OP.add, u)
                u = V.stt(dst, n, -c3, dst, OP.mult, OP.add, u)
                yield
                if turn:
                    u = V.ts(dst, dst, float(np.float32(np.pi / 2)), None, OP.add, None, u)
                u = V.ts(dst, dst, 3.1415925, -3.1415925, OP.min, OP.max, u)
                w = A.act(dst, dst, AF.Sin, u)
            roping.append(w)

        c2_ready, roping = [], []

        COSN, SINN = CS[:, 512:768], CS[:, 768:1024]

        def second_layer(l, norm):
            cs = roping[0]
            ring[0], ring[1] = 0, [6, 7, 0, 1, 2]
            roped = {}
            adding = []
            turns = [0]
            rbanks = [4, 5]
            tables = []

            def hook():
                norm.finish()
                tables.append(V.tt(COSN, COS, RSB[:, :], OP.mult, norm.r, cs))
                tables.append(V.tt(SINN, SIN, RSB[:, :], OP.mult, norm.r, cs))

            def rope_add():
                while adding:
                    m0, n, f, tmp, w, g = adding.pop()
                    w = V.tt(f, f, tmp, OP.add, w, g)
                    for m in range(m0, m0 + n):
                        roped[m] = w

            def rope(m0, n, ready, plain=False):
                rope_add()
                turns[0] += 1
                b = banks[rbanks[turns[0] % len(rbanks)]]
                E.wait(*ready, *b.free)
                w_ = n * T
                f = QF[:, m0 * T:m0 * T + w_]
                t = mm(b.t[:, 0:w_], C("rot2", CONST2), f, True, True, done=True)
                tmp = RT[:, 0:w_] if turns[0] % 2 else RT[:, 512:512 + w_]
                cos_, sin_ = (COS, SIN) if plain else (COSN, SINN)
                w = V.tt(v3(tmp), b.t[:, 0:w_].rearrange("p (m t) -> p m t", t=T), wide(sin_, 1, n), OP.mult, t, cs, *tables)
                b.free = (w,)
                g = G.tt(v3(f), v3(f), wide(cos_, 1, n), OP.mult, t, cs, *ready, *tables)
                adding.append((m0, n, f, tmp, w, g))

            pend = []

            def flush():
                while pend:
                    rope(*pend.pop(0))

            normed = []

            def keys():
                while normed:
                    s, f, n, t = normed.pop()
                    bb = banks[3]
                    E.wait(s, *bb.free)
                    t2 = mm(bb.t[:, 0:T], C("half", CONST2), REL[:, 0:T], True, True, done=True)
                    r = rstd_of(bb, T, 1.0 / 64, C("eps6"), REL[:, 256:512], t2)
                    w = V.stt(f, f, Q("idxk", DEPTH + l), REL[:, 256:512], OP.mult, OP.mult, r)
                    pend.append((8, 1, (w,), True))
                    pend.append((9, n - 1, (t,)))

            def evac_from(base):
                def evac(m0, n, b, tok):
                    m0 += base
                    keys()
                    t = A.copy(QF[:, m0 * T:(m0 + n) * T], b.t[:, 0:n * T], tok)
                    b.free = (t,)
                    flush()
                    if m0 == 8:
                        f = QF[:, 8 * T:9 * T]
                        w = V.tt(f, f, RSB[:, :], OP.mult, t, norm.r)
                        s = A.act(REL[:, 0:T], f, AF.Square, w)
                        normed.append((s, f, n, t))
                    else:
                        pend.append((m0, n, (t,)))
                return evac

            vt = []
            bv = lambda half, head: VT[:, 960 * half + 64 * head:960 * half + 64 * head + 64]
            cv = lambda half, kv: VT[:, 960 * half + 768 + 64 * kv:960 * half + 832 + 64 * kv]
            av = lambda half: VT[:, 960 * half + 896:960 * half + 960]

            def v_evac(group):
                def evac(s, b, tok):
                    r = RST[:, s:s + 1]
                    if group == 0:
                        t = A.act(VT[:, 960 * s:960 * s + 512], b.t[:, :], AF.Copy, tok, norm.rt, scale=r)
                    else:
                        A.act(VT[:, 960 * s + 512:960 * s + 960], b.t[:, 0:448], AF.Copy, tok, scale=r)
                        t = A.act(IW[:, 8 * s:8 * s + 8], b.t[:, 448:456], AF.Copy, tok, scale=r)
                    b.free = (t,)
                    vt.append(t)
                return evac

            run(project(("q2a", l), 11, (hh, hl), 8, norm.toks, evac_from(0), hook))
            run(by_token(("v2a", l), norm.toks, v_evac(0)))
            flush()
            run(by_token(("v2b", l), norm.toks, v_evac(1)))
            rope_add()
            rbanks[:] = [5, 4]
            ring[0], ring[1] = 0, [6, 7]

            def index(half):
                nk = 128 * (half + 1)
                per = 512 // nk
                qs = slice(128 * half, 128 * half + 128)
                E.wait(roped[7], roped[8])
                rel = REL[:, 0:8 * nk].rearrange("p (c n t) -> p c n t", c=2, t=nk)
                toks = {}
                for par_ in range(2):
                    r = slice(64 * par_, 64 * par_ + 64)
                    for j in range(4):
                        b = banks[2 * par_ + j // per]
                        if j % per == 0:
                            E.wait(*b.free)
                        t = mm(b.t[:, nk * (j % per):nk * (j % per) + nk], QF3[r, 4 + j, qs], QF3[r, 8, 0:nk], True, True,
                               done=j % per == per - 1 or j == 3)
                        toks[par_, j // per] = t
                for par_ in range(2):
                    for k in range((4 + per - 1) // per):
                        b = banks[2 * par_ + k]
                        n = min(per, 4 - k * per)
                        w = A.act(rel[:, par_, k * per:k * per + n, :], b.t[:, 0:n * nk].rearrange("p (n t) -> p n t", t=nk), AF.Relu,
                                  toks[par_, k], *relfree, scale=0.125 * 8.0 ** -0.5)
                        b.free = (w,)
                relfree.clear()
                sc = [SC[:, 0:nk], SC[:, 256:256 + nk]]
                causal = C(f"mA{half}", CONST2)
                first = True
                for par_ in range(2):
                    for j in range(4):
                        w = V.stt(sc[0], rel[:, par_, j, :], IW[:, 8 * half + 2 * j + par_:8 * half + 2 * j + par_ + 1],
                                  causal if first else sc[0], OP.mult, OP.add, w, vt[-1], vt[-2])
                        first = False
                relfree.append(w)
                yield
                m8 = SS[:, 16:24]
                for r in range(8):
                    w = V.do(lambda e, i=sc[0]: e.max(m8, i), w)
                    w = V.do(lambda e, i=sc[0], o=sc[1]: e.match_replace(o, m8, i, TAKEN), w)
                    sc = sc[::-1]
                    if r % 2 == 1:
                        yield
                am = AM[:, 128 * half:128 * half + nk]
                w = V.ts(am, sc[0], -2.0e38, NEG, OP.is_gt, OP.mult, w)
                w = V.tt(am, am, causal, OP.add, w)
                amask[half] = w
                yield

            relfree = []
            amask = {}
            lfree = {0: [], 1: []}

            def attend(turn, half, n, qtile, ktile, mask, mready, joint, sink, values, dst, otoks):
                nk = 128 * (half + 1)
                per = 512 // nk
                qs = slice(128 * half, 128 * half + 128)
                mready = (mready(),) if mready else ()
                if any(m(i) not in roped for m in (qtile, ktile) for i in range(n)):
                    rope_add()
                E.wait(*(roped[qtile(i)] for i in range(n)), *(roped[ktile(i)] for i in range(n)))
                LB, free = LG[turn % 2][:, 0:2 * n * nk], lfree[turn % 2]
                L = LB.rearrange("p (c n t) -> p c n t", c=2, t=nk)
                if half == 0:
                    plan = [(0, [(0, i) for i in range(n)]), (2, [(1, i) for i in range(n)])]
                elif n == 2:
                    plan = [(0, [(0, 0), (0, 1)]), (2, [(1, 0), (1, 1)])]
                else:
                    plan = [(1, [(0, 2)]), (0, [(0, 0), (0, 1)]), (2, [(1, 0), (1, 1)]), (1, [(1, 2)])]
                where = {}
                for q, (bk, heads) in enumerate(plan):
                    b = banks[bk]
                    E.wait(*b.free)
                    if q == 3:
                        E.wait(where[0][3])
                    c0 = nk if q == 3 else 0
                    for m, (c, i) in enumerate(heads):
                        r = slice(64 * c, 64 * c + 64)
                        t = mm(b.t[:, c0 + nk * m:c0 + nk * m + nk], QF3[r, qtile(i), qs], QF3[r, ktile(i), 0:nk], True, True,
                               done=m == len(heads) - 1)
                    where[q] = (b, c0, heads, t)
                if len(plan) == 4:
                    where[0] = (*where[0][:3], where[3][3])
                for q in ((1, 2, 0, 3) if len(plan) == 4 else (0, 1)):
                    b, c0, heads, t = where[q]
                    (c, i), m = heads[0], len(heads)
                    w = V.tt(L[:, c, i:i + m, :], b.t[:, c0:c0 + m * nk].rearrange("p (n t) -> p n t", t=nk), mask(i, m), OP.add,
                             t, *mready, *free)
                    b.free = (w,)
                free.clear()
                st = [SS[:, 32 + 64 * (turn % 2) + 16 * i:40 + 64 * (turn % 2) + 16 * i] for i in range(3)]
                ng = 2 if joint else 2 * n
                Lg = LB.rearrange("p (g t) -> p g t", g=ng)
                mx, den, ex = (x[:, 0:ng] for x in st)
                w = V.red(mx, Lg, OP.max, w)
                if sink is None:
                    w = V.ts(mx, mx, -0.125, None, OP.mult, None, w)
                else:
                    w = V.stt(mx, mx, 0.125, sink, OP.mult, OP.max, w)
                    w = V.tt(ex, sink, mx, OP.subtract, w)
                    ed = w
                    w = V.ts(mx, mx, -1.0, None, OP.mult, None, w)
                yield
                if sink is not None:
                    se = A.act(ex, ex, AF.Exp, ed)
                for g in range(ng):
                    a = A.act(Lg[:, g, :], Lg[:, g, :], AF.Exp, w, scale=0.125, bias=mx[:, g:g + 1], accum=den[:, g:g + 1])
                yield
                w = a
                if sink is not None:
                    w = V.tt(den, den, ex, OP.add, a, se)
                rd = V.recip(den, den, w)
                E.wait(a)
                spread = [(3, 0, [(0, j) for j in range(4)])]
                if half:
                    spread.append((5 if n > 2 else 4, 768, [(1, j) for j in range(4)]))
                if n > 2:
                    spread.append((4, 512, [(kb, j) for kb in range(half + 1) for j in (4, 5)]))
                for bk, c0, heads in spread:
                    b = banks[bk]
                    E.wait(*b.free)
                    for q, (kb, j) in enumerate(heads):
                        fn = lambda e, o=b.t[:, 128 * q:128 * q + 128], i=L[:, j % 2, j // 2, 128 * kb:128 * kb + 128]: e.transpose(o, i, C("eye", CONST2))
                        t = E.do(fn) if q == len(heads) - 1 else E.quiet(fn)
                    m = 128 * len(heads)
                    if c0 == 512 and half:
                        p = A.copy(PT[:, 0:1536].rearrange("p (k c) -> p k c", k=2)[:, :, 512:768], b.t[:, 0:m].rearrange("p (k c) -> p k c", k=2), t)
                    else:
                        p = A.copy(PT[:, c0:c0 + m], b.t[:, 0:m], t)
                    b.free = (p,)
                free.append(t)
                yield
                E.wait(p, *vt)
                b = banks[5]
                E.wait(*b.free)
                heads = [(0, c) for c in range(2)] if joint else [(i, c) for i in range(n) for c in range(2)]
                for q, (i0, c) in enumerate(heads):
                    terms = [(i, kb) for i in (range(n) if joint else [i0]) for kb in range(half + 1)]
                    for u, (i, kb) in enumerate(terms):
                        t = mm(b.t[:, 64 * q:64 * q + 64], PT[:, 768 * kb + 128 * (2 * i + c):768 * kb + 128 * (2 * i + c) + 128],
                               values(kb, i, c), u == 0, u == len(terms) - 1, done=(q, u) == (len(heads) - 1, len(terms) - 1))
                nh = len(heads)
                by = (den if joint else den.rearrange("p (c n) -> p n c", c=2))
                src = b.t[:, 0:64 * nh]
                o4 = OTK[:, 0:64 * nh]
                if joint:
                    w = V.tt(o4.rearrange("p (h d) -> p h d", d=64), src.rearrange("p (h d) -> p h d", d=64), wide(by, 2, 64), OP.mult, t, rd)
                else:
                    w = V.tt(o4.rearrange("p (n c d) -> p n c d", c=2, d=64), src.rearrange("p (n c d) -> p n c d", c=2, d=64),
                             wide(by, 3, 64), OP.mult, t, rd)
                b.free = (w,)
                yield
                b = banks[3]
                E.wait(w, *b.free)
                for q in range(nh // 2):
                    fn = lambda e, o=b.t[:, 128 * q:128 * q + 128], i=OTK[:, 128 * q:128 * q + 128]: e.transpose(o, i, C("eye", CONST2))
                    t = E.do(fn) if q == nh // 2 - 1 else E.quiet(fn)
                w = A.copy(OO3[:, dst:dst + nh // 2, qs], b.t[:, 0:64 * nh].rearrange("p (n t) -> p n t", t=128), t)
                b.free = (w,)
                otoks.append(w)

            oa, ob, oc, g0, g1, g2, yd = ([] for _ in range(7))
            mA = lambda half: lambda i, m: wide(AM[:, 128 * half:128 * half + 128 * (half + 1)], 1, m)
            mB = lambda half: lambda i, m: C(f"mB{half}", CONST2).rearrange("p (g t) -> p g t", g=3)[:, i:i + m, :]
            mC = lambda half: lambda i, m: wide(C(f"mC{half}", CONST2), 1, m)
            ra = [(half, 3, lambda i: i, lambda i: 3, mA(half), lambda half=half: amask[half], False, None,
                   lambda kb, i, c: av(kb), 0, oa) for half in range(2)]
            rc = [(half, 2, lambda i, r=r: 23 + 2 * r + i, lambda i, r=r: 9 + r, mC(half), None, False,
                   Q("sinks", DEPTH + l)[:, 4 * r:4 * r + 4], lambda kb, i, c, r=r: cv(kb, r), 5 + 2 * r, oc) for half in range(2) for r in range(2)]
            rb = [(half, 3, lambda i, jp=jp: 11 + 2 * i + jp, lambda i, jp=jp: 17 + 2 * i + jp, mB(half), None, True,
                   None, lambda kb, i, c, jp=jp: bv(kb, 4 * i + 2 * jp + c), 3 + jp, ob) for half in range(2) for jp in range(2)]
            rounds = [*ra, *rb, *rc]

            def attention():
                yield from index(0)
                yield from index(1)
                before = None
                for turn, r in enumerate(rounds):
                    g = attend(turn, *r)
                    next(g)
                    yield
                    if before is not None:
                        next(before)
                    yield
                    next(g)
                    if before is not None:
                        next(before)
                    yield
                    if before is not None:
                        next(before, None)
                    before = g
                for _ in before:
                    yield

            def flushing():
                flush()
                yield
                rope_add()

            g0, g1, g2 = Gate(GT, norm), Gate(REL, norm), Gate(GT, norm, yd, 4)
            wa = Branch(BR0, ("wa", l), OO[:, 0:768], oa, 2, 3, g0, True, yd)
            wb = Branch(BR0, ("wb", l), OO[:, 768:1280], ob, 4, 2, g1, False, yd)
            wc = Branch(BR2, ("wc", l), OO[:, 1280:2304], oc, 4, 4, g2, False, yd)
            fill = chain(project(("q2b", l), 16, (hh, hl), 8, norm.toks, evac_from(11)), flushing(),
                         project(("gate0", 2 + l), 8, (hh, hl), 8, norm.toks, g0.evac),
                         before_end(project(("gate1", 2 + l), 8, (hh, hl), 8, norm.toks, g1.evac), 5, wa.prepare),
                         wa.steps(),
                         before_end(project(("gate2", 2 + l), 8, (hh, hl), 8, norm.toks, g2.evac), 5, wb.prepare),
                         wb.steps())
            helped[0] = 2
            run(attention(), fill)
            helped[0] = 0
            wc.prepare()
            run(fill)
            merged = Merged(wc)
            run(wc.steps(merged.evac))
            merged.flush()
            ring[0], ring[1] = 0, [4, 5, 6, 7]
            norm = Norm(Q("mlp", DEPTH + l), banks[0])
            run(project(("wo", l), 8, (FH, FL), 8, merged.toks, Residual(norm).evac, lead=True))
            ready, late = [], []

            def parts():
                while late:
                    m0, f, s = late.pop()
                    hi = A.copy(FH[:, m0:m0 + 2, :], v3(f), s)
                    lo = V.tt(FL[:, m0:m0 + 2, :], v3(f), FH[:, m0:m0 + 2, :].bitcast(F32), OP.subtract, hi)
                    ready.extend([(hi, lo)] * 2)

            def mlp_evac(m0, n, b, tok):
                f = FT[:, 256 * (m0 % 8):256 * (m0 % 8) + 512]
                w = V.stt(v3(f), b.t[:, :].rearrange("p (m t) -> p m t", t=T), 0.0, wide(RSB[:, :], 1, n), OP.max, OP.mult,
                          tok, norm.r, *(ready[m0 - 8] if m0 >= 8 else ()))
                b.free = (w,)
                parts()
                late.append((m0, f, A.act(f, f, AF.Square, w)))

            run(project(("up", l), 32, (hh, hl), 8, norm.toks, mlp_evac, norm.finish))
            if l + 1 < DEPTH:
                norm = Norm(Q("attn", DEPTH + l + 1), banks[4], True)
                down(("down2", l), 32, FH, FL, ready, Residual(norm).evac, (parts,))
                return norm
            last = Last(banks[7])
            down(("down2", l), 32, FH, FL, ready, Residual(last).evac, (parts,))
            r = last.st.rstd()
            for k in range(8):
                x = V.stt(xT[:, k, :], xT[:, k, :], Q("final", DEPTH + l)[:, k:k + 1], RS[:, 0:T], OP.mult, OP.mult, r)
            return x

        A.preload()
        x_ready = []

        def load_x(j):
            x_ready.append(load(xT[:, 2 * j:2 * j + 2, :], ins["x"][:, 2 * j:2 * j + 2, :], s_x4[j]))

        load_x(0)
        par_ready = load(par[:, :], ins["par"], s_par)
        fetch()
        load_x(1)
        fetch()
        load_x(2)
        load_x(3)
        head_ready = load(cst[:, 0:HEAD], ins["const1"][:, 0:HEAD], s_head)
        small_ready = [load(small[:, :], ins["small"][:, 0:N_SMALL], s_small)]
        for _ in range(RAW - 2):
            fetch()
        c1_ready = load(cst[:, HEAD:N_CONST1], ins["const1"][:, HEAD:N_CONST1], s_c1)
        lev_loads = [load(LEV, ins["lev"], s_lev[0])]
        for e in (A, V):
            e.wait(par_ready)
        h = Norm(Q("mixpre", 0), banks[0], True)
        for j in range(4):
            h.parts(j, x_ready[j])
            if j < 2:
                stage()
        for j in range(4):
            h.square(j, x_ready[j])
        for e in (A, V, G, E):
            e.wait(head_ready)
        for l in range(DEPTH):
            h = first_layer(l, h)
        for e in (A, V, G, E):
            e.wait(*c2_ready)
        consts[0] = CONST2
        for l in range(DEPTH):
            h = second_layer(l, h)
        last = everything()
        S.wait(*last)
        for i in range(fetched[0]):
            if i >= fetched[0] - RAW:
                S.wait((s_raw[i % RAW], 16 * (i // RAW + 1)))
        S.queue.append(lambda e: e.dma_start(out, xT[:, :, :]).then_inc(s_out, 16))
        S.wait((s_out, 16))
        assert len(order) == NCHUNK, len(order)
        block = ctx.enter_context(nc.Block())
        block.sync(S.play)
        block.scalar(A.play)
        block.vector(V.play)
        block.gpsimd(G.play)
        block.tensor(E.play)
    return order


LOG_GAMMA = [np.log1p(-np.exp2(np.float32(-5.0 - h))) for h in range(4)]
CHUNK_DECAY = [float(np.exp(np.float32(64.0 * g))) for g in LOG_GAMMA]


def levels():
    p, f = np.arange(P)[:, None], np.arange(P)[None, :]
    return [(p // (2 << s) == f // (2 << s)) & (p // (1 << s) % 2 == 1) & (f // (1 << s) % 2 == 0) for s in range(6)]


def constants1():
    c = np.zeros((P, N_CONST1), np.float32)

    def put(name, a):
        o, w = CONST1[name]
        c[:, o:o + w] = a

    p = np.arange(P)[:, None]
    f = np.arange(P)[None, :]
    same = p // 64 == f // 64
    put("ones", 1.0)
    put("eye", p == f)
    put("eps6", 1e-6)
    put("eps5", 1e-5)
    put("one", 1.0)
    put("upper", same & (p <= f))
    put("chunk", same)
    lev = levels()
    put("levT", np.concatenate([a.T for a in lev], 1))
    rot = np.zeros((P, P))
    for i in range(64):
        rot[i + 64, i] = -1.0
        rot[i, i + 64] = 1.0
    put("rot", rot)
    inv = np.float32(10000.0) ** (-np.arange(64, dtype=np.float32) / 64)
    ang = inv.astype(np.float32)[:, None] * np.arange(T, dtype=np.float32)[None, :]
    put("cos", np.tile(np.cos(ang.astype(np.float64)), (2, 1)))
    put("sin", np.tile(np.sin(ang.astype(np.float64)), (2, 1)))
    lg = [float(g) for g in LOG_GAMMA]
    put("rmask", np.concatenate([np.where(same, np.exp(np.abs(p - f) * g), 0) * 128 ** -0.5 for g in lg], 1))
    t = np.arange(T)[None, :]
    put("xi", np.concatenate([np.exp((t[:, 0:64] + 1) * g) for g in lg], 1))
    put("zeta", np.concatenate([np.exp((63 - p % 64) * g) * 128 ** -0.5 for g in lg], 1))
    put("cnt", np.concatenate([1.0 / np.minimum(t[:, 0:16] + 1, w) for w in (2, 4, 8, 16)], 1))
    put("cntw", np.array([[1.0 / w for w in (2, 4, 8, 16)]]))
    return c


def _split_pi():
    rest = 2.0 * np.pi - 6.28125
    c2 = round(rest * 2.0 ** 21) / 2.0 ** 21
    return c2, float(np.float32(rest - c2))


SPLIT_PI = _split_pi()


def constants2():
    c = np.zeros((P, N_CONST2), np.float32)

    def put(name, a):
        o, w = CONST2[name]
        c[:, o:o + w] = a

    p = np.arange(P)[:, None]
    f = np.arange(P)[None, :]
    put("ones", 1.0)
    put("eye", p == f)
    put("eps6", 1e-6)
    put("eps5", 1e-5)
    put("one", 1.0)
    put("half", p // 64 == f // 64)
    rot = np.zeros((P, P))
    for b in range(0, P, 64):
        for i in range(32):
            rot[b + i + 32, b + i] = -1.0
            rot[b + i, b + i + 32] = 1.0
    put("rot2", rot)
    inv = np.float32(10000.0) ** (-np.arange(32, dtype=np.float32) / 32)
    put("inv", np.tile(inv, 4)[:, None])
    for half in range(2):
        t = p + 128 * half
        s = np.arange(128 * (half + 1))[None, :]
        neg = lambda ok: np.where(ok, 0.0, NEG)
        put(f"mA{half}", neg(s <= t))
        put(f"mC{half}", neg((s <= t) & (s > t - 128)))
        put(f"mB{half}", np.concatenate([neg((s <= t) & (t - s <= w) & ((t - s) % d == 0)) for w, d in ((128, 1), (512, 4), (2048, 16))], 1))
    return c


S1 = dict(qkv=(0, 1536), z=(1536, 512), ab=(2048, 8), rqk=(2056, 1024), rv=(3080, 512), rg=(3592, 512), pu=(4104, 512), gate=(4616, 3072))
S2 = {}
_at = 0
for _n, _w in (("aq", 384), ("ak", 64), ("av", 64), ("iq", 512), ("ik", 64), ("iw", 8), ("bq", 768), ("bk", 768), ("bv", 768),
               ("cq", 512), ("ck", 128), ("cv", 128), ("gate", 3072)):
    S2[_n] = (_at, _w)
    _at += _w


def pack(order, inputs):
    w = {k: np.asarray(inputs[k]) for k in ("w_in", "w_branch_dn", "w_branch_ret", "w_branch_pool", "w_out", "ffn_gate", "ffn_up", "ffn_down",
                                            "w_in_2", "w_a_2", "w_b_2", "w_c_2", "w_o_2", "w_up_2", "w_down_2")}
    made = {}

    def cols(a, at, n):
        return a[:, at:at + n]

    def tiles(a):
        k, m = a.shape[0] // P, a.shape[1] // P
        t = a.reshape(k, P, m, P).transpose(2, 0, 1, 3).reshape(-1, 8, P, P)
        return t.transpose(0, 2, 1, 3).reshape(-1, P, 1024)

    def rows(a):
        return a.reshape(-1, P, 1024)

    def moving(a):
        return a.reshape(4, 2, P, 512).transpose(0, 2, 1, 3).reshape(4, P, 1024)

    def make(name, l):
        if name in ("qkv", "z", "rqk", "rg", "pu"):
            return tiles(cols(w["w_in"][l], *S1[name]))
        if name == "rv":
            return moving(cols(w["w_in"][l], *S1["rv"]))
        if name in ("gate0", "gate1", "gate2"):
            a, s = (w["w_in"][l], S1) if l < 2 else (w["w_in_2"][l - 2], S2)
            return tiles(cols(a, s["gate"][0] + 1024 * int(name[4]), 1024))
        if name == "gu":
            g, u = w["ffn_gate"][l], w["ffn_up"][l]
            return tiles(np.stack([g.reshape(D, 22, P), u.reshape(D, 22, P)], 2).reshape(D, 2 * FF1))
        direct = dict(wdn="w_branch_dn", wpool="w_branch_pool", wret="w_branch_ret", wout="w_out", wa="w_a_2", wb="w_b_2", wc="w_c_2",
                      wo="w_o_2", up="w_up_2")
        if name == "wb":
            return tiles(w["w_b_2"][l])
        if name in direct:
            return tiles(w[direct[name]][l])
        if name == "down":
            return rows(w["ffn_down"][l])
        if name == "down2":
            return rows(w["w_down_2"][l])
        a = w["w_in_2"][l]
        c = lambda n, lo=0, m=None: a[:, S2[n][0] + lo:S2[n][0] + (lo + m if m else S2[n][1])]
        if name == "q2a":
            return tiles(np.concatenate([c("aq"), c("ak"), c("ak"), c("iq"), c("ik"), c("ik"),
                                         c("ck", 0, 64), c("ck", 0, 64), c("ck", 64, 64), c("ck", 64, 64)], 1))
        if name == "q2b":
            return tiles(np.concatenate([c("bq"), c("bk"), c("cq")], 1))
        if name == "v2a":
            return moving(c("bv", 0, 512))
        if name == "v2b":
            return moving(np.concatenate([c("bv", 512, 256), c("cv"), c("av"), c("iw"), np.zeros((D, 56), np.float32)], 1))
        raise ValueError(name)

    out = np.zeros((NCHUNK, P, 1024), np.float32)
    for i, (name, l, n) in enumerate(order):
        if (name, l) not in made:
            made = {(name, l): make(name, l)}
        out[i] = made[name, l][n]
    return out


def feature_rows(a, n):
    return np.asarray(a).reshape(n, P).T


def parameters(inputs):
    x = {k: np.asarray(v) for k, v in inputs.items()}
    par1 = np.zeros((DEPTH, P, N_PAR1), np.float32)
    par2 = np.zeros((DEPTH, P, N_PAR2), np.float32)
    small = np.zeros((DEPTH, P, N_SMALL), np.float32)
    for l in range(DEPTH):
        def put(table, dst, name, a):
            o, n = table[name]
            dst[l][:, o:o + n] = a
        put(PAR1, par1, "mixpre", feature_rows(x["mix_pre_norm"][l], 8))
        put(PAR1, par1, "mixpost", feature_rows(x["mix_post_norm"][l], 8))
        put(PAR1, par1, "ffnpre", feature_rows(x["ffn_pre_norm"][l], 8))
        put(PAR1, par1, "ffnpost", feature_rows(x["ffn_post_norm"][l], 8))
        put(PAR1, par1, "conv", x["dn_conv"][l].reshape(4, 12, P).transpose(2, 1, 0).reshape(P, 48))
        put(PAR1, par1, "dnout", feature_rows(x["dn_out_norm"][l], 1))
        put(PAR1, par1, "retout", feature_rows(x["ret_out_norm"][l], 4))
        put(PAR1, par1, "pscale", feature_rows(x["pool_scale"][l], 4))
        put(PAR1, par1, "alog", np.repeat(x["dn_A_log"][l], 2)[None, :])
        put(PAR1, par1, "dtb", np.repeat(x["dn_dt_bias"][l], 2)[None, :])
        put(PAR2, par2, "attn", feature_rows(x["attn_norm_2"][l], 8))
        put(PAR2, par2, "mlp", feature_rows(x["mlp_norm_2"][l], 8))
        put(PAR2, par2, "final", feature_rows(x["final_norm_2"], 8))
        put(PAR2, par2, "idxk", np.concatenate([x["idx_k_norm_2"][l]] * 2)[:, None])
        put(PAR2, par2, "sinks", x["sinks_2"][l].reshape(2, 2, 2).transpose(0, 2, 1).reshape(1, 8))
        small[l][:, 0:64] = x["w_in"][l][:, 2048:2056].reshape(8, P, 8).transpose(1, 0, 2).reshape(P, 64)
        small[l][:, 64:576] = x["pool_w"][l].transpose(1, 0, 2).reshape(P, 512)
    return par1, par2, small


def declare(nc):
    d = lambda n, s, t=F32: nc.dram_tensor(f"in_{n}", s, t, kind="ExternalInput").ap()
    ins = {
        "weights": d("weights", (NCHUNK, P, 1024)), "x": d("x", (P, 8, T)), "positions": d("positions", (P, T), I32),
        "const1": d("const1", (P, N_CONST1)), "lev": d("lev", (P, 6 * P)), "const2": d("const2", (P, N_CONST2)),
        "par": d("par", (P, N_PAR)), "small": d("small", (P, DEPTH * N_SMALL)),
    }
    return ins, nc.dram_tensor("out", (P, 8, T), F32, kind="ExternalOutput").ap()


def lay_out(order, inputs):
    par1, par2, small = parameters(inputs)
    x = np.asarray(inputs["x"])[0]
    return {
        "in_weights": pack(order, inputs),
        "in_x": np.ascontiguousarray(x.T.reshape(8, P, T).transpose(1, 0, 2)),
        "in_positions": np.ascontiguousarray(np.broadcast_to(np.asarray(inputs["positions_2"])[0][None, :], (P, T))),
        "in_const1": constants1(), "in_lev": np.concatenate(levels(), 1).astype(np.float32), "in_const2": constants2(),
        "in_par": np.concatenate([*par1, *par2], 1), "in_small": np.concatenate([*small], 1),
    }


def kernel(**inputs):
    from concourse import bacc
    from concourse.bass_utils import run_bass_kernel_spmd

    nc = bacc.Bacc("TRN2", target_bir_lowering=False, num_devices=1)
    ins, out = declare(nc)
    order = program(nc, ins, out)
    r = run_bass_kernel_spmd(nc, [lay_out(order, inputs)], core_ids=[0])
    got = np.asarray(r.results[0]["out"])
    return np.ascontiguousarray(got.transpose(1, 0, 2).reshape(D, T).T)[None]
```
